# Optimizing a Trainium2 kernel written in Bass

```python
import math
import jax
import jax.numpy as jnp
from jax import lax
import numpy as np
import jax, jax.numpy as jnp

D_MODEL = 1024
BATCH = 1
SEQ = 256
DEPTH = 2

MEM_LEN = 256
EPS = 1e-6
NEG_INF = -1e30
FORCE_SCORE = 1e4

CONV_CH = 512
CONV_WIDTH = 31

NSA_HEADS = 8
NSA_KV_GROUPS = 2
NSA_HEAD_DIM = 64
CMP_BLOCK = 32
CMP_STRIDE = 16
CMP_HIDDEN = 256
SLC_BLOCK = 64
N_SELECT = 16
WINDOW = 512
NSA_QBLOCK = 64

MLA_HEADS = 4
Q_RANK = 384
KV_RANK = 256
QK_NOPE = 128
QK_ROPE = 64
V_DIM = 128
ROPE_THETA = 10000.0
ATTN_QBLOCK = 128

REL_BUCKETS = 32
REL_MAX_DIST = 128

XATTN_HEADS = 4
XATTN_HEAD_DIM = 128

FFN_HIDDEN = -(-8 * D_MODEL // (3 * 256)) * 256

IN_SIZES = (2 * CONV_CH, NSA_HEADS * NSA_HEAD_DIM, 6 * NSA_KV_GROUPS * NSA_HEAD_DIM, 3 * NSA_HEADS, Q_RANK, KV_RANK, QK_ROPE, 3 * D_MODEL)
IN_COLS = 2 * CONV_CH + NSA_HEADS * NSA_HEAD_DIM + 6 * NSA_KV_GROUPS * NSA_HEAD_DIM + 3 * NSA_HEADS + Q_RANK + KV_RANK + QK_ROPE + 3 * D_MODEL


def rmsnorm(x, g):
    xf = x.astype(jnp.float32)
    y = xf * lax.rsqrt(jnp.mean(xf * xf, axis=-1, keepdims=True) + EPS)
    return (y * g.astype(jnp.float32)).astype(x.dtype)

def layernorm(x, g, b):
    xf = x.astype(jnp.float32)
    mu = jnp.mean(xf, axis=-1, keepdims=True)
    var = jnp.mean(jnp.square(xf - mu), axis=-1, keepdims=True)
    y = (xf - mu) * lax.rsqrt(var + EPS) * g.astype(jnp.float32) + b.astype(jnp.float32)
    return y.astype(x.dtype)

def t5_bucket(dist):
    exact = REL_BUCKETS // 2
    d = jnp.maximum(dist, 0)
    log_ratio = jnp.log(jnp.maximum(d, 1).astype(jnp.float32) / exact) / math.log(REL_MAX_DIST / exact)
    large = jnp.minimum(exact + (log_ratio * (REL_BUCKETS - exact)).astype(jnp.int32), REL_BUCKETS - 1)
    return jnp.where(d < exact, d, large)

def apply_rope(x, cos, sin):
    xf = x.astype(jnp.float32)
    x1, x2 = jnp.split(xf, 2, axis=-1)
    return jnp.concatenate([x1 * cos - x2 * sin, x2 * cos + x1 * sin], axis=-1).astype(x.dtype)

def conformer_conv(u_glu, conv_w, conv_b, ln_g, ln_b, w_proj):
    a, b = jnp.split(u_glu, 2, axis=-1)
    u = a * jax.nn.sigmoid(b)
    u = lax.conv_general_dilated(u, conv_w[:, None, :], window_strides=(1,), padding=[(CONV_WIDTH - 1, 0)],
                                 dimension_numbers=('NWC', 'WIO', 'NWC'), feature_group_count=CONV_CH) + conv_b
    u = jax.nn.silu(layernorm(u, ln_g, ln_b))
    return u @ w_proj

def compress_blocks(tok, pos, w1, b1, w2, n_cmp):
    bsz = tok.shape[0]
    idx = CMP_STRIDE * jnp.arange(n_cmp)[:, None] + jnp.arange(CMP_BLOCK)[None, :]
    blk = tok[:, idx] + pos[:, None, :]
    blk = blk.transpose(0, 1, 3, 2, 4).reshape(bsz, n_cmp, NSA_KV_GROUPS, CMP_BLOCK * NSA_HEAD_DIM)
    return jax.nn.gelu(blk @ w1 + b1) @ w2

def nsa_attention(q, kv, gate_logits, rel_bias, cmp_pos_k, cmp_w1_k, cmp_b1_k, cmp_w2_k,
                  cmp_pos_v, cmp_w1_v, cmp_b1_v, cmp_w2_v):
    bsz, seq = q.shape[0], q.shape[1]
    G, HG, dh = NSA_KV_GROUPS, NSA_HEADS // NSA_KV_GROUPS, NSA_HEAD_DIM
    n_cmp = (seq - CMP_BLOCK) // CMP_STRIDE + 1
    n_sb = seq // SLC_BLOCK
    n_sel = min(N_SELECT, n_sb)
    n_keys = n_sel * SLC_BLOCK
    kw_len = NSA_QBLOCK + WINDOW
    scale = dh ** -0.5
    q = q.reshape(bsz, seq, G, HG, dh)
    kv = kv.reshape(bsz, seq, 6, G, dh)
    k_cmp = compress_blocks(kv[:, :, 0], cmp_pos_k, cmp_w1_k, cmp_b1_k, cmp_w2_k, n_cmp)
    v_cmp = compress_blocks(kv[:, :, 1], cmp_pos_v, cmp_w1_v, cmp_b1_v, cmp_w2_v, n_cmp)
    k_slc = kv[:, :, 2].reshape(bsz, n_sb, SLC_BLOCK, G, dh).transpose(0, 3, 1, 2, 4)
    v_slc = kv[:, :, 3].reshape(bsz, n_sb, SLC_BLOCK, G, dh).transpose(0, 3, 1, 2, 4)
    k_win = jnp.pad(kv[:, :, 4], ((0, 0), (WINDOW, 0), (0, 0), (0, 0)))
    v_win = jnp.pad(kv[:, :, 5], ((0, 0), (WINDOW, 0), (0, 0), (0, 0)))
    gates = jax.nn.sigmoid(gate_logits.astype(jnp.float32)).astype(q.dtype).reshape(bsz, seq, G, HG, 3)
    rb_group = rel_bias.reshape(REL_BUCKETS, G, HG).transpose(1, 0, 2)
    c_start = CMP_STRIDE * jnp.arange(n_cmp)
    c_end = c_start + CMP_BLOCK - 1
    s_start = SLC_BLOCK * jnp.arange(n_sb)
    cover = ((c_start[:, None] < s_start[None, :] + SLC_BLOCK) & (c_start[:, None] + CMP_BLOCK > s_start[None, :])).astype(jnp.float32)
    b_idx = jnp.arange(bsz)[:, None, None, None]
    g_idx = jnp.arange(G)[None, :, None, None]
    j_idx = jnp.arange(n_sb)

    def block(i):
        q0 = i * NSA_QBLOCK
        tq = q0 + jnp.arange(NSA_QBLOCK)
        qb = lax.dynamic_slice_in_dim(q, q0, NSA_QBLOCK, axis=1)
        gb = lax.dynamic_slice_in_dim(gates, q0, NSA_QBLOCK, axis=1)
        dist_c = tq[:, None] - c_end[None, :]
        valid_c = dist_c >= 0
        bias_c = rel_bias[t5_bucket(dist_c)].reshape(NSA_QBLOCK, n_cmp, G, HG).transpose(2, 3, 0, 1)
        lc = jnp.einsum('bqghd,bcgd->bghqc', qb, k_cmp, preferred_element_type=jnp.float32) * scale + bias_c
        pc = jax.nn.softmax(jnp.where(valid_c, lc, NEG_INF), axis=-1) * jnp.any(valid_c, axis=-1)[:, None]
        o_cmp = jnp.einsum('bghqc,bcgd->bqghd', pc.astype(q.dtype), v_cmp)
        imp = jnp.einsum('bghqc,cn->bgqn', pc, cover)
        cur = tq // SLC_BLOCK
        forced = (j_idx[None] == 0) | (j_idx[None] == cur[:, None]) | (j_idx[None] == cur[:, None] - 1)
        causal_s = s_start[None, :] <= tq[:, None]
        score = jnp.where(forced, FORCE_SCORE, jnp.where(causal_s, imp, -1.0))
        top_val, top_idx = lax.top_k(score, n_sel)
        ks = k_slc[b_idx, g_idx, top_idx]
        vs = v_slc[b_idx, g_idx, top_idx]
        k_pos = top_idx[..., None] * SLC_BLOCK + jnp.arange(SLC_BLOCK)
        dist_s = tq[None, None, :, None, None] - k_pos
        valid_s = ((top_val >= 0)[..., None] & (dist_s >= 0)).reshape(bsz, G, 1, NSA_QBLOCK, n_keys)
        bias_s = rb_group[g_idx[..., None], t5_bucket(dist_s)]
        bias_s = bias_s.transpose(0, 1, 5, 2, 3, 4).reshape(bsz, G, HG, NSA_QBLOCK, n_keys)
        ls = jnp.einsum('bqghd,bgqnkd->bghqnk', qb, ks, preferred_element_type=jnp.float32)
        ls = ls.reshape(bsz, G, HG, NSA_QBLOCK, n_keys) * scale + bias_s
        ps = jax.nn.softmax(jnp.where(valid_s, ls, NEG_INF), axis=-1)
        o_slc = jnp.einsum('bghqk,bgqkd->bqghd', ps.astype(q.dtype), vs.reshape(bsz, G, NSA_QBLOCK, n_keys, dh))
        kw = lax.dynamic_slice_in_dim(k_win, q0, kw_len, axis=1)
        vw = lax.dynamic_slice_in_dim(v_win, q0, kw_len, axis=1)
        k_pos_w = q0 - WINDOW + jnp.arange(kw_len)
        dist_w = tq[:, None] - k_pos_w[None, :]
        valid_w = (dist_w >= 0) & (dist_w < WINDOW) & (k_pos_w[None, :] >= 0)
        bias_w = rel_bias[t5_bucket(dist_w)].reshape(NSA_QBLOCK, kw_len, G, HG).transpose(2, 3, 0, 1)
        lw = jnp.einsum('bqghd,bkgd->bghqk', qb, kw, preferred_element_type=jnp.float32) * scale + bias_w
        pw = jax.nn.softmax(jnp.where(valid_w, lw, NEG_INF), axis=-1)
        o_win = jnp.einsum('bghqk,bkgd->bqghd', pw.astype(q.dtype), vw)
        out = gb[..., 0:1] * o_cmp + gb[..., 1:2] * o_slc + gb[..., 2:3] * o_win
        return out.reshape(bsz, NSA_QBLOCK, NSA_HEADS * dh)

    out = lax.map(block, jnp.arange(seq // NSA_QBLOCK))
    return out.transpose(1, 0, 2, 3).reshape(bsz, seq, NSA_HEADS * dh)

def mla_attention(c_q, c_kv, k_rope, positions, norm_q, norm_kv, w_uq, w_ukv):
    bsz, seq = c_q.shape[0], c_q.shape[1]
    q = (rmsnorm(c_q, norm_q) @ w_uq).reshape(bsz, seq, MLA_HEADS, QK_NOPE + QK_ROPE)
    kv = (rmsnorm(c_kv, norm_kv) @ w_ukv).reshape(bsz, seq, MLA_HEADS, QK_NOPE + V_DIM)
    q_nope, q_pe = q[..., :QK_NOPE], q[..., QK_NOPE:]
    k_nope, v = kv[..., :QK_NOPE], kv[..., QK_NOPE:]
    half = QK_ROPE // 2
    inv_freq = ROPE_THETA ** (-jnp.arange(half, dtype=jnp.float32) / half)
    ang = positions.astype(jnp.float32)[..., None] * inv_freq
    cos, sin = jnp.cos(ang), jnp.sin(ang)
    q_pe = apply_rope(q_pe, cos[:, :, None, :], sin[:, :, None, :])
    k_pe = apply_rope(k_rope, cos, sin)
    scale = (QK_NOPE + QK_ROPE) ** -0.5
    k_idx = jnp.arange(seq)

    def block(i):
        q0 = i * ATTN_QBLOCK
        qn = lax.dynamic_slice_in_dim(q_nope, q0, ATTN_QBLOCK, axis=1)
        qp = lax.dynamic_slice_in_dim(q_pe, q0, ATTN_QBLOCK, axis=1)
        logits = (jnp.einsum('bqhd,bkhd->bhqk', qn, k_nope, preferred_element_type=jnp.float32)
                  + jnp.einsum('bqhr,bkr->bhqk', qp, k_pe, preferred_element_type=jnp.float32)) * scale
        causal = k_idx[None, :] <= (q0 + jnp.arange(ATTN_QBLOCK))[:, None]
        p = jax.nn.softmax(jnp.where(causal, logits, NEG_INF), axis=-1)
        return jnp.einsum('bhqk,bkhd->bqhd', p.astype(v.dtype), v)

    out = lax.map(block, jnp.arange(seq // ATTN_QBLOCK))
    return out.transpose(1, 0, 2, 3, 4).reshape(bsz, seq, MLA_HEADS * V_DIM)

def memory_cross_attention(h, mem_n, w_q, w_kv, w_o):
    bsz, seq = h.shape[0], h.shape[1]
    m_len = mem_n.shape[1]
    q = (h @ w_q).reshape(bsz, seq, XATTN_HEADS, XATTN_HEAD_DIM)
    kv = (mem_n @ w_kv).reshape(bsz, m_len, 2, XATTN_HEADS, XATTN_HEAD_DIM)
    logits = jnp.einsum('bqhd,bmhd->bhqm', q, kv[:, :, 0], preferred_element_type=jnp.float32) * XATTN_HEAD_DIM ** -0.5
    p = jax.nn.softmax(logits, axis=-1)
    o = jnp.einsum('bhqm,bmhd->bqhd', p.astype(h.dtype), kv[:, :, 1]).reshape(bsz, seq, XATTN_HEADS * XATTN_HEAD_DIM)
    return o @ w_o

def first_inputs(seed: int = 0) -> dict:
    key = jax.random.key(seed)
    keys = jax.random.split(key, 48)
    counter = [0]
    L = DEPTH

    def nxt():
        k = keys[counter[0]]
        counter[0] += 1
        return k

    def dense(shape, fan_in):
        return jax.random.normal(nxt(), shape, jnp.float32) * fan_in ** -0.5

    def gain(shape):
        return 1.0 + 0.02 * jax.random.normal(nxt(), shape, jnp.float32)

    def small(shape):
        return 0.02 * jax.random.normal(nxt(), shape, jnp.float32)

    dh = NSA_HEAD_DIM
    x = jax.random.normal(nxt(), (BATCH, SEQ, D_MODEL), jnp.float32)
    mem = jax.random.normal(nxt(), (BATCH, MEM_LEN, D_MODEL), jnp.float32)
    offsets = jax.random.randint(nxt(), (BATCH, 1), 0, 2048, dtype=jnp.int32)
    positions = offsets + jnp.arange(SEQ, dtype=jnp.int32)[None, :]
    return {
        'x': x,
        'mem': mem,
        'positions': positions,
        'rel_bias': 0.1 * jax.random.normal(nxt(), (REL_BUCKETS, NSA_HEADS), jnp.float32),
        'norm_mix': gain((L, D_MODEL)),
        'norm_xattn': gain((L, D_MODEL)),
        'norm_mem': gain((L, D_MODEL)),
        'norm_ffn': gain((L, D_MODEL)),
        'norm_final': gain((D_MODEL,)),
        'w_in': dense((L, D_MODEL, IN_COLS), D_MODEL),
        'conv_w': dense((L, CONV_WIDTH, CONV_CH), CONV_WIDTH),
        'conv_b': small((L, CONV_CH)),
        'conv_ln_g': gain((L, CONV_CH)),
        'conv_ln_b': small((L, CONV_CH)),
        'w_branch_conv': dense((L, CONV_CH, D_MODEL), CONV_CH),
        'cmp_pos_k': dense((L, CMP_BLOCK, dh), 4),
        'cmp_w1_k': dense((L, CMP_BLOCK * dh, CMP_HIDDEN), CMP_BLOCK * dh),
        'cmp_b1_k': small((L, CMP_HIDDEN)),
        'cmp_w2_k': dense((L, CMP_HIDDEN, dh), CMP_HIDDEN),
        'cmp_pos_v': dense((L, CMP_BLOCK, dh), 4),
        'cmp_w1_v': dense((L, CMP_BLOCK * dh, CMP_HIDDEN), CMP_BLOCK * dh),
        'cmp_b1_v': small((L, CMP_HIDDEN)),
        'cmp_w2_v': dense((L, CMP_HIDDEN, dh), CMP_HIDDEN),
        'w_branch_nsa': dense((L, NSA_HEADS * dh, D_MODEL), NSA_HEADS * dh),
        'mla_norm_q': gain((L, Q_RANK)),
        'mla_norm_kv': gain((L, KV_RANK)),
        'w_uq': dense((L, Q_RANK, MLA_HEADS * (QK_NOPE + QK_ROPE)), Q_RANK),
        'w_ukv': dense((L, KV_RANK, MLA_HEADS * (QK_NOPE + V_DIM)), KV_RANK),
        'w_branch_mla': dense((L, MLA_HEADS * V_DIM, D_MODEL), MLA_HEADS * V_DIM),
        'w_out': dense((L, D_MODEL, D_MODEL), D_MODEL),
        'w_xq': dense((L, D_MODEL, XATTN_HEADS * XATTN_HEAD_DIM), D_MODEL),
        'w_xkv': dense((L, D_MODEL, 2 * XATTN_HEADS * XATTN_HEAD_DIM), D_MODEL),
        'w_xo': dense((L, XATTN_HEADS * XATTN_HEAD_DIM, D_MODEL), XATTN_HEADS * XATTN_HEAD_DIM),
        'w_gate_up': dense((L, D_MODEL, 2 * FFN_HIDDEN), D_MODEL),
        'w_down': dense((L, FFN_HIDDEN, D_MODEL), FFN_HIDDEN),
    }

def first_block(x, mem, positions, rel_bias, norm_mix, norm_xattn, norm_mem, norm_ffn, norm_final,
              w_in, conv_w, conv_b, conv_ln_g, conv_ln_b, w_branch_conv,
              cmp_pos_k, cmp_w1_k, cmp_b1_k, cmp_w2_k, cmp_pos_v, cmp_w1_v, cmp_b1_v, cmp_w2_v, w_branch_nsa,
              mla_norm_q, mla_norm_kv, w_uq, w_ukv, w_branch_mla, w_out,
              w_xq, w_xkv, w_xo, w_gate_up, w_down):
    split_at = [int(v) for v in np.cumsum(IN_SIZES)[:-1]]
    for layer in range(DEPTH):
        h = rmsnorm(x, norm_mix[layer])
        z = h @ w_in[layer]
        u_glu, q_nsa, kv_nsa, g_nsa, c_q, c_kv, k_rope, g_merge = jnp.split(z, split_at, axis=-1)
        y_conv = conformer_conv(u_glu, conv_w[layer], conv_b[layer], conv_ln_g[layer], conv_ln_b[layer], w_branch_conv[layer])
        y_nsa = nsa_attention(q_nsa, kv_nsa, g_nsa, rel_bias,
                              cmp_pos_k[layer], cmp_w1_k[layer], cmp_b1_k[layer], cmp_w2_k[layer],
                              cmp_pos_v[layer], cmp_w1_v[layer], cmp_b1_v[layer], cmp_w2_v[layer]) @ w_branch_nsa[layer]
        y_mla = mla_attention(c_q, c_kv, k_rope, positions, mla_norm_q[layer], mla_norm_kv[layer],
                              w_uq[layer], w_ukv[layer]) @ w_branch_mla[layer]
        g = jax.nn.sigmoid(g_merge.astype(jnp.float32)).astype(x.dtype)
        g_conv, g_attn, g_mla = jnp.split(g, 3, axis=-1)
        x = x + (g_conv * y_conv + g_attn * y_nsa + g_mla * y_mla) @ w_out[layer]
        x = x + memory_cross_attention(rmsnorm(x, norm_xattn[layer]), rmsnorm(mem, norm_mem[layer]),
                                       w_xq[layer], w_xkv[layer], w_xo[layer])
        gate, up = jnp.split(rmsnorm(x, norm_ffn[layer]) @ w_gate_up[layer], 2, axis=-1)
        x = x + (jax.nn.silu(gate) * up) @ w_down[layer]
    return rmsnorm(x, norm_final)


N_HYB = (DEPTH + 1) // 2
N_REC = DEPTH // 2
NORM_EPS = 1e-6
CONV_K = 4
D_FF = 2816
D_SSM = D_MODEL
SSM_HEAD_DIM = 64
SSM_HEADS = D_SSM // SSM_HEAD_DIM
SSM_GROUPS = 2
SSM_STATE = 128
SSM_CONV_DIM = D_SSM + 2 * SSM_GROUPS * SSM_STATE
SSD_CHUNK = 128
FOX_HEAD_DIM = 128
FOX_HEADS = 8
D_FOX = FOX_HEADS * FOX_HEAD_DIM
Q_BLOCK = 128
HYB_IN = D_SSM + SSM_CONV_DIM + SSM_HEADS + 3 * D_FOX + FOX_HEADS
D_RNN = D_MODEL
RNN_BLOCKS = 8
RNN_BLOCK = D_RNN // RNN_BLOCKS
RG_LRU_C = 8.0


def rms_norm(x, g):
    xf = x.astype(jnp.float32)
    y = xf * lax.rsqrt(jnp.mean(xf * xf, axis=-1, keepdims=True) + NORM_EPS)
    return (y * g.astype(jnp.float32)).astype(x.dtype)

def swiglu(x, w_in, w_out):
    gate, up = jnp.split(x @ w_in, 2, axis=-1)
    return (jax.nn.silu(gate) * up) @ w_out

def causal_conv(x, w, bias):
    s = x.shape[1]
    kw = w.shape[0]
    xp = jnp.pad(x, ((0, 0), (kw - 1, 0), (0, 0)))
    y = xp[:, 0:s] * w[0]
    for k in range(1, kw):
        y = y + xp[:, k:k + s] * w[k]
    return y + bias

def ssd_chunked(xh, dt, a, bm, cm):
    b, s, nh, p = xh.shape
    g, n = bm.shape[-2:]
    kh = nh // g
    c = s // SSD_CHUNK
    X = (xh.astype(jnp.float32) * dt[..., None]).reshape(b, c, SSD_CHUNK, g, kh, p)
    Bc = bm.astype(jnp.float32).reshape(b, c, SSD_CHUNK, g, n)
    Cc = cm.astype(jnp.float32).reshape(b, c, SSD_CHUNK, g, n)
    dA = (dt * a).reshape(b, c, SSD_CHUNK, g, kh).transpose(0, 3, 4, 1, 2)
    a_cs = jnp.cumsum(dA, axis=-1)
    causal = jnp.tril(jnp.ones((SSD_CHUNK, SSD_CHUNK), dtype=bool))
    seg = a_cs[..., :, None] - a_cs[..., None, :]
    L = jnp.exp(jnp.where(causal, seg, -jnp.inf))
    cb = jnp.einsum("bclgn,bcsgn->bgcls", Cc, Bc)
    y_diag = jnp.einsum("bgkcls,bcsgkp->bclgkp", L * cb[:, :, None], X)
    decay_states = jnp.exp(a_cs[..., -1:] - a_cs)
    states = jnp.einsum("bclgn,bgkcl,bclgkp->bcgkpn", Bc, decay_states, X)
    chunk_tot = a_cs[..., -1]
    chunk_cs = jnp.cumsum(chunk_tot, axis=-1)
    cs_prev = chunk_cs - chunk_tot
    seg_c = cs_prev[..., :, None] - chunk_cs[..., None, :]
    strict = jnp.tril(jnp.ones((c, c), dtype=bool), k=-1)
    decay_chunk = jnp.exp(jnp.where(strict, seg_c, -jnp.inf))
    init_states = jnp.einsum("bgkzc,bcgkpn->bzgkpn", decay_chunk, states)
    state_decay_out = jnp.exp(a_cs)
    y_off = jnp.einsum("bclgn,bcgkpn,bgkcl->bclgkp", Cc, init_states, state_decay_out)
    return (y_diag + y_off).reshape(b, s, nh, p)

def forgetting_attention(q, k, v, log_f):
    b, s, h, d = q.shape
    nblk = s // Q_BLOCK
    cum = jnp.cumsum(log_f, axis=1).transpose(0, 2, 1)
    qb = q.reshape(b, nblk, Q_BLOCK, h, d).transpose(1, 0, 2, 3, 4)
    cqb = cum.reshape(b, h, nblk, Q_BLOCK).transpose(2, 0, 1, 3)
    kpos = jnp.arange(s)
    scale = d ** -0.5

    def block(args):
        qi, ci, i = args
        logits = jnp.einsum("bqhd,bkhd->bhqk", qi, k).astype(jnp.float32) * scale
        logits = logits + ci[..., :, None] - cum[:, :, None, :]
        qpos = i * Q_BLOCK + jnp.arange(Q_BLOCK)
        mask = kpos[None, :] <= qpos[:, None]
        probs = jax.nn.softmax(jnp.where(mask, logits, -jnp.inf), axis=-1)
        return jnp.einsum("bhqk,bkhd->bqhd", probs.astype(v.dtype), v)

    out = lax.map(block, (qb, cqb, jnp.arange(nblk)))
    return out.transpose(1, 0, 2, 3, 4).reshape(b, s, h, d)

def hybrid_mixer(h, w_in, conv_w, conv_b, dt_bias, a_log, d_skip, ssm_norm_g, fox_b_f, w_out):
    b, s, _ = h.shape
    sizes = (D_SSM, SSM_CONV_DIM, SSM_HEADS, D_FOX, D_FOX, D_FOX)
    offs = np.cumsum(sizes).tolist()
    z, xbc, dt_raw, q, k, v, f_raw = jnp.split(h @ w_in, offs, axis=-1)
    xbc = jax.nn.silu(causal_conv(xbc, conv_w, conv_b))
    xs, bm, cm = jnp.split(xbc, [D_SSM, D_SSM + SSM_GROUPS * SSM_STATE], axis=-1)
    xh = xs.reshape(b, s, SSM_HEADS, SSM_HEAD_DIM)
    dt = jax.nn.softplus(dt_raw.astype(jnp.float32) + dt_bias.astype(jnp.float32))
    a = -jnp.exp(a_log.astype(jnp.float32))
    y = ssd_chunked(xh, dt, a,
                    bm.reshape(b, s, SSM_GROUPS, SSM_STATE),
                    cm.reshape(b, s, SSM_GROUPS, SSM_STATE))
    y = y + d_skip.astype(jnp.float32)[:, None] * xh.astype(jnp.float32)
    y = y.reshape(b, s, D_SSM) * jax.nn.silu(z.astype(jnp.float32))
    yg = y.reshape(b, s, SSM_GROUPS, D_SSM // SSM_GROUPS)
    yg = yg * lax.rsqrt(jnp.mean(yg * yg, axis=-1, keepdims=True) + NORM_EPS)
    y_ssm = (yg.reshape(b, s, D_SSM) * ssm_norm_g.astype(jnp.float32)).astype(h.dtype)
    log_f = jax.nn.log_sigmoid(f_raw.astype(jnp.float32) + fox_b_f.astype(jnp.float32))
    o = forgetting_attention(q.reshape(b, s, FOX_HEADS, FOX_HEAD_DIM),
                             k.reshape(b, s, FOX_HEADS, FOX_HEAD_DIM),
                             v.reshape(b, s, FOX_HEADS, FOX_HEAD_DIM), log_f)
    o = o.reshape(b, s, D_FOX).astype(h.dtype)
    return jnp.concatenate([y_ssm, o], axis=-1) @ w_out

def rg_lru(x, w_a, b_a, w_x, b_x, lam):
    b, s, d = x.shape
    xb = x.reshape(b, s, RNN_BLOCKS, RNN_BLOCK)
    r = jax.nn.sigmoid((jnp.einsum("bsnj,njk->bsnk", xb, w_a).reshape(b, s, d) + b_a).astype(jnp.float32))
    i = jax.nn.sigmoid((jnp.einsum("bsnj,njk->bsnk", xb, w_x).reshape(b, s, d) + b_x).astype(jnp.float32))
    log_a = RG_LRU_C * r * jax.nn.log_sigmoid(lam.astype(jnp.float32))
    a = jnp.exp(log_a)
    u = jnp.sqrt(-jnp.expm1(2.0 * log_a)) * (i * x.astype(jnp.float32))

    def combine(left, right):
        a1, b1 = left
        a2, b2 = right
        return a1 * a2, a2 * b1 + b2

    _, hs = lax.associative_scan(combine, (a, u), axis=1)
    return hs.astype(x.dtype)

def recurrent_mixer(h, w_in, conv_w, conv_b, w_a, b_a, w_x, b_x, lam, w_out):
    gate, xr = jnp.split(h @ w_in, 2, axis=-1)
    gate = jax.nn.gelu(gate, approximate=True)
    xr = causal_conv(xr, conv_w, conv_b)
    return (rg_lru(xr, w_a, b_a, w_x, b_x, lam) * gate) @ w_out

def second_inputs(seed: int = 0) -> dict:
    key = jax.random.key(seed)
    ks = jax.random.split(key, 24)
    f32 = jnp.float32

    def nrm(k, shape, scale):
        return jax.random.normal(k, shape, f32) * scale

    def unif(k, shape, lo, hi):
        return jax.random.uniform(k, shape, f32, lo, hi)

    x = nrm(ks[0], (BATCH, SEQ, D_MODEL), 1.0)
    norm_g = 1.0 + nrm(ks[1], (DEPTH, 6, D_MODEL), 0.05)
    ffn_w_in = nrm(ks[2], (DEPTH, 2, D_MODEL, 2 * D_FF), D_MODEL ** -0.5)
    ffn_w_out = nrm(ks[3], (DEPTH, 2, D_FF, D_MODEL), D_FF ** -0.5)
    hyb_w_in = nrm(ks[4], (N_HYB, D_MODEL, HYB_IN), D_MODEL ** -0.5)
    ssm_conv_w = nrm(ks[5], (N_HYB, CONV_K, SSM_CONV_DIM), CONV_K ** -0.5)
    ssm_conv_b = nrm(ks[6], (N_HYB, SSM_CONV_DIM), 0.02)
    dt0 = jnp.exp(unif(ks[7], (N_HYB, SSM_HEADS), math.log(1e-3), math.log(1e-1)))
    ssm_dt_bias = dt0 + jnp.log(-jnp.expm1(-dt0))
    ssm_a_log = jnp.log(unif(ks[8], (N_HYB, SSM_HEADS), 1.0, 16.0))
    ssm_d = 1.0 + nrm(ks[9], (N_HYB, SSM_HEADS), 0.1)
    ssm_norm_g = 1.0 + nrm(ks[10], (N_HYB, D_SSM), 0.05)
    fox_b_f = unif(ks[11], (N_HYB, FOX_HEADS), 1.0, 4.0)
    hyb_w_out = nrm(ks[12], (N_HYB, D_SSM + D_FOX, D_MODEL), (D_SSM + D_FOX) ** -0.5)
    rec_w_in = nrm(ks[13], (N_REC, D_MODEL, 2 * D_RNN), D_MODEL ** -0.5)
    rec_conv_w = nrm(ks[14], (N_REC, CONV_K, D_RNN), CONV_K ** -0.5)
    rec_conv_b = nrm(ks[15], (N_REC, D_RNN), 0.02)
    rec_w_a = nrm(ks[16], (N_REC, RNN_BLOCKS, RNN_BLOCK, RNN_BLOCK), RNN_BLOCK ** -0.5)
    rec_b_a = nrm(ks[17], (N_REC, D_RNN), 0.02)
    rec_w_x = nrm(ks[18], (N_REC, RNN_BLOCKS, RNN_BLOCK, RNN_BLOCK), RNN_BLOCK ** -0.5)
    rec_b_x = nrm(ks[19], (N_REC, D_RNN), 0.02)
    a0 = unif(ks[20], (N_REC, D_RNN), 0.9, 0.999)
    s0 = a0 ** (1.0 / RG_LRU_C)
    rec_lambda = jnp.log(s0) - jnp.log1p(-s0)
    rec_w_out = nrm(ks[21], (N_REC, D_RNN, D_MODEL), D_RNN ** -0.5)
    return {"x": x, "norm_g": norm_g, "ffn_w_in": ffn_w_in, "ffn_w_out": ffn_w_out,
            "hyb_w_in": hyb_w_in, "ssm_conv_w": ssm_conv_w, "ssm_conv_b": ssm_conv_b,
            "ssm_dt_bias": ssm_dt_bias, "ssm_a_log": ssm_a_log, "ssm_d": ssm_d,
            "ssm_norm_g": ssm_norm_g, "fox_b_f": fox_b_f, "hyb_w_out": hyb_w_out,
            "rec_w_in": rec_w_in, "rec_conv_w": rec_conv_w, "rec_conv_b": rec_conv_b,
            "rec_w_a": rec_w_a, "rec_b_a": rec_b_a, "rec_w_x": rec_w_x, "rec_b_x": rec_b_x,
            "rec_lambda": rec_lambda, "rec_w_out": rec_w_out}

def second_block(x, norm_g, ffn_w_in, ffn_w_out, hyb_w_in, ssm_conv_w, ssm_conv_b, ssm_dt_bias,
              ssm_a_log, ssm_d, ssm_norm_g, fox_b_f, hyb_w_out, rec_w_in, rec_conv_w, rec_conv_b,
              rec_w_a, rec_b_a, rec_w_x, rec_b_x, rec_lambda, rec_w_out):
    for layer in range(DEPTH):
        g = norm_g[layer]
        h = swiglu(rms_norm(x, g[0]), ffn_w_in[layer, 0], ffn_w_out[layer, 0])
        x = x + 0.5 * rms_norm(h, g[1])
        h = rms_norm(x, g[2])
        if layer % 2 == 0:
            i = layer // 2
            h = hybrid_mixer(h, hyb_w_in[i], ssm_conv_w[i], ssm_conv_b[i], ssm_dt_bias[i],
                             ssm_a_log[i], ssm_d[i], ssm_norm_g[i], fox_b_f[i], hyb_w_out[i])
        else:
            j = layer // 2
            h = recurrent_mixer(h, rec_w_in[j], rec_conv_w[j], rec_conv_b[j], rec_w_a[j], rec_b_a[j],
                                rec_w_x[j], rec_b_x[j], rec_lambda[j], rec_w_out[j])
        x = x + rms_norm(h, g[3])
        h = swiglu(rms_norm(x, g[4]), ffn_w_in[layer, 1], ffn_w_out[layer, 1])
        x = x + 0.5 * rms_norm(h, g[5])
    return x


def setup_inputs(seed=0):
    out = dict(first_inputs(seed))
    for name, value in second_inputs(seed + 1).items():
        if name != "x":
            out[name + "_2"] = value
    return out


def reference(
    x, mem, positions, rel_bias, norm_mix, norm_xattn, norm_mem, norm_ffn, norm_final, w_in,
    conv_w, conv_b, conv_ln_g, conv_ln_b, w_branch_conv, cmp_pos_k, cmp_w1_k, cmp_b1_k,
    cmp_w2_k, cmp_pos_v, cmp_w1_v, cmp_b1_v, cmp_w2_v, w_branch_nsa, mla_norm_q, mla_norm_kv,
    w_uq, w_ukv, w_branch_mla, w_out, w_xq, w_xkv, w_xo, w_gate_up, w_down, norm_g_2,
    ffn_w_in_2, ffn_w_out_2, hyb_w_in_2, ssm_conv_w_2, ssm_conv_b_2, ssm_dt_bias_2, ssm_a_log_2,
    ssm_d_2, ssm_norm_g_2, fox_b_f_2, hyb_w_out_2, rec_w_in_2, rec_conv_w_2, rec_conv_b_2,
    rec_w_a_2, rec_b_a_2, rec_w_x_2, rec_b_x_2, rec_lambda_2, rec_w_out_2,
):
    x = first_block(
        x, mem, positions, rel_bias, norm_mix, norm_xattn, norm_mem, norm_ffn, norm_final, w_in,
        conv_w, conv_b, conv_ln_g, conv_ln_b, w_branch_conv, cmp_pos_k, cmp_w1_k, cmp_b1_k,
        cmp_w2_k, cmp_pos_v, cmp_w1_v, cmp_b1_v, cmp_w2_v, w_branch_nsa, mla_norm_q,
        mla_norm_kv, w_uq, w_ukv, w_branch_mla, w_out, w_xq, w_xkv, w_xo, w_gate_up, w_down,
    )
    return second_block(
        x, norm_g_2, ffn_w_in_2, ffn_w_out_2, hyb_w_in_2, ssm_conv_w_2, ssm_conv_b_2,
        ssm_dt_bias_2, ssm_a_log_2, ssm_d_2, ssm_norm_g_2, fox_b_f_2, hyb_w_out_2, rec_w_in_2,
        rec_conv_w_2, rec_conv_b_2, rec_w_a_2, rec_b_a_2, rec_w_x_2, rec_b_x_2, rec_lambda_2,
        rec_w_out_2,
    )


_drawn_inputs = setup_inputs


def setup_inputs(seed=0):
    import zlib

    import numpy as np

    out = dict(_drawn_inputs(seed))
    spreads = {}
    factors = {'rel_bias': 3.051,
     'norm_xattn': 8.0,
     'norm_mem': 7.097,
     'conv_ln_g': 2.844,
     'conv_ln_b': 2.837,
     'cmp_b1_k': 8.0,
     'cmp_b1_v': 6.199,
     'mla_norm_q': 8.0,
     'mla_norm_kv': 6.287,
     'rec_b_a_2': 32.239,
     'rec_b_x_2': 8.0}
    for name, (base, spread) in spreads.items():
        noise = np.random.default_rng([zlib.crc32(name.encode()), seed]).standard_normal(out[name].shape)
        drawn = base * np.exp(spread * noise) if base else spread * noise
        out[name] = jnp.asarray(drawn.astype(out[name].dtype))
    for name, factor in factors.items():
        out[name] = (out[name] * factor).astype(out[name].dtype)
    return out
```

```python
from contextlib import contextmanager
from math import log, pi, sqrt

import numpy as np

import concourse.bass as bass
from concourse import mybir

F32 = mybir.dt.float32
I32 = mybir.dt.int32
ALU = mybir.AluOpType
ACT = mybir.ActivationFunctionType
AX_X = mybir.AxisListType.X
ET = mybir.EngineType
ds = bass.ds

P = 128
TT = 2
T = P * TT
D = 1024
DEPTH = 2
KT = D // P
RING = 6
CHUNK = 2048
BLK = 512
FF = 2816
FT = FF // P
GU = FF // 256
EPS = 1e-6
NEG = -1e30

Z_GM = 0
Z_GLU = 3072
Z_Q = 4096
Z_KV = 4608
Z_CQ, Z_CKV, Z_KR, Z_GN = 5376, 5760, 6016, 6080
Z_COLS = 6104
ZW = 6144
CONV_W, CONV_CT = 31, 4
Q_RANK, KV_RANK = 384, 256
N_CMP = (T - 32) // 16 + 1
BAND = 384
S1 = {}
_o = 0
for _n, _w in (("mix", 8), ("xattn", 8), ("mem", 8), ("ffn", 8), ("conv_w", CONV_W * 4), ("conv_b", 4), ("ln_g", 4),
               ("ln_b", 4), ("pos", 32), ("b1", 4), ("w2k", 256), ("w2v", 128), ("mq", 3), ("mkv", 2)):
    S1[_n] = (_o, _o + _w)
    _o += _w
S1_W = _o
S2 = {}
_o = 0
for _n, _w in (("pre", 48), ("cw", 48), ("cb", 12), ("ng", 8), ("rw", 32), ("rb", 8), ("ba", 8), ("bx", 8), ("lam", 8),
               ("dtb", 16), ("alog", 16), ("dskip", 16), ("fb", 8)):
    S2[_n] = (_o, _o + _w)
    _o += _w
S2_W = _o
CC = {}
_o = 0
for _n, _w in (("ident", 128), ("ones", 128), ("upper", BAND), ("maskU", 128), ("mask", BAND), ("freq", 32), ("valid", 2)):
    CC[_n] = (_o, _o + _w)
    _o += _w
CC_W = _o
N_GAIN = 7

LAYER_CHUNKS = 24 + 4 + 2 + 2 + 3 + 2 + 4 + 4 + 2 + 2 + 33 + 2
TAIL_CHUNKS = 4 * 33 + 22 + 1 + 8 + 8 + 1 + 4
N_CHUNKS = 2 * LAYER_CHUNKS + TAIL_CHUNKS
assert LAYER_CHUNKS % RING == 0


class Point:

    def __init__(self, sem, const, steps):
        self.sem, self.const, self.steps = sem, const, steps


class Count:

    def __init__(self, core, name):
        self.name, self.h, self.const, self.steps = name, core.nc.alloc_semaphore(name), 0, {}
        core.counts.append(self)

    def add(self, n=1):
        self.const += n
        return Point(self, self.const, dict(self.steps))


class Engine:
    def __init__(self, core, e, name):
        self.core, self.e, self.name, self.count, self.known = core, e, name, Count(core, "s_" + name), {}

    def wait(self, *points):
        for p in points:
            if isinstance(p, (tuple, list)):
                self.wait(*p)
                continue
            key = (p.sem.name, tuple(sorted(p.steps.items())))
            if self.known.get(key, -1) >= p.const or p.const <= 0 and not p.steps:
                continue
            self.known[key] = p.const
            v = p.const
            for name, step in p.steps.items():
                v = v + self.core.iteration(name) * step
            self.e.wait_ge(p.sem.h, v)
        return self.e

    def do(self, ins, count=None, n=1):
        count = count or self.count
        ins.then_inc(count.h, n)
        p = count.add(n)
        self.core.last[self.name] = (p,)
        return p

    @property
    def now(self):
        return self.core.last.get(self.name, ())

    def chain(self):
        return self.wait(self.now)


class Core:
    def __init__(self, nc, learned):
        self.nc, self.learned, self.counts, self.last, self.vars, self.trips = nc, learned, [], {}, {}, {}
        self.seen = {}
        self.PE, self.V = Engine(self, nc.tensor, "pe"), Engine(self, nc.vector, "dve")
        self.A, self.G = Engine(self, nc.scalar, "act"), Engine(self, nc.gpsimd, "pool")
        self.engines = (self.PE, self.V, self.A, self.G)
        self.n_loops = 0

    def iteration(self, name):
        return self.vars[name] if name in self.vars else self.trips[name] - 1

    @contextmanager
    def loop(self, n, meet=False):
        name = f"l{self.n_loops}"
        self.n_loops += 1
        if meet:
            self.meet()
        base = {c.name: c.const for c in self.counts}
        steps, ends = self.learned.get(name, ({}, {}))
        for c in self.counts:
            c.steps[name] = steps.get(c.name, 0)
        before = dict(self.last)
        if not meet:
            for key, points in ends.items():
                back = tuple(Point(next(c for c in self.counts if c.name == s), k - steps.get(s, 0), st)
                             for s, k, st in points)
                assert all(p.const > 0 for p in back), (name, key)
                self.last[key] = before.get(key, ()) + back
        started = dict(self.last)
        with self.nc.Fori(0, n, engines=(ET.Pool, ET.Activation, ET.PE, ET.DVE)) as i:
            self.vars[name] = i
            yield i
            if meet:
                self.meet()
        self.seen[name] = (
            {c.name: c.const - base.get(c.name, 0) for c in self.counts},
            {k: [(p.sem.name, p.const, p.steps) for p in v if name in p.steps]
             for k, v in self.last.items() if v is not started.get(k)})
        del self.vars[name]
        self.trips[name] = n
        for c in self.counts:
            c.const += (n - 1) * (c.const - base.get(c.name, 0))
            c.steps.pop(name, None)
        for e in self.engines:
            e.known = {k: v for k, v in e.known.items() if name not in dict(k[1])}

    def meet(self):
        ends = [e.now for e in self.engines]
        for e in self.engines:
            e.wait(*ends)
        self.last = {e.name: self.last.get(e.name, ()) for e in self.engines}


def bc(ap, n):
    return ap.unsqueeze(len(ap.shape)).to_broadcast([*ap.shape, n])


def mid(ap, n):
    return ap.unsqueeze(1).to_broadcast([ap.shape[0], n, *ap.shape[1:]])


def build(nc, io, learned):
    core = Core(nc, learned)
    PE, V, A, G = core.engines

    def sb(name, shape, dt=F32):
        return nc.alloc_sbuf_tensor(name, shape, dt)

    ps = nc.alloc_psum_tensor("ps", [P, 8, BLK], F32)
    ring = sb("ring", [P, RING, CHUNK])
    x = sb("x", [P, TT, D])
    nT = sb("nT", [P, KT, T])
    big = sb("big", [P, 2048 + 8 * BAND])
    memT = big[:, 0:2048].rearrange("p (c n) -> p c n", c=KT)
    xn = sb("xn", [P, TT, D])
    z = sb("z", [P, TT, ZW])
    tT = sb("tT", [P, FT, T])
    band = big[:, 2048:].rearrange("p (h n) -> p h n", h=8)
    S = sb("S", [P, 2, 4, T])
    PTs = sb("PTs", [P, 2, 8, P])
    cbuf = sb("cbuf", [P, 1152])
    acc = sb("acc", [P, 6, T])
    const = sb("const", [P, CC_W])
    sm = sb("sm", [P, S1_W])
    sm2 = sb("sm2", [P, S2_W])
    st = sb("st", [P, 16])
    half = sb("half", [P, T])
    rope = sb("rope", [P, 2, TT, 32])
    ostage = sb("ostage", [P, TT, 512])
    junk = ostage[:, :, :].rearrange("p t n -> p (t n)")
    rs = sb("rs", [P, 2, 3, 4])

    def c_(name):
        a, b = CC[name]
        return const[:, a:b]

    def s1(name):
        a, b = S1[name]
        return sm[:, a:b]

    def s2(name, a=0, b=None):
        o, e = S2[name]
        return sm2[:, o + a:o + b if b is not None else e]

    ident, mask = c_("ident"), c_("mask")

    def load(queue, dst, src, *after):
        queue.wait(*after)
        c = Count(core, f"s_dma{len(core.counts)}")
        queue.e.dma_start(dst, src).then_inc(c.h, 16)
        return c.add(16)

    landed = [nc.alloc_semaphore(f"landed{s}") for s in range(RING)]
    used = Count(core, "used")
    with nc.named_scope("weights"):
        for s in range(RING):
            nc.sync.dma_start(ring[:, s, :], io["w"][s]).then_inc(landed[s], 16)
        whole = N_CHUNKS // RING
        with nc.Fori(0, whole - 1, engines=(ET.SP,)) as i:
            for s in range(RING):
                nc.sync.wait_ge(used.h, i * RING + (s + 2))
                nc.sync.dma_start(ring[:, s, :], io["w"][ds(i * RING + (RING + s), 1), :, :].rearrange("a p n -> p (a n)")
                                  ).then_inc(landed[s], 16)
        for g in range(whole * RING, N_CHUNKS):
            nc.sync.wait_ge(used.h, g - RING + 2)
            nc.sync.dma_start(ring[:, g % RING, :], io["w"][g]).then_inc(landed[g % RING], 16)

    def chunk():
        g = used.const - 1
        v = 16 * (g // RING + 1)
        for name, step in used.steps.items():
            assert step % RING == 0 or not learned
            v = v + core.iteration(name) * (16 * step // RING)
        PE.e.wait_ge(landed[g % RING], v)
        return ring[:, g % RING, :]

    bank_turn = [0]

    def free(*banks):
        return [core.last.get(f"b{b}", ()) for b in banks]

    def released(point, *banks):
        for b in banks:
            core.last[f"b{b}"] = (point,)

    def gemm_block(lhs, kts, pair, ready, width=BLK):
        PE.wait(free(2 * pair, 2 * pair + 1), ready)
        for c in range(kts // 4):
            w = chunk()
            for k in range(4):
                for t in range(TT):
                    m = PE.e.matmul(ps[:, 2 * pair + t, :], lhs[:, 4 * c + k, t * P:(t + 1) * P],
                                    w[:, k * BLK:(k + 1) * BLK], start=(c == 0 and k == 0), stop=(4 * c + k == kts - 1))
            p = PE.do(m, used)
        return p, ps[:, 2 * pair:2 * pair + 2, :]

    def gemm(lhs, kts, blocks, evac, ready=(), first=0):
        def body(at, j):
            p, o = gemm_block(lhs, kts, j, ready)
            released(evac(p, o, at, j), 2 * j, 2 * j + 1)
        whole = blocks // 3
        if whole > 1 and 3 * kts // 4 % RING == 0:
            with core.loop(whole) as i:
                for j in range(3):
                    body(i * 3 + (j + first), j)
        else:
            whole = 0
        for b in range(3 * whole, blocks):
            body(first + b, b % 3)

    def to_T(src, tiles, dst, evac=None, ready=()):
        out = ()
        for c in range(0, tiles, 2):
            n = min(2, tiles - c)
            b = 6 + bank_turn[0] % 2
            bank_turn[0] += 1
            PE.wait(free(b), ready)
            for i in range(n):
                for t in range(TT):
                    m = PE.e.transpose(ps[:, b, (i * TT + t) * P:(i * TT + t + 1) * P], src(c + i, t), ident)
            p = PE.do(m)
            o = ps[:, b, 0:n * T].rearrange("p (c n) -> p c n", c=n)
            if evac:
                e = evac(p, o, c, n)
            elif b == 6:
                e = V.do(V.wait(p, dst_free).tensor_copy(dst[:, c:c + n, :], o))
            else:
                e = A.do(A.wait(p, dst_free).copy(dst[:, c:c + n, :], o))
            released(e, b)
            out = out + (e,)
        return out[-2:]

    dst_free = ()

    def rstd(srcs, n, at, ready):
        k = len(srcs)
        for i, s in enumerate(srcs):
            p = A.do(A.wait(ready, V.now, PE.now, A.now).activation(junk[:, 0:n], s, ACT.Square, accum_out=st[:, at + i:at + i + 1]))
        p = V.do(V.wait(p, G.now).tensor_scalar(st[:, at:at + k], st[:, at:at + k], 1.0 / n, EPS, ALU.mult, ALU.add))
        return G.do(G.wait(p).tensor_tensor(st[:, at:at + k], st[:, at:at + k], half[:, 0:k], ALU.pow))

    def norm_T(src, n, dst, g, ready, srcT=None):
        r = rstd([src[:, t, :] for t in range(TT)], n, 0, ready)
        buf = xn[:, :, 0:n]
        for t in range(TT):
            if t == 0:
                p0 = V.do(V.wait(r, PE.now, V.now, ready).tensor_scalar(buf[:, t, :], src[:, t, :], st[:, t:t + 1], None, ALU.mult))
            else:
                p1 = A.do(A.wait(r, PE.now, V.now, ready).mul(buf[:, t, :], src[:, t, :], st[:, t:t + 1]))

        def evac(p, o, c, k):
            return V.do(V.wait(p).tensor_tensor(dst[:, c:c + k, :], o, bc(g[:, c:c + k], T), ALU.mult))
        return to_T(lambda c, t: buf[:, t, c * P:(c + 1) * P], n // P, dst, evac, ready=(p0, p1))

    def add_x(p, o, b, pair):
        cols = x[:, :, ds(b * BLK, BLK)] if not isinstance(b, int) else x[:, :, b * BLK:(b + 1) * BLK]
        return V.do(V.wait(p, A.now).tensor_tensor(cols, cols, o, ALU.add))

    def ffn_up(ready):
        def evac(p, o, b, pair):
            g = acc[:, 2 * pair:2 * pair + 2, :]
            a = A.do(A.wait(p, last_of(f"sg{pair}")).activation(g, o[:, :, 0:256], ACT.Silu))
            v = V.do(V.wait(a).tensor_tensor(z[:, :, ds(b * 256, 256)] if not isinstance(b, int) else z[:, :, b * 256:(b + 1) * 256],
                                             g, o[:, :, 256:512], ALU.mult))
            core.last[f"sg{pair}"] = (v,)
            return v
        for j in range(3):
            core.last[f"sg{j}"] = V.now
        gemm(nT, KT, GU, evac, ready)
        return to_T(lambda c, t: z[:, t, c * P:(c + 1) * P], FT, tT, ready=V.now)

    def last_of(name):
        return core.last.get(name, ())

    def ffn_down(ready):
        PE.wait(free(0, 1, 2, 3), ready)
        for c in range(FT // 2):
            w = chunk()
            for k in range(2):
                for h in range(2):
                    for t in range(TT):
                        m = PE.e.matmul(ps[:, 2 * h + t, :], tT[:, 2 * c + k, t * P:(t + 1) * P],
                                        w[:, k * D + h * BLK:k * D + (h + 1) * BLK],
                                        start=(c == 0 and k == 0), stop=(2 * c + k == FT - 1))
            p = PE.do(m, used)
        return p

    def attention(units):
        def front(u, i):
            s, b = i % 2, 2 * (i % 2)
            PE.wait(free(b, b + 1), u.get("ready", ()))
            o = ps[:, b:b + 2, :].rearrange("p a (h k) -> p (a h) k", h=2)
            p = PE.do(u["scores"](o))
            Su, nm, sums = S[:, s], rs[:, s, 0, :], rs[:, s, 1, :]
            V.wait(p, last_of(f"S{s}"), last_of(f"rs{s}"))
            if u["add"] is not None:
                v = V.do(V.e.scalar_tensor_tensor(Su, o, u["scale"], u["add"], ALU.mult, ALU.add))
                src, scale = Su, 1.0
                released(v, b, b + 1)
                V.wait(v)
                v = V.do(V.e.tensor_reduce(nm, Su, AX_X, ALU.max, negate=True))
            else:
                v = V.do(V.e.tensor_reduce(nm, o, AX_X, ALU.max, negate=True))
                v = V.do(V.wait(v).tensor_scalar(nm, nm, u["scale"], None, ALU.mult))
                src, scale = o, u["scale"]
            A.wait(v, last_of(f"S{s}"))
            for h in range(4):
                a = A.do(A.e.activation(Su[:, h, :], src[:, h, :], ACT.Exp, bias=nm[:, h:h + 1], scale=scale,
                                        accum_out=sums[:, h:h + 1]))
            if u["add"] is None:
                released(a, b, b + 1)
            core.last[f"P{s}"] = (a,)

        def back(u, i):
            s, b = i % 2, 6 + i % 2
            v = V.do(V.wait(last_of(f"P{s}")).reciprocal(rs[:, s, 2, :], rs[:, s, 1, :]))
            PE.wait(last_of(f"P{s}"), free(4, 5))
            for h in range(4):
                for kt in range(TT):
                    m = PE.e.transpose(ps[:, 4 + h // 2, (h % 2 * TT + kt) * P:(h % 2 * TT + kt + 1) * P],
                                       S[:, s, h, kt * P:(kt + 1) * P], ident)
            p = PE.do(m)
            core.last[f"S{s}"] = (p,)
            e0 = V.do(V.wait(p, last_of(f"PT{s}")).tensor_copy(PTs[:, s, 0:4, :], ps[:, 4, :].rearrange("p (a b) -> p a b", a=4)))
            e1 = A.do(A.wait(p, last_of(f"PT{s}")).copy(PTs[:, s, 4:8, :], ps[:, 5, :].rearrange("p (a b) -> p a b", a=4)))
            released(e0, 4)
            released(e1, 5)
            PE.wait(e0, e1, free(b))
            dv = u["dv"]
            for h in range(4):
                for kt in range(TT):
                    m = PE.e.matmul(ps[:, b, h * dv:(h + 1) * dv], PTs[:, s, 2 * h + kt, :], u["value"](h, kt),
                                    start=(kt == 0), stop=(kt == TT - 1))
            p = PE.do(m)
            core.last[f"PT{s}"] = (p,)
            e = u["out"](ps[:, b, 0:4 * dv].rearrange("p (h d) -> p h d", h=4), rs[:, s, 2, :], (p, v))
            core.last[f"rs{s}"] = (e,)
            released(e, b)
            return e

        front(units[0], 0)
        for i in range(len(units)):
            if i + 1 < len(units):
                front(units[i + 1], i + 1)
            e = back(units[i], i)
        return e

    def plain_out(dst):
        def out(o, inv, ready):
            return V.do(V.wait(*ready).tensor_tensor(dst, o, bc(inv, o.shape[2]), ALU.mult))
        return out

    l_const = load(A, const[:, :], io["const"])
    l_x = load(A, x[:, :, :], io["x"])
    l_mem = load(A, z[:, :, 0:D], io["mem"])
    l_sm2 = load(A, sm2[:, :], io["smalls2"])
    G.do(G.e.memset(half[:, :], -0.5))
    relT = acc[0:33, 0, 0:8]
    hot = cbuf[0:33, 0:BLK]
    l_rel = load(A, acc[0:33, 0, 0:8], io["rel"])
    l_hot = load(A, hot, io["onehot"])
    PE.wait(l_rel, l_hot)
    p = PE.do(PE.e.matmul(ps[0:8, 6, :], relT, hot, start=True, stop=True), used)
    p = V.do(V.wait(p).tensor_copy(acc[0:8, 2:4, :], ps[0:8, 6, :].rearrange("p (a b) -> p a b", a=2)))
    released(p, 6)
    skew = io["skew"]
    p = load(A, skew.rearrange("h (r j) -> h r j", r=P), mid(acc[0:8, 2:4, :].rearrange("p a b -> p (a b)"), P), p)
    A.wait(p)
    skewed = bass.AP(skew.tensor, skew.offset + P - 1, [[BLK - 1, P], [P * BLK, 8], [1, BAND]])
    l_band = load(A, band[:, :, :], skewed)
    l_pos = load(A, st[:, 0:TT].bitcast(I32), io["positions"])
    V.wait(l_pos, l_const)
    V.do(V.e.tensor_copy(st[:, 2:4], st[:, 0:TT].bitcast(I32)))
    ang = junk[:, 0:64].rearrange("p (t f) -> p t f", t=TT)
    V.do(V.chain().tensor_tensor(ang, bc(st[:, 2:4], 32), mid(c_("freq"), TT), ALU.mult))
    MAGIC = 1.5 * 2.0 ** 23
    two_pi = 2 * pi
    c1 = float(np.float32(np.floor(two_pi * 2 ** 9) / 2 ** 9))
    c2 = float(np.float32(np.floor((two_pi - c1) * 2 ** 22) / 2 ** 22))
    c3 = float(np.float32(two_pi - c1 - c2))
    for i, shift in ((0, 0.25), (1, 0.0)):
        a, k = junk[:, 64:128].rearrange("p (t f) -> p t f", t=TT), junk[:, 128:192].rearrange("p (t f) -> p t f", t=TT)
        V.do(V.chain().tensor_scalar(k, ang, 1 / two_pi, shift, ALU.mult, ALU.add))
        V.do(V.chain().tensor_scalar(k, k, MAGIC, None, ALU.add))
        V.do(V.chain().tensor_scalar(k, k, -MAGIC, None, ALU.add))
        V.do(V.chain().scalar_tensor_tensor(a, k, -c1, ang, ALU.mult, ALU.add))
        V.do(V.chain().scalar_tensor_tensor(a, k, -c2, a, ALU.mult, ALU.add))
        V.do(V.chain().scalar_tensor_tensor(a, k, -c3, a, ALU.mult, ALU.add))
        V.do(V.chain().tensor_scalar(a, a, 2 * pi * shift, 3.1415925, ALU.add, ALU.min))
        V.do(V.chain().tensor_scalar(a, a, -3.1415925, None, ALU.max))
        p = A.do(A.wait(V.now).activation(rope[:, i], a, ACT.Sin))
        V.wait(p)
    def view(buf, a, b):
        return buf[:, a:b, :].rearrange("p a b -> p (a b)")
    kz = view(tT, 12, 16).rearrange("p (b g n) -> p b g n", b=2, g=2)
    vb = view(tT, 16, 18).rearrange("p (g m d) -> p g m d", g=2, m=4)
    pcmp = view(tT, 18, 20).rearrange("p (t g m c) -> p t g m c", t=TT, g=2, m=4)
    cmpb = view(nT, 0, 4)[:, 0:32 * 2 * N_CMP].rearrange("p (k j g c) -> p k j g c", k=2, j=16, g=2)
    kpz = nT[:, 4:6, :]
    kcz = sb("kcz", [P, 2, 16])
    hidT = sb("hidT", [P, 2, 2, 32])
    cmp_in = tT[:, 8:12, :].rearrange("p a b -> p (a b)").rearrange("p (t k r d) -> p t k r d", t=TT, k=4, r=2)
    r = rstd([z[:, t, 0:D] for t in range(TT)], D, 4, (l_mem, V.now))
    for t in range(TT):
        p = V.do(V.wait(r).tensor_scalar(xn[:, t, :], z[:, t, 0:D], st[:, 4 + t:5 + t], None, ALU.mult))
    to_T(lambda c, t: xn[:, t, c * P:(c + 1) * P], KT, memT, ready=p)
    for e in core.engines:
        e.wait(l_const, l_x, l_band, l_sm2, l_mem)
    sm_count = Count(core, "s_sm")

    with core.loop(DEPTH, meet=True) as layer:
        A.e.dma_start(sm[:, :], io["smalls"][ds(layer, 1), :, :].rearrange("a p n -> p (a n)")).then_inc(sm_count.h, 16)
        l_sm = sm_count.add(16)
        for e in core.engines:
            e.wait(l_sm)
        n = norm_T(x[:, :, :], D, nT, s1("mix"), ())

        def evac_gate(p, o, b, pair):
            return A.do(A.wait(p).activation(z[:, :, ds(b * BLK, BLK)], o, ACT.Sigmoid))

        def evac_z(p, o, b, pair):
            dst = z[:, :, ds(b * BLK, BLK)] if not isinstance(b, int) else z[:, :, b * BLK:(b + 1) * BLK]
            if pair == 1:
                return A.do(A.wait(p).copy(dst, o))
            return V.do(V.wait(p).tensor_copy(dst, o))
        gemm(nT, KT, 6, evac_gate, n)
        gemm(nT, KT, 6, evac_z, n, first=6)
        z_done = (V.now, A.now)
        V.wait(z_done, PE.now)
        for buf in (kz, vb, pcmp, kpz, kcz[:, :, :]):
            zeroed = V.do(V.e.memset(buf, 0.0))

        p = A.do(A.wait(z_done).activation(ostage[:, :, :], z[:, :, Z_GLU + 512:Z_GLU + 1024], ACT.Sigmoid))
        g_n = A.do(A.wait(z_done).activation(z[:, :, Z_GN:Z_GN + 24], z[:, :, Z_GN:Z_GN + 24], ACT.Sigmoid))
        p = V.do(V.wait(p).tensor_tensor(ostage[:, :, :], ostage[:, :, :], z[:, :, Z_GLU:Z_GLU + 512], ALU.mult))
        LEFT = CONV_W - 1
        u = cbuf[:, 0:CONV_CT * (LEFT + T)].rearrange("p (c n) -> p c n", c=CONV_CT)
        m0 = V.do(V.e.memset(u[:, :, 0:LEFT], 0.0))

        def evac_u(p, o, c, k):
            return A.do(A.wait(p).copy(u[:, c:c + k, LEFT:LEFT + T], o))
        e = to_T(lambda c, t: ostage[:, t, c * P:(c + 1) * P], CONV_CT, u, evac_u, p)
        V.wait(e, m0)
        cw = s1("conv_w").rearrange("p (c k) -> p c k", c=CONV_CT)
        taps = {}
        for k in range(CONV_W):
            for c in range(CONV_CT):
                V.wait(taps.get(c, ()))
                if k == 0:
                    ins = V.e.tensor_scalar(acc[:, c, :], u[:, c, 0:T], cw[:, c, 0:1], s1("conv_b")[:, c:c + 1], ALU.mult, ALU.add)
                else:
                    ins = V.e.scalar_tensor_tensor(acc[:, c, :], u[:, c, k:k + T], cw[:, c, k:k + 1], acc[:, c, :], ALU.mult, ALU.add)
                taps[c] = V.do(ins)
        conv_done = V.now
        p = V.do(V.wait(z_done).tensor_copy(cmp_in[:, 0], z[:, 0, Z_KV:Z_KV + 256].rearrange("p (k d) -> p k d", k=4).unsqueeze(2).to_broadcast([P, 4, 2, 64])))
        p = V.do(V.wait(z_done).tensor_copy(cmp_in[:, 1], z[:, 1, Z_KV:Z_KV + 256].rearrange("p (k d) -> p k d", k=4).unsqueeze(2).to_broadcast([P, 4, 2, 64])))
        cmp_ready = p
        qT = tT
        q_ready = to_T(lambda c, t: z[:, t, Z_Q + c * P:Z_Q + (c + 1) * P], 4, qT, ready=z_done)

        def evac_k(p, o, c, k):
            a = A.do(A.wait(p, zeroed).copy(kz[0:64, :, 0, :], o[0:64]))
            return A.do(A.e.copy(kz[64:128, :, 1, :], o[64:128]))
        k_ready = to_T(lambda c, t: z[:, t, Z_KV + (2 + 2 * c) * P:Z_KV + (3 + 2 * c) * P], 2, None, evac_k, z_done)

        pos = s1("pos").rearrange("p (k j) -> p k j", k=2)

        def evac_b(p, o, c, k):
            V.wait(p)
            for i in range(k):
                kind, g = (c + i) // 2, (c + i) % 2
                for lo in range(2):
                    half_ = slice(64 * lo, 64 * lo + 64)
                    src = o[half_, i, :]
                    src = bass.AP(src.tensor, src.offset + lo, [list(src.ap[0]), [2, 16], [16, N_CMP]])
                    v = V.do(V.e.tensor_tensor(cmpb[half_, kind, :, g, :], src, bc(pos[half_, kind, :], N_CMP), ALU.add))
            return v
        b_ready = to_T(lambda c, t: cmp_in[:, t, c].rearrange("p r d -> p (r d)"), 4, None, evac_b, cmp_ready)
        for kind in range(2):
            banks = (6, 7) if kind == 0 else (4, 5)
            PE.wait(b_ready, free(*banks))
            for cc in range(2):
                w = chunk()
                for j in range(8):
                    for ht in range(2):
                        m = PE.e.matmul(ps[:, banks[ht], 0:30], w[:, j * 256 + ht * P:j * 256 + (ht + 1) * P],
                                        cmpb[:, kind, 8 * cc + j, :, :].rearrange("p g c -> p (g c)"),
                                        start=(cc == 0 and j == 0), stop=(cc == 1 and j == 7))
                p = PE.do(m, used)
            for ht in range(2):
                a = A.do(A.wait(p).activation(hidT[:, kind, ht, 0:30], ps[:, banks[ht], 0:30], ACT.Gelu_apprx_tanh,
                                              bias=s1("b1")[:, 2 * kind + ht:2 * kind + ht + 1]))
                released(a, banks[ht])
        w2k, w2v = s1("w2k").rearrange("p (h n) -> p h n", h=2), s1("w2v").rearrange("p (h n) -> p h n", h=2)
        PE.wait(a, free(6, 7))
        for ht in range(2):
            m = PE.e.matmul(ps[:, 6, 0:30], w2k[:, ht, :], hidT[:, 0, ht, 0:30], start=(ht == 0), stop=(ht == 1))
        p = PE.do(m)
        for g in range(2):
            for ht in range(2):
                m = PE.e.matmul(ps[0:15, 7, g * 64:(g + 1) * 64], hidT[:, 1, ht, g * 15:(g + 1) * 15], w2v[:, ht, :],
                                start=(ht == 0), stop=(ht == 1))
        q = PE.do(m)
        V.wait(p, zeroed)
        V.do(V.e.tensor_copy(kcz[0:64, 0, 0:15], ps[0:64, 6, 0:15]))
        released(V.do(V.e.tensor_copy(kcz[64:128, 1, 0:15], ps[64:128, 6, 15:30])), 6)
        A.wait(q)
        for m_ in range(4):
            a = A.do(A.e.copy(vb[32 * m_:32 * m_ + 15, :, m_, :], ps[0:15, 7, 0:128].rearrange("p (g d) -> p g d", g=2)))
        released(a, 7)
        kv_ready = (V.now, A.now)
        PE.wait(kv_ready, q_ready, free(6, 7))
        for t in range(TT):
            for m_ in range(4):
                m = PE.e.matmul(ps[:, 6, (t * 4 + m_) * 32:(t * 4 + m_ + 1) * 32], qT[:, m_, t * P:(t + 1) * P],
                                kcz[:, :, :].rearrange("p g c -> p (g c)"), start=True, stop=True)
        p = PE.do(m)
        sc = S[:, 0, 0, 0:TT * 8 * 16].rearrange("p (t h c) -> p t h c", t=TT, h=8)
        V.wait(p, PE.now)
        for t in range(TT):
            first = 31 + P * (1 - t)
            V.do(V.e.scalar_tensor_tensor(sc[:, t, :, 0:N_CMP], ps[:, 6, t * 128:(t + 1) * 128].rearrange("p (h c) -> p h c", h=8)[:, :, 0:N_CMP],
                                          0.125, band[:, :, first:first + 16 * (N_CMP - 1) + 1:16], ALU.mult, ALU.add))
        released(V.now[0], 6)
        scf = sc.rearrange("p t h c -> p (t h) c")[:, :, 0:N_CMP]
        cst = S[:, 1, 0, 0:128]
        cmx, csum, cf = cst[:, 0:16], cst[:, 16:32], cst[:, 32:48]
        V.do(V.chain().tensor_reduce(cmx, scf, AX_X, ALU.max))
        V.do(V.chain().tensor_tensor(scf, scf, bc(cmx, N_CMP), ALU.subtract))
        p = A.do(A.wait(V.now).activation(scf, scf, ACT.Exp))
        V.do(V.wait(p).tensor_reduce(csum, scf, AX_X, ALU.add))
        for t in range(TT):
            pc = V.do(V.wait(p, PE.now).tensor_copy(pcmp[:, t, :, :, 0:N_CMP], sc[:, t, :, 0:N_CMP].rearrange("p (m g) c -> p g m c", m=4)))
        V.do(V.chain().reciprocal(cf, csum))
        cf4 = cf.rearrange("p (t h) -> p t h", t=TT)
        gates = z[:, :, Z_GN:Z_GN + 24].rearrange("p t (j h) -> p t j h", j=3)
        V.do(V.wait(g_n, V.now).tensor_tensor(cf4, cf4, gates[:, :, 0, :], ALU.mult))
        V.do(V.chain().tensor_tensor(cf4, cf4, bc(c_("valid"), 8), ALU.mult))
        PE.wait(pc, free(7, 6))
        for t in range(TT):
            for g in range(2):
                m = PE.e.transpose(ps[:, 7, (2 * t + g) * P:(2 * t + g + 1) * P], pcmp[:, t, g].rearrange("p m c -> p (m c)"), ident)
        p = PE.do(m)
        pcT = S[:, 1, 2:4, :].rearrange("p a b -> p (a b)")
        a = A.do(A.wait(p).copy(pcT, ps[:, 7, :]))
        released(a, 7)
        PE.wait(a, free(4, 5))
        for t in range(TT):
            for g in range(2):
                m = PE.e.matmul(ps[:, 4 + t, g * 256:(g + 1) * 256], pcT[:, (2 * t + g) * P:(2 * t + g + 1) * P],
                                vb[:, g].rearrange("p m d -> p (m d)"), start=True, stop=True)
        p = PE.do(m)
        ov = ostage[:, :, :].rearrange("p t (m g d) -> p t m g d", m=4, g=2)
        cfg = cf.rearrange("p (t m g) -> p t m g", t=TT, m=4)
        for t in range(TT):
            for g in range(2):
                v = V.do(V.wait(p, V.now).tensor_tensor(ov[:, t, :, g, :], ps[:, 4 + t, g * 256:(g + 1) * 256].rearrange("p (m d) -> p m d", m=4),
                                                 bc(cfg[:, t, :, g], 64), ALU.mult))
            released(v, 4 + t)
        for nm in ("S0", "S1", "rs0", "rs1", "PT0", "PT1"):
            core.last[nm] = V.now + A.now + PE.now
        fac = sb("fac", [P, 2, 4])
        with core.loop(2) as br:
            units = []
            for t in range(TT):
                for mp in range(2):
                    def scores(o, t=t, mp=mp):
                        for i in range(2):
                            m = PE.e.matmul(o[:, 2 * i:2 * i + 2, :].rearrange("p g k -> p (g k)"), qT[:, 2 * mp + i, t * P:(t + 1) * P],
                                            kz[:, ds(br, 1), :, :].rearrange("p a g k -> p (a g k)"), start=True, stop=True)
                        return m

                    def out(o, inv, ready, t=t, mp=mp):
                        f = fac[:, mp, :]
                        V.do(V.wait(*ready, V.now).tensor_tensor(f, inv, z[:, t, ds(Z_GN + 8 + br * 8 + 4 * mp, 4)], ALU.mult))
                        tmp = acc[:, 4 + mp, :].rearrange("p (h d) -> p h d", h=4)
                        e = V.do(V.chain().tensor_tensor(tmp, o, bc(f, 64), ALU.mult))
                        dst = ostage[:, t, 256 * mp:256 * (mp + 1)].rearrange("p (h d) -> p h d", h=4)
                        V.do(V.chain().tensor_tensor(dst, dst, tmp, ALU.add))
                        return e
                    off = P * (1 - t)
                    units.append(dict(
                        scores=scores, scale=0.125, add=band[:, 4 * mp:4 * mp + 4, off:off + T], dv=64, out=out, ready=(k_ready, q_ready),
                        value=lambda h, kt: z[:, kt, ds(Z_KV + 3 * P + br * (2 * P) + h % 2 * 64, 64)]))
            attention(units)
        nsa_done = V.now

        ones = c_("ones")
        PE.wait(conv_done, free(6, 7), nsa_done)
        for c in range(CONV_CT):
            m = PE.e.matmul(ps[:, 6, 0:T], ones, acc[:, c, :], start=(c == 0), stop=(c == CONV_CT - 1))
        p = PE.do(m)
        acc4 = acc[:, 0:4, :]
        sq = cbuf[:, 0:4 * T].rearrange("p (c n) -> p c n", c=4)
        mu = S[:, 0, 0, :]
        rd = S[:, 0, 1, :]
        V.do(V.wait(p).tensor_scalar(mu, ps[:, 6, 0:T], 1.0 / 512, None, ALU.mult))
        V.do(V.chain().tensor_tensor(acc4, acc4, mid(mu, 4), ALU.subtract))
        p = A.do(A.wait(V.now, PE.now).activation(sq, acc4, ACT.Square))
        PE.wait(p)
        for c in range(CONV_CT):
            m = PE.e.matmul(ps[:, 7, 0:T], ones, sq[:, c, :], start=(c == 0), stop=(c == CONV_CT - 1))
        p = PE.do(m)
        V.do(V.wait(p).tensor_scalar(rd, ps[:, 7, 0:T], 1.0 / 512, EPS, ALU.mult, ALU.add))
        released(V.now[0], 6, 7)
        p = G.do(G.wait(V.now).tensor_tensor(rd, rd, half[:, :], ALU.pow))
        V.do(V.wait(p).tensor_tensor(acc4, acc4, mid(rd, 4), ALU.mult))
        A.wait(V.now)
        for c in range(CONV_CT):
            p = A.do(A.e.activation(acc[:, c, :], acc[:, c, :], ACT.Silu, bias=s1("ln_b")[:, c:c + 1], scale=s1("ln_g")[:, c:c + 1]))
        conv_T = p

        merged = xn

        def evac_merge(j):
            def evac(p, o, b, pair):
                g = z[:, :, j * D + b * BLK:j * D + (b + 1) * BLK]
                dst = merged[:, :, b * BLK:(b + 1) * BLK]
                if j == 0:
                    return V.do(V.wait(p).tensor_tensor(dst, o, g, ALU.mult))
                e = V.do(V.wait(p, G.now).tensor_tensor(g, o, g, ALU.mult))
                V.do(V.chain().tensor_tensor(dst, dst, g, ALU.add))
                return e
            return evac
        gemm(acc, 4, 2, evac_merge(0), conv_T)
        e = to_T(lambda c, t: ostage[:, t, c * P:(c + 1) * P], 4, tT, ready=nsa_done)
        gemm(tT, 4, 2, evac_merge(1), e)

        r1 = rstd([z[:, t, Z_CQ:Z_CQ + Q_RANK] for t in range(TT)], Q_RANK, 4, ())
        r2 = rstd([z[:, t, Z_CKV:Z_CKV + KV_RANK] for t in range(TT)], KV_RANK, 6, ())
        for t in range(TT):
            V.do(V.wait(r1).tensor_scalar(z[:, t, Z_CQ:Z_CQ + Q_RANK], z[:, t, Z_CQ:Z_CQ + Q_RANK], st[:, 4 + t:5 + t], None, ALU.mult))
            V.do(V.wait(r2).tensor_scalar(z[:, t, Z_CKV:Z_CKV + KV_RANK], z[:, t, Z_CKV:Z_CKV + KV_RANK], st[:, 6 + t:7 + t], None, ALU.mult))
        gq = sm[:, S1["mq"][0]:S1["mkv"][1]]
        cT = tT[:, 4:9, :]

        def evac_c(p, o, c, k):
            return V.do(V.wait(p).tensor_tensor(cT[:, c:c + k, :], o, bc(gq[:, c:c + k], T), ALU.mult))
        e = to_T(lambda c, t: z[:, t, Z_CQ + c * P:Z_CQ + (c + 1) * P], 5, cT, evac_c, V.now)
        QN, QP, KN, VN = 3072, 3584, 4096, 4608
        for pair, (width, at) in enumerate(((512, QN), (256, QP))):
            PE.wait(e, free(2 * pair, 2 * pair + 1), V.now)
            w = chunk()
            for k in range(3):
                for t in range(TT):
                    m = PE.e.matmul(ps[:, 2 * pair + t, 0:width], cT[:, k, t * P:(t + 1) * P], w[:, k * width:(k + 1) * width],
                                    start=(k == 0), stop=(k == 2))
            p = PE.do(m, used)
            v = V.do(V.wait(p, PE.now).tensor_copy(z[:, :, at:at + width], ps[:, 2 * pair:2 * pair + 2, 0:width]))
            released(v, 2 * pair, 2 * pair + 1)
        PE.wait(free(4, 5, 0, 1))
        w = chunk()
        for hf, b in ((0, 4), (1, 0)):
            for k in range(2):
                for t in range(TT):
                    m = PE.e.matmul(ps[:, b + t, :], cT[:, 3 + k, t * P:(t + 1) * P], w[:, k * D + hf * BLK:k * D + (hf + 1) * BLK],
                                    start=(k == 0), stop=(k == 1))
        p = PE.do(m, used)
        a = A.do(A.wait(p, PE.now, V.now).copy(z[:, :, KN:KN + 512], ps[:, 4:6, :]))
        released(a, 4, 5)
        v = A.do(A.e.copy(z[:, :, VN:VN + 512], ps[:, 0:2, :]))
        released(v, 0, 1)
        V.do(V.wait(A.now).tensor_copy(z[:, :, QP + 256:QP + 320], z[:, :, Z_KR:Z_KR + 64]))
        rot = tT[:, 16:19, :].rearrange("p a b -> p (a b)").rearrange("p (t h r) -> p t h r", t=TT, h=6)
        tmp = tT[:, 19:21, :].rearrange("p a b -> p (a b)")[:, 0:320].rearrange("p (h f) -> p h f", h=10)
        for t in range(TT):
            src = z[:, t, QP:QP + 320].rearrange("p (h r) -> p h r", h=5)
            x1, x2 = src[:, :, 0:32], src[:, :, 32:64]
            cos, sin = mid(rope[:, 0, t, :], 5), mid(rope[:, 1, t, :], 5)
            y1, y2, t1, t2 = rot[:, t, 0:5, 0:32], rot[:, t, 0:5, 32:64], tmp[:, 0:5, :], tmp[:, 5:10, :]
            V.do(V.chain().tensor_tensor(y1, x1, cos, ALU.mult))
            V.do(V.e.tensor_tensor(t1, x2, sin, ALU.mult))
            V.do(V.e.tensor_tensor(y2, x2, cos, ALU.mult))
            V.do(V.e.tensor_tensor(t2, x1, sin, ALU.mult))
            V.do(V.chain().tensor_tensor(y1, y1, t1, ALU.subtract))
            V.do(V.e.tensor_tensor(y2, y2, t2, ALU.add))
            V.do(V.chain().tensor_copy(rot[:, t, 5, :], rot[:, t, 4, :]))
        e1 = to_T(lambda c, t: z[:, t, QN + c * P:QN + (c + 1) * P], 4, tT, ready=(V.now, A.now))
        kT = tT[:, 9:13, :]
        e2 = to_T(lambda c, t: z[:, t, KN + c * P:KN + (c + 1) * P], 4, kT, ready=(V.now, A.now))
        e3 = to_T(lambda c, t: rot[:, t, 2 * c:2 * c + 2, :].rearrange("p h r -> p (h r)"), 2, tT[:, 13:15, :], ready=V.now)

        def evac_kp(p, o, c, k):
            A.do(A.wait(p).copy(kpz[0:64, 0, :], o[0:64, 0, :]))
            return A.do(A.e.copy(kpz[64:128, 1, :], o[64:128, 0, :]))
        e4 = to_T(lambda c, t: rot[:, t, 4:6, :].rearrange("p h r -> p (h r)"), 1, None, evac_kp, V.now)
        units = []
        for t in range(TT):
            def scores(o, t=t):
                for h in range(4):
                    PE.e.matmul(o[:, h, :], tT[:, h, t * P:(t + 1) * P], kT[:, h, :], start=True, stop=False)
                    m = PE.e.matmul(o[:, h, :], tT[:, 13 + h // 2, t * P:(t + 1) * P], kpz[:, h % 2, :], start=False, stop=True)
                return m
            off = P * (1 - t)
            units.append(dict(scores=scores, scale=192.0 ** -0.5, add=mid(mask[:, off:off + T], 4), dv=P, ready=(e1, e2, e3, e4),
                              value=lambda h, kt: z[:, kt, VN + h * P:VN + (h + 1) * P],
                              out=plain_out(ostage[:, t, :].rearrange("p (h d) -> p h d", h=4))))
        attention(units)
        e = to_T(lambda c, t: ostage[:, t, c * P:(c + 1) * P], 4, cT, ready=V.now)
        gemm(cT, 4, 2, evac_merge(2), e)
        e = to_T(lambda c, t: merged[:, t, c * P:(c + 1) * P], KT, nT, ready=V.now)
        gemm(nT, KT, 2, add_x, e)

        g = s1("mem")
        mn = tT[:, 4:12, :]
        e = V.do(V.wait(PE.now).tensor_tensor(mn, memT, bc(g, T), ALU.mult))
        XK, XV, XQ = 0, 512, 1024

        def evac_to(at):
            def evac(p, o, b, pair):
                return A.do(A.wait(p, V.now).copy(z[:, :, at + b * BLK:at + (b + 1) * BLK], o))
            return evac
        gemm(mn, KT, 2, evac_to(0), e)
        n = norm_T(x[:, :, :], D, nT, s1("xattn"), V.now)
        gemm(nT, KT, 1, evac_to(XQ), n)
        kT = tT[:, 12:16, :]
        e1 = to_T(lambda c, t: z[:, t, XQ + c * P:XQ + (c + 1) * P], 4, tT, ready=A.now)
        e2 = to_T(lambda c, t: z[:, t, XK + c * P:XK + (c + 1) * P], 4, kT, ready=A.now)
        units = []
        for t in range(TT):
            def scores(o, t=t):
                for h in range(4):
                    m = PE.e.matmul(o[:, h, :], tT[:, h, t * P:(t + 1) * P], kT[:, h, :], start=True, stop=True)
                return m
            units.append(dict(scores=scores, scale=P ** -0.5, add=None, dv=P, ready=(e1, e2),
                              value=lambda h, kt: z[:, kt, XV + h * P:XV + (h + 1) * P],
                              out=plain_out(ostage[:, t, :].rearrange("p (h d) -> p h d", h=4))))
        attention(units)
        e = to_T(lambda c, t: ostage[:, t, c * P:(c + 1) * P], 4, cT, ready=V.now)
        gemm(cT, 4, 2, add_x, e)
        n = norm_T(x[:, :, :], D, nT, s1("ffn"), V.now)
        p = ffn_down(ffn_up(n))
        for hf in range(2):
            released(add_x(p, ps[:, 2 * hf:2 * hf + 2, :], hf, 0), 2 * hf, 2 * hf + 1)
        PE.wait(free(7))
        for _ in range(2):
            chunk()
            p = PE.do(PE.e.matmul(ps[:, 7, 0:1], ident, ident[:, 0:1], start=True, stop=True), used)

    gain = big[:, 4096:4096 + D]
    wk = sb("wk", [P, 12, 32])
    loading = {}

    def load_gain(i):
        loading["gain"] = load(A, gain, io["gains"][i].partition_broadcast(P), V.now, PE.now)

    def scale_rows(buf, r):
        for t in range(TT):
            v = V.do(V.wait(r, loading["gain"], PE.now).scalar_tensor_tensor(buf[:, t, :], buf[:, t, :], st[:, t:t + 1], gain, ALU.mult, ALU.mult))
        return v

    def post_norm(factor, i, ready):
        r = rstd([xn[:, t, :] for t in range(TT)], D, 0, ready)
        scale_rows(xn, r)
        load_gain((i + 1) % N_GAIN)
        for t in range(TT):
            V.do(V.wait(V.now).scalar_tensor_tensor(x[:, t, :], xn[:, t, :], factor, x[:, t, :], ALU.mult, ALU.add))
        return V.now

    def evac_xn(p, o, b, pair):
        dst = xn[:, :, b * BLK:(b + 1) * BLK]
        if b % 2:
            return A.do(A.wait(p, V.now).copy(dst, o))
        return V.do(V.wait(p, A.now).tensor_copy(dst, o))

    def ffn2(pre, post):
        n = norm_T(x[:, :, :], D, nT, s2("pre", 8 * pre, 8 * pre + 8), V.now)
        p = ffn_down(ffn_up(n))
        ends = []
        for hf in range(2):
            ends.append(evac_xn(p, ps[:, 2 * hf:2 * hf + 2, :], hf, 0))
            released(ends[-1], 2 * hf, 2 * hf + 1)
        post_norm(0.5, post, ends)

    def softplus(out, src, k, tmp):
        m, e, zz, z2 = (tmp[:, i, 0:k] for i in range(4))
        V.do(V.chain().tensor_scalar(m, src, 0.0, None, ALU.max))
        V.do(V.chain().scalar_tensor_tensor(e, src, -1.0, src, ALU.mult, ALU.max))
        a = A.do(A.wait(V.now).activation(e, e, ACT.Exp, scale=-1.0))
        V.do(V.wait(a).tensor_scalar(zz, e, 2.0, None, ALU.add))
        V.do(V.chain().reciprocal(zz, zz))
        V.do(V.chain().tensor_tensor(zz, zz, e, ALU.mult))
        V.do(V.chain().tensor_tensor(z2, zz, zz, ALU.mult))
        V.do(V.chain().tensor_scalar(e, z2, 1.0 / 15, None, ALU.mult))
        for c in (13, 11, 9, 7, 5, 3):
            V.do(V.chain().scalar_tensor_tensor(e, e, 1.0 / c, z2, ALU.add, ALU.mult))
        V.do(V.chain().scalar_tensor_tensor(e, e, 1.0, zz, ALU.add, ALU.mult))
        return V.do(V.chain().scalar_tensor_tensor(out, e, 2.0, m, ALU.mult, ALU.add))

    def conv4(tiles, left, w, b, dst, ready):
        taps = {}
        for k in range(4):
            for c in range(tiles):
                V.wait(taps.get(c, ready))
                if k == 0:
                    ins = V.e.tensor_scalar(dst[:, c, :], left[:, c, 0:T], w[:, 4 * c:4 * c + 1], b[:, c:c + 1], ALU.mult, ALU.add)
                else:
                    ins = V.e.scalar_tensor_tensor(dst[:, c, :], left[:, c, k:k + T], w[:, 4 * c + k:4 * c + k + 1], dst[:, c, :], ALU.mult, ALU.add)
                taps[c] = V.do(ins)
        return V.now

    load_gain(0)
    r = rstd([x[:, t, :] for t in range(TT)], D, 0, V.now)
    scale_rows(x, r)
    load_gain(1)
    ffn2(0, 1)

    n = norm_T(x[:, :, :], D, nT, s2("pre", 8, 16), V.now)
    gemm(nT, KT, 11, evac_z, n)
    H_Z, H_X, H_Q, H_K, H_V = 0, 1024, 2560, 3584, 4608
    PE.wait(free(4, 5), n)
    w = chunk()
    for t in range(TT):
        for k in range(KT):
            m = PE.e.matmul(ps[:, 4 + t, 0:24], nT[:, k, t * P:(t + 1) * P], w[:, k * 24:(k + 1) * 24], start=(k == 0), stop=(k == KT - 1))
    p = PE.do(m, used)
    dtb, fbb = mid(s2("dtb"), TT), mid(s2("fb"), TT)
    raw, dt, dA = wk[:, 0:2, :], wk[:, 2:4, 0:16], wk[:, 4:6, 0:16]
    V.do(V.wait(p).tensor_tensor(raw[:, :, 0:16], ps[:, 4:6, 0:16], dtb, ALU.add))
    V.do(V.e.tensor_tensor(raw[:, :, 16:24], ps[:, 4:6, 16:24], fbb, ALU.add))
    released(V.now[0], 4, 5)
    V.do(V.chain().tensor_scalar(raw[:, :, 16:24], raw[:, :, 16:24], -1.0, None, ALU.mult))
    sp = acc[:, 0:2, 0:24]
    for t in range(TT):
        softplus(sp[:, t, :], raw[:, t, 0:24], 24, acc[:, 2:6, :])
    a_neg = wk[:, 6, 0:16]
    p = A.do(A.wait(V.now).activation(a_neg, s2("alog"), ACT.Exp))
    V.do(V.wait(p, V.now).tensor_scalar(a_neg, a_neg, -1.0, None, ALU.mult))
    V.do(V.chain().tensor_copy(dt, sp[:, :, 0:16]))
    V.do(V.chain().tensor_tensor(dA, dt, mid(a_neg, TT), ALU.mult))
    lf = wk[:, 7:9, 0:8]
    V.do(V.e.tensor_scalar(lf, sp[:, :, 16:24], -1.0, None, ALU.mult))
    up = c_("upper")
    tri = up[:, P:2 * P]
    PE.wait(V.now, free(6))
    for t in range(TT):
        PE.e.matmul(ps[:, 6, 16 * t:16 * t + 16], tri, dA[:, t, :], start=True, stop=True)
    PE.e.matmul(ps[:, 6, 32:40], tri, lf[:, 0, :], start=True, stop=True)
    PE.e.matmul(ps[:, 6, 40:48], c_("ones"), lf[:, 0, :], start=True, stop=False)
    p = PE.do(PE.e.matmul(ps[:, 6, 40:48], tri, lf[:, 1, :], start=False, stop=True))
    cs = sb("cs", [P, 48])
    V.do(V.wait(p).tensor_copy(cs[:, :], ps[:, 6, 0:48]))
    released(V.now[0], 6)
    acs, cumq = cs[:, 0:32].rearrange("p (t h) -> p t h", t=TT), cs[:, 32:48].rearrange("p (t h) -> p t h", t=TT)
    eacs = wk[:, 9, 0:16]
    A.do(A.wait(V.now).activation(eacs, acs[:, 1, :], ACT.Exp))

    cin = big[:, 0:12 * (T + 3)].rearrange("p (c n) -> p c n", c=12)
    m0 = G.do(G.wait(PE.now, V.now).memset(cin[:, :, 0:3], 0.0))

    def evac_cin(p, o, c, k):
        return A.do(A.wait(p, m0).copy(cin[:, c:c + k, 3:3 + T], o))
    e = to_T(lambda c, t: z[:, t, H_X + c * P:H_X + (c + 1) * P], 12, None, evac_cin, (V.now, A.now))
    xbcT = tT[:, 0:12, :]
    v = conv4(12, cin, s2("cw"), s2("cb"), xbcT, (e, m0, PE.now))
    a = A.do(A.wait(v).activation(xbcT, xbcT, ACT.Silu))
    for t in range(TT):
        for q, (first, n_) in enumerate(((0, 4), (4, 4), (8, 2))):
            b = 6 + bank_turn[0] % 2
            bank_turn[0] += 1
            PE.wait(free(b), a)
            for i in range(n_):
                m = PE.e.transpose(ps[:, b, i * P:(i + 1) * P], tT[:, first + i, t * P:(t + 1) * P], ident)
            p = PE.do(m)
            dst = z[:, t, H_X + first * P:H_X + (first + n_) * P]
            if q % 2:
                released(A.do(A.wait(p).copy(dst, ps[:, b, 0:n_ * P])), b)
            else:
                released(V.do(V.wait(p).tensor_copy(dst, ps[:, b, 0:n_ * P])), b)
    BT, CT = tT[:, 8:10, :], tT[:, 10:12, :]
    tok_ready = (V.now, A.now)
    Sf = S[:, :, :, :].rearrange("p a b c -> p (a b c)").rearrange("p (h l) -> p h l", h=16)
    LT = PTs[:, :, :, :].rearrange("p a b c -> p (a b) c")
    S0 = acc[:, 0:4, :].rearrange("p a b -> p (a b)")
    X = xn
    for t in range(TT):
        xt = z[:, t, H_X:H_X + D]
        x3 = xt.rearrange("p (h d) -> p h d", h=16)
        V.wait(tok_ready, PE.now)
        V.do(V.chain().tensor_tensor(Sf, bc(dA[:, t, :], P), mid(tri, 16), ALU.mult))
        V.do(V.e.tensor_tensor(X[:, t, :].rearrange("p (h d) -> p h d", h=16), x3, bc(dt[:, t, :], 64), ALU.mult))
        PE.wait(V.now, free(0, 1, 2, 3))
        for b in range(4):
            m = PE.e.matmul(ps[:, b, :], c_("ones"), Sf[:, 4 * b:4 * b + 4, :].rearrange("p h l -> p (h l)"), start=True, stop=True)
        p = PE.do(m)
        PE.wait(free(4))
        for g in range(2):
            m = PE.e.matmul(ps[:, 4, g * P:(g + 1) * P], BT[:, g, t * P:(t + 1) * P], CT[:, g, t * P:(t + 1) * P], start=True, stop=True)
        pcb = PE.do(m)
        V.do(V.wait(p).tensor_tensor(LT, ps[:, 0:4, :].rearrange("p a (b l) -> p (a b) l", b=4), bc(acs[:, t, :], P), ALU.subtract))
        released(V.now[0], 0, 1, 2, 3)
        V.do(V.chain().tensor_tensor(LT, LT, mid(c_("maskU"), 16), ALU.add))
        a = A.do(A.wait(V.now).activation(LT, LT, ACT.Exp))
        V.wait(a)
        if t == 0:
            Xd = nT[:, 0:4, :].rearrange("p a b -> p (a b)")
            V.do(V.wait(PE.now).tensor_tensor(Xd.rearrange("p (h d) -> p h d", h=16), X[:, 0, :].rearrange("p (h d) -> p h d", h=16),
                                              LT[:, :, P - 1:P].to_broadcast([P, 16, 64]), ALU.mult))
            xd_ready = V.now
        for g in range(2):
            V.do(V.wait(pcb, V.now).tensor_tensor(LT[:, 8 * g:8 * g + 8, :], LT[:, 8 * g:8 * g + 8, :], mid(ps[:, 4, g * P:(g + 1) * P], 8), ALU.mult))
        released(V.now[0], 4)
        PE.wait(V.now, free(5, 6))
        for h in range(16):
            m = PE.e.matmul(ps[:, 5 + h // 8, h % 8 * 64:(h % 8 + 1) * 64], LT[:, h, :], X[:, t, h * 64:(h + 1) * 64], start=True, stop=True)
        py = PE.do(m)
        V.do(V.wait(V.now).tensor_tensor(x3, x3, bc(s2("dskip"), 64), ALU.mult))
        V.do(V.wait(py, V.now).tensor_tensor(xt, xt, ps[:, 5:7, :].rearrange("p a b -> p (a b)"), ALU.add))
        released(V.now[0], 5, 6)
        if t == 0:
            PE.wait(xd_ready, free(0, 1))
            for g in range(2):
                m = PE.e.matmul(ps[:, g, :], z[:, 0, H_X + D + g * P:H_X + D + (g + 1) * P], Xd[:, g * 512:(g + 1) * 512], start=True, stop=True)
            p = PE.do(m)
            s0_ready = A.do(A.wait(p, V.now).copy(S0, ps[:, 0:2, :].rearrange("p a b -> p (a b)")))
            released(s0_ready, 0, 1)
        else:
            PE.wait(s0_ready, free(0, 1))
            for g in range(2):
                m = PE.e.matmul(ps[:, g, :], CT[:, g, P:2 * P], S0[:, g * 512:(g + 1) * 512], start=True, stop=True)
            p = PE.do(m)
            yo = nT[:, 4:8, :].rearrange("p a b -> p (a b)")
            V.do(V.wait(p, A.now).tensor_tensor(yo.rearrange("p (h d) -> p h d", h=16), ps[:, 0:2, :].rearrange("p a (h d) -> p (a h) d", h=8), bc(eacs, 64), ALU.mult))
            released(V.now[0], 0, 1)
            V.do(V.chain().tensor_tensor(xt, xt, yo, ALU.add))
        a = A.do(A.wait(V.now).activation(z[:, t, 0:D], z[:, t, 0:D], ACT.Silu))
        V.do(V.wait(a).tensor_tensor(z[:, t, 0:D], z[:, t, 0:D], xt, ALU.mult))
    groups = [z[:, t, g * 512:(g + 1) * 512] for t in range(TT) for g in range(2)]
    r = rstd(groups, 512, 0, V.now)
    for i, s in enumerate(groups):
        V.do(V.wait(r).tensor_scalar(s, s, st[:, i:i + 1], None, ALU.mult))

    def evac_y(p, o, c, k):
        return V.do(V.wait(p).tensor_tensor(tT[:, c:c + k, :], o, bc(s2("ng", c, c + k), T), ALU.mult))
    to_T(lambda c, t: z[:, t, c * P:(c + 1) * P], 8, None, evac_y, (V.now, PE.now))

    for hg in range(2):
        V.wait(PE.now, A.now)
        for i in range(TT):
            V.do(V.chain().tensor_tensor(S[:, i], bc(lf[:, i, 4 * hg:4 * hg + 4], T), mid(up[:, P * (1 - i):P * (1 - i) + T], 4), ALU.mult))
        PE.wait(V.now, free(0, 1))
        for b in range(2):
            for i in range(TT):
                m = PE.e.matmul(ps[:, b, :], c_("ones"), S[:, i, 2 * b:2 * b + 2, :].rearrange("p h k -> p (h k)"), start=(i == 0), stop=(i == 1))
        p = PE.do(m)
        R = [z[:, t, H_X:H_X + D].rearrange("p (h k) -> p h k", h=4) for t in range(TT)]
        o = ps[:, 0:2, :].rearrange("p a (h k) -> p (a h) k", h=2)
        for t in range(TT):
            off = P * (1 - t)
            V.do(V.wait(p, V.now).scalar_tensor_tensor(R[t], o, -1.0, mid(mask[:, off:off + T], 4), ALU.mult, ALU.add))
            released(V.now[0], 0, 1)
            V.do(V.chain().tensor_tensor(R[t], R[t], bc(cumq[:, t, 4 * hg:4 * hg + 4], T), ALU.add))

        e1 = to_T(lambda c, t: z[:, t, H_Q + (4 * hg + c) * P:H_Q + (4 * hg + c + 1) * P], 4, nT[:, 0:4, :], ready=(V.now, A.now))
        e2 = to_T(lambda c, t: z[:, t, H_K + (4 * hg + c) * P:H_K + (4 * hg + c + 1) * P], 4, nT[:, 4:8, :], ready=(V.now, A.now))
        for nm in ("S0", "S1", "rs0", "rs1", "PT0", "PT1"):
            core.last[nm] = V.now + A.now + PE.now
        units = []
        for t in range(TT):
            def scores(o, t=t):
                for h in range(4):
                    m = PE.e.matmul(o[:, h, :], nT[:, h, t * P:(t + 1) * P], nT[:, 4 + h, :], start=True, stop=True)
                return m
            units.append(dict(scores=scores, scale=P ** -0.5, add=R[t], dv=P, ready=(e1, e2),
                              value=lambda h, kt, hg=hg: z[:, kt, H_V + (4 * hg + h) * P:H_V + (4 * hg + h + 1) * P],
                              out=plain_out(ostage[:, t, :].rearrange("p (h d) -> p h d", h=4))))
        attention(units)
        e = to_T(lambda c, t: ostage[:, t, c * P:(c + 1) * P], 4, tT[:, 8 + 4 * hg:12 + 4 * hg, :], ready=V.now)
    gemm(tT, 16, 2, evac_xn, (V.now, A.now))
    post_norm(1.0, 2, (V.now, A.now))
    ffn2(2, 3)
    ffn2(3, 4)

    n = norm_T(x[:, :, :], D, nT, s2("pre", 32, 40), V.now)
    gemm(nT, KT, 4, evac_z, n)
    cin = big[:, 0:8 * (T + 3)].rearrange("p (c n) -> p c n", c=8)
    m0 = G.do(G.wait(PE.now, V.now).memset(cin[:, :, 0:3], 0.0))
    e = to_T(lambda c, t: z[:, t, D + c * P:D + (c + 1) * P], 8, None, evac_cin, (V.now, A.now))
    xT, rT, iT = tT[:, 0:8, :], tT[:, 8:16, :], nT[:, :, :]
    v = conv4(8, cin, s2("rw"), s2("rb"), xT, (e, m0, PE.now))
    w = chunk()
    PE.wait(v, free(0, 1, 2, 3, 4, 5, 6, 7))
    for j in range(16):
        m = PE.e.matmul(ps[:, j // 2, j % 2 * T:(j % 2 + 1) * T], w[:, j * P:(j + 1) * P], xT[:, j % 8, :], start=True, stop=True)
    p = PE.do(m, used)
    for j in range(16):
        dst, bias = (rT, s2("ba", j, j + 1)) if j < 8 else (iT, s2("bx", j - 8, j - 7))
        a = A.do(A.wait(p).activation(dst[:, j % 8, :], ps[:, j // 2, j % 2 * T:(j % 2 + 1) * T], ACT.Sigmoid, bias=bias))
        released(a, j // 2)
    lam = wk[:, 10, 0:8]
    V.do(V.chain().tensor_scalar(wk[:, 11, 0:8], s2("lam"), -1.0, None, ALU.mult))
    softplus(lam, wk[:, 11, 0:8], 8, acc[:, 2:6, :])
    V.do(V.chain().tensor_scalar(lam, lam, -8.0, None, ALU.mult))

    def zbuf(t, i):
        return z[:, t, 2048 * (1 + i):2048 * (2 + i)].rearrange("p (c n) -> p c n", c=8)
    aT, th, dn, gT = zbuf(0, 0), zbuf(0, 1), zbuf(1, 0), zbuf(1, 1)
    V.do(V.wait(A.now, V.now).tensor_tensor(rT, rT, bc(lam, T), ALU.mult))
    A.do(A.wait(V.now).activation(aT, rT, ACT.Exp))
    p = A.do(A.e.activation(th, rT, ACT.Tanh))
    V.do(V.wait(p).tensor_scalar(dn, th, -1.0, 1.0, ALU.mult, ALU.add))
    V.do(V.chain().reciprocal(dn, dn))
    V.do(V.chain().scalar_tensor_tensor(th, th, -2.0, dn, ALU.mult, ALU.mult))
    p = A.do(A.wait(V.now).activation(th, th, ACT.Sqrt))
    V.do(V.e.tensor_tensor(iT, iT, xT, ALU.mult))
    V.do(V.wait(p, V.now).tensor_tensor(iT, iT, th, ALU.mult))
    V.wait(V.now)
    for c in range(8):
        V.do(V.e.tensor_tensor_scan(rT[:, c, :], aT[:, c, :], iT[:, c, :], 0.0, ALU.mult, ALU.add))

    def evac_g(p, o, c, k):
        return A.do(A.wait(p).activation(gT[:, c:c + k, :], o, ACT.Gelu_apprx_tanh))
    e = to_T(lambda c, t: z[:, t, c * P:(c + 1) * P], 8, None, evac_g, (V.now, A.now))
    v = V.do(V.wait(e, V.now).tensor_tensor(nT[:, :, :], rT, gT, ALU.mult))
    gemm(nT, KT, 2, evac_xn, v)
    post_norm(1.0, 5, (V.now, A.now))
    ffn2(5, 6)
    for t in range(TT):
        p = load(A, io["out"][:, t, :], x[:, t, :], V.now, G.now)
        A.wait(p)
    core.meet()
    return core.seen


def t5_bucket(dist):
    f = np.float32
    ratio = np.log(np.maximum(dist, 1).astype(f) / f(16)) / f(log(8))
    return np.where(dist < 16, dist, np.minimum(16 + (ratio * f(16)).astype(np.int32), 31))


def constants():
    c = np.zeros((P, CC_W), np.float32)

    def put(name, a):
        c[:, CC[name][0]:CC[name][1]] = a
    p, n = np.arange(P)[:, None], np.arange(BAND)[None, :]
    put("ident", np.eye(P))
    put("ones", 1.0)
    put("upper", n - P >= p)
    put("maskU", np.where(n[:, :P] >= p, 0.0, NEG))
    put("mask", np.where(p + P - n >= 0, 0.0, NEG))
    put("freq", (np.float32(10000.0) ** (-np.arange(32, dtype=np.float32) / np.float32(32)))[None, :])
    put("valid", np.stack([(np.arange(P) >= 31), np.ones(P)], 1))
    hot = np.zeros((33, BLK), np.float32)
    d = 255 - np.arange(BLK)
    hot[t5_bucket(np.maximum(d, 0))[:256], np.arange(256)] = 1.0
    hot[32, 256:] = NEG
    return c, hot


def rows(a):
    return np.ascontiguousarray(a.reshape(TT, P, -1).transpose(1, 0, 2))


def feat(a):
    return a.reshape(-1, P).T


def layout(v):
    chunks = []

    def put(a):
        a = a.transpose(1, 0, 2).reshape(P, -1)
        c = np.zeros((P, CHUNK), np.float32)
        c[:, :a.shape[1]] = a
        chunks.append(c)

    def blocks(w):
        k, n = w.shape
        for b in range(0, n, BLK):
            part = np.zeros((k, BLK), np.float32)
            part[:, :min(BLK, n - b)] = w[:, b:b + BLK]
            for c in range(0, k, 4 * P):
                put(part[c:c + 4 * P].reshape(4, P, BLK))

    def ffn(w_in, w_out):
        gu = np.concatenate([w_in[:, :FF].reshape(D, GU, 256), w_in[:, FF:].reshape(D, GU, 256)], 2)
        blocks(gu.reshape(D, GU * BLK))
        for c in range(FT // 2):
            put(w_out[2 * c * P:(2 * c + 2) * P].reshape(2, P, D))

    smalls = np.zeros((DEPTH, P, S1_W), np.float32)
    for l in range(DEPTH):
        def small(name, a):
            smalls[l, :, S1[name][0]:S1[name][1]] = a
        w = v["w_in"][l]
        at = np.cumsum([0, 1024, 512, 768, 24, 384, 256, 64, 3072])
        glu, q, kv, gn, cq, ckv, kr, gm = (w[:, a:b] for a, b in zip(at, at[1:]))
        q = q.reshape(D, 2, 4, 64).transpose(0, 2, 1, 3).reshape(D, 512)
        gn = gn.reshape(D, 2, 4, 3).transpose(0, 3, 2, 1).reshape(D, 24)
        blocks(np.concatenate([gm, glu, q, kv, cq, ckv, kr, gn], 1))
        for n in "kv":
            w1 = v["cmp_w1_" + n][l].reshape(2, 8, P, 256)
            put(w1[0])
            put(w1[1])
        blocks(v["w_branch_conv"][l])
        blocks(v["w_branch_nsa"][l].reshape(2, 4, 64, D).transpose(1, 0, 2, 3).reshape(512, D))
        uq = v["w_uq"][l].reshape(3, P, 4, 192)
        put(uq[..., :128].reshape(3, P, 512))
        put(uq[..., 128:].reshape(3, P, 256))
        ukv = v["w_ukv"][l].reshape(2, P, 4, 2, 128).transpose(0, 1, 3, 2, 4)
        put(ukv.reshape(2, P, 1024))
        blocks(v["w_branch_mla"][l])
        blocks(v["w_out"][l])
        blocks(v["w_xkv"][l])
        blocks(v["w_xq"][l])
        blocks(v["w_xo"][l])
        ffn(v["w_gate_up"][l], v["w_down"][l])
        for _ in range(2):
            put(np.zeros((1, P, 1), np.float32))
        for name in ("mix", "xattn", "mem", "ffn"):
            small(name, feat(v["norm_" + name][l]))
        small("conv_w", v["conv_w"][l].reshape(CONV_W, 4, P).transpose(2, 1, 0).reshape(P, -1))
        small("conv_b", feat(v["conv_b"][l]))
        small("ln_g", feat(v["conv_ln_g"][l]))
        small("ln_b", feat(v["conv_ln_b"][l]))
        small("pos", np.concatenate([feat(v["cmp_pos_k"][l].reshape(-1)), feat(v["cmp_pos_v"][l].reshape(-1))], 1))
        small("b1", np.concatenate([feat(v["cmp_b1_k"][l]), feat(v["cmp_b1_v"][l])], 1))
        w2k = v["cmp_w2_k"][l].reshape(2, P, 64).transpose(1, 0, 2)
        small("w2k", np.concatenate([w2k, w2k], 2).reshape(P, 256))
        small("w2v", v["cmp_w2_v"][l].reshape(2, P, 64).transpose(1, 0, 2).reshape(P, 128))
        small("mq", feat(v["mla_norm_q"][l]))
        small("mkv", feat(v["mla_norm_kv"][l]))

    smalls2 = np.zeros((P, S2_W), np.float32)

    def small2(name, a):
        smalls2[:, S2[name][0]:S2[name][1]] = a
    wi, wo, ng = v["ffn_w_in_2"], v["ffn_w_out_2"], v["norm_g_2"]
    ffn(wi[0, 0], wo[0, 0])
    w = v["hyb_w_in_2"][0]
    at = np.cumsum([0, 1024, 1536, 16, 1024, 1024, 1024, 8])
    zc, xbc, dt, q, k, vv, f = (w[:, a:b] for a, b in zip(at, at[1:]))
    blocks(np.concatenate([zc, xbc, q, k, vv], 1))
    put(np.concatenate([dt, f], 1).reshape(8, P, 24))
    blocks(v["hyb_w_out_2"][0])
    ffn(wi[0, 1], wo[0, 1])
    ffn(wi[1, 0], wo[1, 0])
    blocks(v["rec_w_in_2"][0])
    put(np.concatenate([v["rec_w_a_2"][0], v["rec_w_x_2"][0]], 0))
    blocks(v["rec_w_out_2"][0])
    ffn(wi[1, 1], wo[1, 1])
    small2("pre", np.concatenate([feat(ng[l, i]) for l in range(2) for i in (0, 2, 4)], 1))
    small2("cw", v["ssm_conv_w_2"][0].reshape(4, 12, P).transpose(2, 1, 0).reshape(P, -1))
    small2("cb", feat(v["ssm_conv_b_2"][0]))
    small2("ng", feat(v["ssm_norm_g_2"][0]))
    small2("rw", v["rec_conv_w_2"][0].reshape(4, 8, P).transpose(2, 1, 0).reshape(P, -1))
    small2("rb", feat(v["rec_conv_b_2"][0]))
    small2("ba", feat(v["rec_b_a_2"][0]))
    small2("bx", feat(v["rec_b_x_2"][0]))
    small2("lam", feat(v["rec_lambda_2"][0]))
    small2("dtb", v["ssm_dt_bias_2"][0][None])
    small2("alog", v["ssm_a_log_2"][0][None])
    small2("dskip", v["ssm_d_2"][0][None])
    small2("fb", v["fox_b_f_2"][0][None])
    gains = np.stack([v["norm_final"]] + [ng[l, i] for l in range(2) for i in (1, 3, 5)])
    assert len(chunks) == 2 * LAYER_CHUNKS + TAIL_CHUNKS, len(chunks)
    const, hot = constants()
    rel = np.ones((33, 8), np.float32)
    rel[:32] = v["rel_bias"].reshape(32, 2, 4).transpose(0, 2, 1).reshape(32, 8)
    return {
        "w": np.stack(chunks), "const": const, "onehot": hot, "rel": rel, "x": rows(v["x"][0]), "mem": rows(v["mem"][0]),
        "positions": np.ascontiguousarray(v["positions"].reshape(TT, P).T), "smalls": smalls, "smalls2": smalls2, "gains": gains,
    }


def kernel(**inputs):
    import concourse.bacc as bacc
    from concourse.bass_utils import run_bass_kernel_spmd

    arrays = {"in_" + k: np.ascontiguousarray(a) for k, a in layout({k: np.asarray(a) for k, a in inputs.items()}).items()}
    learned = {}
    while True:
        nc = bacc.Bacc("TRN2", target_bir_lowering=False, num_devices=1)
        io = {k[3:]: nc.dram_tensor(k, a.shape, mybir.dt.from_np(a.dtype), kind="ExternalInput").ap() for k, a in arrays.items()}
        io["out"] = nc.dram_tensor("out", (P, TT, D), F32, kind="ExternalOutput").ap()
        io["skew"] = nc.dram_tensor("skew", (8, P * BLK), F32, kind="Internal").ap()
        seen = build(nc, io, learned)
        if seen == learned:
            break
        learned = seen
    r = run_bass_kernel_spmd(nc, [arrays], core_ids=[0])
    got = r.results[0]["out"]
    return got.transpose(1, 0, 2).reshape(1, T, D)
```

```python
from contextlib import contextmanager
from math import log, pi, sqrt

import numpy as np

import concourse.bass as bass
from concourse import mybir

F32 = mybir.dt.float32
F32R = mybir.dt.float32r
I32 = mybir.dt.int32
ALU = mybir.AluOpType
ACT = mybir.ActivationFunctionType
AX_X = mybir.AxisListType.X
ET = mybir.EngineType
ds = bass.ds

P = 128
TT = 2
T = P * TT
D = 1024
DEPTH = 2
KT = D // P
RING = 4
HALF = 1024
AHEAD = 4
CHUNK = 2048
BLK = 512
FF = 2816
FT = FF // P
GU = FF // 256
EPS = 1e-6
NEG = -1e30

Z_GM = 0
Z_GLU = 3072
Z_Q = 4096
Z_KV = 4608
Z_CQ, Z_CKV, Z_KR, Z_GN = 5376, 5760, 6016, 6080
Z_COLS = 6104
ZW = 6144
CONV_W, CONV_CT = 31, 4
Q_RANK, KV_RANK = 384, 256
N_CMP = (T - 32) // 16 + 1
BAND = 384
S1 = {}
_o = 0
for _n, _w in (("mix", 8), ("xattn", 8), ("mem", 8), ("ffn", 8), ("conv_w", CONV_W * 4), ("conv_b", 4), ("ln_g", 4),
               ("ln_b", 4), ("pos", 32), ("b1", 4), ("w2k", 256), ("w2v", 128), ("mq", 3), ("mkv", 2)):
    S1[_n] = (_o, _o + _w)
    _o += _w
S1_W = _o
S2 = {}
_o = 0
for _n, _w in (("pre", 48), ("cw", 48), ("cb", 12), ("ng", 8), ("rw", 32), ("rb", 8), ("ba", 8), ("bx", 8), ("lam", 8),
               ("dtb", 16), ("alog", 16), ("dskip", 16), ("fb", 8)):
    S2[_n] = (_o, _o + _w)
    _o += _w
S2_W = _o
CC = {}
_o = 0
for _n, _w in (("ident", 128), ("ones", 128), ("upper", BAND), ("maskU", 128), ("mask", BAND), ("freq", 32), ("valid", 2)):
    CC[_n] = (_o, _o + _w)
    _o += _w
CC_W = _o
N_GAIN = 7

LAYER_CHUNKS = 24 + 4 + 2 + 2 + 3 + 2 + 4 + 4 + 2 + 2 + 33 + 2
TAIL_CHUNKS = 4 * 33 + 22 + 1 + 8 + 8 + 1 + 4
N_CHUNKS = 2 * LAYER_CHUNKS + TAIL_CHUNKS
LAYER_HALVES = 2 * (LAYER_CHUNKS - 24 - 4)
assert LAYER_CHUNKS % RING == 0


class Point:

    def __init__(self, sem, const, steps):
        self.sem, self.const, self.steps = sem, const, steps


class Count:

    def __init__(self, core, name):
        self.name, self.h, self.const, self.steps = name, core.nc.alloc_semaphore(name), 0, {}
        core.counts.append(self)

    def add(self, n=1):
        self.const += n
        return Point(self, self.const, dict(self.steps))


class Engine:
    def __init__(self, core, e, name):
        self.core, self.e, self.name, self.count, self.known = core, e, name, Count(core, "s_" + name), {}

    def wait(self, *points):
        for p in points:
            if isinstance(p, (tuple, list)):
                self.wait(*p)
                continue
            key = (p.sem.name, tuple(sorted(p.steps.items())))
            if self.known.get(key, -1) >= p.const or p.const <= 0 and not p.steps:
                continue
            self.known[key] = p.const
            v = p.const
            for name, step in p.steps.items():
                v = v + self.core.iteration(name) * step
            self.e.wait_ge(p.sem.h, v)
        return self.e

    def do(self, ins, count=None, n=1):
        count = count or self.count
        ins.then_inc(count.h, n)
        p = count.add(n)
        self.core.last[self.name] = (p,)
        return p

    @property
    def now(self):
        return self.core.last.get(self.name, ())

    def chain(self):
        return self.wait(self.now)


class Core:
    def __init__(self, nc, learned):
        self.nc, self.learned, self.counts, self.last, self.vars, self.trips = nc, learned, [], {}, {}, {}
        self.seen = {}
        self.PE, self.V = Engine(self, nc.tensor, "pe"), Engine(self, nc.vector, "dve")
        self.A, self.G = Engine(self, nc.scalar, "act"), Engine(self, nc.gpsimd, "pool")
        self.engines = (self.PE, self.V, self.A, self.G)
        self.n_loops = 0

    def iteration(self, name):
        return self.vars[name] if name in self.vars else self.trips[name] - 1

    @contextmanager
    def loop(self, n, meet=False):
        name = f"l{self.n_loops}"
        self.n_loops += 1
        if meet:
            self.meet()
        base = {c.name: c.const for c in self.counts}
        steps, ends = self.learned.get(name, ({}, {}))
        for c in self.counts:
            c.steps[name] = steps.get(c.name, 0)
        before = dict(self.last)
        if not meet:
            for key, points in ends.items():
                back = tuple(Point(next(c for c in self.counts if c.name == s), k - steps.get(s, 0), st)
                             for s, k, st in points)
                assert all(p.const > 0 for p in back), (name, key)
                self.last[key] = before.get(key, ()) + back
        started = dict(self.last)
        with self.nc.Fori(0, n, engines=(ET.Pool, ET.Activation, ET.PE, ET.DVE)) as i:
            self.vars[name] = i
            yield i
            if meet:
                self.phase(None)
                self.meet()
        self.seen[name] = (
            {c.name: c.const - base.get(c.name, 0) for c in self.counts},
            {k: [(p.sem.name, p.const, p.steps) for p in v if name in p.steps]
             for k, v in self.last.items() if v is not started.get(k)})
        del self.vars[name]
        self.trips[name] = n
        for c in self.counts:
            c.const += (n - 1) * (c.const - base.get(c.name, 0))
            c.steps.pop(name, None)
        for e in self.engines:
            e.known = {k: v for k, v in e.known.items() if name not in dict(k[1])}

    def meet(self):
        ends = [e.now for e in self.engines]
        for e in self.engines:
            e.wait(*ends)
        self.last = {e.name: self.last.get(e.name, ()) for e in self.engines}


def bc(ap, n):
    return ap.unsqueeze(len(ap.shape)).to_broadcast([*ap.shape, n])


def mid(ap, n):
    return ap.unsqueeze(1).to_broadcast([ap.shape[0], n, *ap.shape[1:]])


def build(nc, io, learned):
    core = Core(nc, learned)
    core.phase = lambda name: phase(name)
    PE, V, A, G = core.engines

    def sb(name, shape, dt=F32):
        return nc.alloc_sbuf_tensor(name, shape, dt)

    def twin(name, other, shape):
        if other is None:
            return sb(name, shape, F32R)
        return nc.alloc_sbuf_tensor_at(name, shape, F32R, offset=other)

    def sb_at(name, shape):
        at = (nc.sbuf_base + 31) // 32 * 32
        return sb(name, shape), at

    ps = nc.alloc_psum_tensor("ps", [P, 8, BLK], F32)
    ring, at = sb_at("ring", [P, RING, CHUNK])
    ring_lo = twin("ring_lo", at, [P, RING, CHUNK])
    upper_w = twin("upper_w", None, [P, AHEAD, HALF])
    x = sb("x", [P, TT, D])
    nT, at = sb_at("nT", [P, KT, T])
    nT_lo = twin("nT_lo", at, [P, KT, T])
    nT_hi = twin("nT_hi", None, [P, KT, T])
    big = sb("big", [P, 3200 + D])
    xn, at = sb_at("xn", [P, TT, D])
    xn_hi = twin("xn_hi", at, [P, KT, T])
    z, at = sb_at("z", [P, TT, ZW])
    z_hi = twin("z_hi", at, [P, TT, ZW])
    tT, at = sb_at("tT", [P, FT, T])
    tT_lo = twin("tT_lo", at, [P, FT, T])
    band = big[:, 0:8 * BAND].rearrange("p (h n) -> p h n", h=8)
    S = sb("S", [P, 2, 4, T])
    PTs = sb("PTs", [P, 2, 8, P])
    cbuf = sb("cbuf", [P, 1152])
    acc = sb("acc", [P, 6, T])
    const = sb("const", [P, CC_W])
    sm = sb("sm", [P, S1_W])
    sm2 = sb("sm2", [P, S2_W])
    st = sb("st", [P, 16])
    half = sb("half", [P, T])
    rope = sb("rope", [P, 2, TT, 32])
    ostage = sb("ostage", [P, TT, 512])
    junk = ostage[:, :, :].rearrange("p t n -> p (t n)")
    rs = sb("rs", [P, 2, 3, 4])

    def c_(name):
        a, b = CC[name]
        return const[:, a:b]

    def s1(name):
        a, b = S1[name]
        return sm[:, a:b]

    def s2(name, a=0, b=None):
        o, e = S2[name]
        return sm2[:, o + a:o + b if b is not None else e]

    ident, mask = c_("ident"), c_("mask")

    def load(queue, dst, src, *after):
        queue.wait(*after)
        c = Count(core, f"s_dma{len(core.counts)}")
        queue.e.dma_start(dst, src).then_inc(c.h, 16)
        return c.add(16)

    sm_count, mem_count = Count(core, "s_sm"), Count(core, "s_mem")
    loads_x = Count(core, "s_x")
    nc.sync.dma_start(x[:, :, :], io["x"]).then_inc(loads_x.h, 16)
    l_x = loads_x.add(16)
    landed = [nc.alloc_semaphore(f"landed{s}") for s in range(RING)]
    used = Count(core, "used")
    cut = Count(core, "cut")
    with nc.named_scope("weights"):
        for s in range(RING):
            nc.sync.dma_start(ring[:, s, :], io["w"][s]).then_inc(landed[s], 16)
        whole = N_CHUNKS // RING
        with nc.Fori(0, whole - 1, engines=(ET.SP,)) as i:
            for s in range(RING):
                nc.sync.wait_ge(used.h, i * (2 * RING) + (2 * s + 3))
                nc.sync.dma_start(ring[:, s, :], io["w"][ds(i * RING + (RING + s), 1), :, :].rearrange("a p n -> p (a n)")
                                  ).then_inc(landed[s], 16)
        assert N_CHUNKS % RING == 0

    def landing(n):
        g = (used.const - 1 + n) // 2
        v = 16 * (g // RING + 1)
        for name, step in used.steps.items():
            assert step % (2 * RING) == 0 or not learned
            v = v + core.iteration(name) * (16 * step // (2 * RING))
        return landed[g % RING], v

    def chunk():
        assert used.const % 2 == 1
        sem, v = landing(0)
        PE.e.wait_ge(sem, v)
        return ring[:, (used.const - 1) // 2 % RING, :]

    run = {"left": 0, "ahead": 0}

    def start_run(halves):
        assert run["left"] == 0 and run["ahead"] == 0
        run["left"] = halves
        feed(AHEAD - 1)

    def feed(upto):
        while run["ahead"] < min(upto, run["left"]):
            n = run["ahead"]
            half_ = used.const - 1 + n
            at_ = (half_ // 2 % RING, slice(half_ % 2 * HALF, (half_ % 2 + 1) * HALF))
            src, rest = ring[:, at_[0], at_[1]], ring_lo[:, at_[0], at_[1]]
            up_ = upper_w[:, half_ % AHEAD, :]
            sem, v = landing(n)
            A.e.wait_ge(sem, v)
            if half_ - AHEAD >= 0:
                A.wait(Point(used, used.const + n - AHEAD + 1, dict(used.steps)))
            a = A.do(A.e.copy(up_, src))
            V.do(V.wait(a).tensor_tensor(rest, src, up_.bitcast(F32), ALU.subtract), cut)
            run["ahead"] += 1

    def next_half():
        feed(AHEAD)
        PE.wait(Point(cut, cut.const - run["ahead"] + 1, dict(cut.steps)))
        h = used.const - 1
        run["ahead"] -= 1
        run["left"] -= 1
        return upper_w[:, h % AHEAD, :], ring_lo[:, h // 2 % RING, h % 2 * HALF:(h % 2 + 1) * HALF]

    def split_lhs(src, hi, lo, ready, tiles):
        out = ()
        step = (tiles + 1) // 2
        for c in range(0, tiles, step):
            k = slice(c, min(c + step, tiles))
            a = A.do(A.wait(ready, PE.now).copy(hi[:, k, :], src[:, k, :]))
            out += (V.do(V.wait(a, PE.now, ready).tensor_tensor(lo[:, k, :], src[:, k, :], hi[:, k, :].bitcast(F32), ALU.subtract)),)
        return out

    def three(out, hi, lo, w_hi, w_lo, start, stop):
        PE.e.matmul(out, hi, w_hi, start=start, stop=False)
        PE.e.matmul(out, hi, w_lo, start=False, stop=False)
        return PE.e.matmul(out, lo, w_hi, start=False, stop=stop)

    bank_turn = [0]
    scope = []

    def phase(name):
        if scope:
            scope.pop().__exit__(None, None, None)
        if name:
            scope.append(nc.named_scope(name))
            scope[-1].__enter__()

    def free(*banks):
        return [core.last.get(f"b{b}", ()) for b in banks]

    def released(point, *banks):
        for b in banks:
            core.last[f"b{b}"] = (point,)

    def gemm_block(lhs, kts, pair, ready, beside=None, at=0):
        each = isinstance(ready, list)
        PE.wait(free(2 * pair, 2 * pair + 1), () if each else ready)
        for c in range(kts // 2):
            if isinstance(lhs, tuple):
                w_hi, w_lo = next_half()
            elif c % 2 == 0:
                w = chunk()
            for k in range(2):
                f, first, last = 2 * c + k, c == 0 and k == 0, 2 * c + k == kts - 1
                if each:
                    PE.wait(ready[f])
                for t in range(TT):
                    o, tok = ps[:, 2 * pair + t, :], slice(t * P, (t + 1) * P)
                    if isinstance(lhs, tuple):
                        m = three(o, lhs[0][:, f, tok], lhs[1][:, f, tok], w_hi[:, k * BLK:(k + 1) * BLK],
                                  w_lo[:, k * BLK:(k + 1) * BLK], first, last)
                    else:
                        m = PE.e.matmul(o, lhs[:, f, tok], w[:, (2 * (c % 2) + k) * BLK:(2 * (c % 2) + k + 1) * BLK], start=first, stop=last)
            p = PE.do(m, used)
            if beside:
                beside(at + c)
        return p, ps[:, 2 * pair:2 * pair + 2, :]

    def gemm(lhs, kts, blocks, evac, ready=(), first=0, beside=None):
        def body(at, j):
            p, o = gemm_block(lhs, kts, j, ready, beside, (at - first) * (kts // 2))
            released(evac(p, o, at, j), 2 * j, 2 * j + 1)
        whole = blocks // 2 if kts == KT and isinstance(lhs, tuple) else 0
        while whole and run["left"] - 8 * whole < AHEAD - 1:
            whole -= 1
        if whole > 1:
            assert run["ahead"] == AHEAD - 1
            with core.loop(whole) as i:
                for j in range(2):
                    body(i * 2 + (j + first), j)
            run["left"] -= 8 * (whole - 1)
        else:
            whole = 0
        for b in range(2 * whole, blocks):
            body(first + b, b % 2)

    def block_of(buf, b):
        return buf[:, :, b * BLK:(b + 1) * BLK] if isinstance(b, int) else buf[:, :, ds(b * BLK, BLK)]

    def to_T(src, tiles, dst, evac=None, ready=()):
        out = ()
        for c in range(0, tiles, 2):
            n = min(2, tiles - c)
            b = 6 + bank_turn[0] % 2
            bank_turn[0] += 1
            PE.wait(free(b), ready)
            for i in range(n):
                for t in range(TT):
                    m = PE.e.transpose(ps[:, b, (i * TT + t) * P:(i * TT + t + 1) * P], src(c + i, t), ident)
            p = PE.do(m)
            o = ps[:, b, 0:n * T].rearrange("p (c n) -> p c n", c=n)
            if evac:
                e = evac(p, o, c, n)
            elif b == 6:
                e = V.do(V.wait(p, dst_free).tensor_copy(dst[:, c:c + n, :], o))
            else:
                e = A.do(A.wait(p, dst_free).copy(dst[:, c:c + n, :], o))
            released(e, b)
            out = out + (e,)
        return out[-2:]

    dst_free = ()

    def rstd(srcs, n, at, ready):
        k = len(srcs)
        for i, s in enumerate(srcs):
            p = A.do(A.wait(ready, V.now, PE.now, A.now).activation(junk[:, 0:n], s, ACT.Square, accum_out=st[:, at + i:at + i + 1]))
        p = V.do(V.wait(p, G.now).tensor_scalar(st[:, at:at + k], st[:, at:at + k], 1.0 / n, EPS, ALU.mult, ALU.add))
        return G.do(G.wait(p).tensor_tensor(st[:, at:at + k], st[:, at:at + k], half[:, 0:k], ALU.pow))

    nT_parts = (nT_hi[:, :, :], nT_lo[:, :, :])

    class Parts:

        def __init__(self, at=0):
            self.at = at

        def __getitem__(self, key):
            _, c, tok = key
            if isinstance(c, slice):
                assert c.start // 11 == (c.stop - 1) // 11
                o = FF + c.start % 11 * T
                return z_hi[:, c.start // 11, o:o + (c.stop - c.start) * T].rearrange("p (c n) -> p c n", n=T)
            o = FF + c % 11 * T
            return z_hi[:, c // 11, o + (tok.start or 0):o + (T if tok.stop is None else tok.stop)]

    class Joined:

        def __init__(self, a, b, n):
            self.a, self.b, self.n = a, b, n

        def __getitem__(self, key):
            _, c, tok = key
            return self.a[:, c, tok] if c < self.n else self.b[:, c - self.n, tok]

    def to_parts(src, tiles, hi, lo, ready, gain=None, banks=(4, 5, 6, 7)):
        points = []
        for c in range(0, tiles, 2):
            b = banks[c // 2 % len(banks)]
            n = min(2, tiles - c)
            PE.wait(free(b), ready[c // 4] if isinstance(ready, list) else ready)
            for i in range(n):
                for t in range(TT):
                    m = PE.e.transpose(ps[:, b, (i * TT + t) * P:(i * TT + t + 1) * P], src(c + i, t), ident)
            p = PE.do(m)
            o = [ps[:, b, i * T:(i + 1) * T] for i in range(2)]
            for i in range(n):
                g = None if gain is None else gain[:, c + i:c + i + 1]
                a = A.do(A.wait(p).copy(hi[:, c + i, :], o[i]) if g is None else A.wait(p).mul(hi[:, c + i, :], o[i], g))
            V.wait(a)
            for i in range(n):
                g, h = None if gain is None else gain[:, c + i:c + i + 1], hi[:, c + i, :].bitcast(F32)
                v = V.do(V.e.tensor_tensor(lo[:, c + i, :], o[i], h, ALU.subtract) if g is None
                         else V.e.scalar_tensor_tensor(lo[:, c + i, :], o[i], g, h, ALU.mult, ALU.subtract))
                points.append(v)
            released(v, b)
            yield points

    def norm_parts(src, gain, ready, at=8, hi=nT_hi, lo=nT_lo):
        for points in to_parts(lambda c, t: src[:, t, c * P:(c + 1) * P], KT, hi, lo, ready, gain):
            pass
        ready = [q for r in ready for q in (r if isinstance(r, (tuple, list)) else (r,))] if isinstance(ready, list) else ready
        r = rstd([src[:, t, :] for t in range(TT)], D, at, ready)
        core.last["rstd"] = (r,)
        return points

    def scaled(engine, p, dst, o, at=8, func=ACT.Copy):
        for t in range(TT):
            if engine is A:
                e = A.do(A.wait(p, last_of("rstd")).activation(dst[:, t, :], o[:, t, :], func, scale=st[:, at + t:at + t + 1]))
            else:
                e = V.do(V.wait(p, last_of("rstd")).tensor_scalar(dst[:, t, :], o[:, t, :], st[:, at + t:at + t + 1], None, ALU.mult))
        return e

    def add_x(p, o, b, pair):
        cols = x[:, :, ds(b * BLK, BLK)] if not isinstance(b, int) else x[:, :, b * BLK:(b + 1) * BLK]
        return V.do(V.wait(p, A.now).tensor_tensor(cols, cols, o, ALU.add))

    def ffn_up(ready):
        def evac(p, o, b, pair):
            g = acc[:, 2 * pair:2 * pair + 2, :]
            a = scaled(A, (p, last_of(f"sg{pair}")), g, o[:, :, 0:256], func=ACT.Silu)
            dst = z[:, :, ds(b * 256, 256)] if not isinstance(b, int) else z[:, :, b * 256:(b + 1) * 256]
            for t in range(TT):
                v = V.do(V.wait(a).scalar_tensor_tensor(dst[:, t, :], o[:, t, 256:512], st[:, 8 + t:9 + t], g[:, t, :], ALU.mult, ALU.mult))
            core.last[f"sg{pair}"] = (v,)
            return v
        for j in range(2):
            core.last[f"sg{j}"] = V.now
        gemm(nT_parts, KT, GU, evac, ready)
        return V.now

    def last_of(name):
        return core.last.get(name, ())

    def ffn_down(ready):
        hi = Parts()
        parts = to_parts(lambda c, t: z[:, t, c * P:(c + 1) * P], FT, hi, tT_lo, ready, banks=(4, 5, 6, 7))
        for _ in range(3):
            points = next(parts)
        PE.wait(free(0, 1, 2, 3))
        for c in range(FT):
            if c % 2 and c + 5 < FT:
                next(parts)
            PE.wait(points[c])
            w_hi, w_lo = next_half()
            for h in range(2):
                for t in range(TT):
                    tok, cols = slice(t * P, (t + 1) * P), slice(h * BLK, (h + 1) * BLK)
                    m = three(ps[:, 2 * h + t, :], hi[:, c, tok], tT_lo[:, c, tok], w_hi[:, cols], w_lo[:, cols], c == 0, c == FT - 1)
            p = PE.do(m, used)
        return p

    def attention(units):
        def front(u, i):
            s, b = i % 2, 2 * (i % 2)
            PE.wait(free(b, b + 1), u.get("ready", ()))
            o = ps[:, b:b + 2, :].rearrange("p a (h k) -> p (a h) k", h=2)
            p = PE.do(u["scores"](o))
            Su, nm, sums = S[:, s], rs[:, s, 0, :], rs[:, s, 1, :]
            V.wait(p, last_of(f"S{s}"), last_of(f"rs{s}"))
            if u["add"] is not None:
                v = V.do(V.e.scalar_tensor_tensor(Su, o, u["scale"], u["add"], ALU.mult, ALU.add))
                src, scale = Su, 1.0
                released(v, b, b + 1)
                V.wait(v)
                v = V.do(V.e.tensor_reduce(nm, Su, AX_X, ALU.max, negate=True))
            else:
                v = V.do(V.e.tensor_reduce(nm, o, AX_X, ALU.max, negate=True))
                v = V.do(V.wait(v).tensor_scalar(nm, nm, u["scale"], None, ALU.mult))
                src, scale = o, u["scale"]
            A.wait(v, last_of(f"S{s}"))
            for h in range(4):
                a = A.do(A.e.activation(Su[:, h, :], src[:, h, :], ACT.Exp, bias=nm[:, h:h + 1], scale=scale,
                                        accum_out=sums[:, h:h + 1]))
            if u["add"] is None:
                released(a, b, b + 1)
            core.last[f"P{s}"] = (a,)

        def middle(u, i):
            s = i % 2
            u["inverse"] = V.do(V.wait(last_of(f"P{s}")).reciprocal(rs[:, s, 2, :], rs[:, s, 1, :]))
            PE.wait(last_of(f"P{s}"), free(4, 5))
            for h in range(4):
                for kt in range(TT):
                    m = PE.e.transpose(ps[:, 4 + h // 2, (h % 2 * TT + kt) * P:(h % 2 * TT + kt + 1) * P],
                                       S[:, s, h, kt * P:(kt + 1) * P], ident)
            p = PE.do(m)
            core.last[f"S{s}"] = (p,)
            e0 = V.do(V.wait(p, last_of(f"PT{s}")).tensor_copy(PTs[:, s, 0:4, :], ps[:, 4, :].rearrange("p (a b) -> p a b", a=4)))
            e1 = A.do(A.wait(p, last_of(f"PT{s}")).copy(PTs[:, s, 4:8, :], ps[:, 5, :].rearrange("p (a b) -> p a b", a=4)))
            released(e0, 4)
            released(e1, 5)
            u["PT"] = (e0, e1)

        def back(u, i):
            s, b = i % 2, 6 + i % 2
            PE.wait(u["PT"], free(b))
            dv = u["dv"]
            for h in range(4):
                for kt in range(TT):
                    m = PE.e.matmul(ps[:, b, h * dv:(h + 1) * dv], PTs[:, s, 2 * h + kt, :], u["value"](h, kt),
                                    start=(kt == 0), stop=(kt == TT - 1))
            p = PE.do(m)
            core.last[f"PT{s}"] = (p,)
            e = u["out"](ps[:, b, 0:4 * dv].rearrange("p (h d) -> p h d", h=4), rs[:, s, 2, :], (p, u["inverse"]))
            core.last[f"rs{s}"] = (e,)
            released(e, b)
            return e

        front(units[0], 0)
        front(units[1], 1)
        for i in range(len(units)):
            middle(units[i], i)
            if i + 2 < len(units):
                front(units[i + 2], i + 2)
            e = back(units[i], i)
        return e

    def plain_out(dst):
        def out(o, inv, ready):
            return V.do(V.wait(*ready).tensor_tensor(dst, o, bc(inv, o.shape[2]), ALU.mult))
        return out

    relT = acc[0:33, 0, 0:8]
    hot = cbuf[0:33, 0:BLK]
    l_rel = load(A, relT, io["rel"])
    l_hot = load(A, hot, io["onehot"])
    l_pos = load(A, st[:, 0:TT].bitcast(I32), io["positions"])
    l_const = load(A, const[:, :], io["const"])
    A.e.dma_start(sm[:, :], io["smalls"][0]).then_inc(sm_count.h, 16)
    sm_count.add(16)
    l_sm2 = load(A, sm2[:, :], io["smalls2"])
    halved = G.do(G.e.memset(half[:, :], -0.5))
    PE.wait(l_rel, l_hot)
    p = PE.do(PE.e.matmul(ps[0:8, 6, :], relT, hot, start=True, stop=True), used)
    p = V.do(V.wait(p).tensor_copy(acc[0:8, 2:4, :], ps[0:8, 6, :].rearrange("p (a b) -> p a b", a=2)))
    released(p, 6)
    skew = io["skew"]
    p = load(G, skew.rearrange("h (r j) -> h r j", r=P), mid(acc[0:8, 2:4, :].rearrange("p a b -> p (a b)"), P), p)
    G.wait(p)
    skewed = bass.AP(skew.tensor, skew.offset + P - 1, [[BLK - 1, P], [P * BLK, 8], [1, BAND]])
    l_band = load(G, band[:, :, :], skewed)
    V.wait(l_pos, l_const)
    V.do(V.e.tensor_copy(st[:, 2:4], st[:, 0:TT].bitcast(I32)))
    ang = junk[:, 0:64].rearrange("p (t f) -> p t f", t=TT)
    V.do(V.chain().tensor_tensor(ang, bc(st[:, 2:4], 32), mid(c_("freq"), TT), ALU.mult))
    MAGIC = 1.5 * 2.0 ** 23
    two_pi = 2 * pi
    c1 = float(np.float32(np.floor(two_pi * 2 ** 9) / 2 ** 9))
    c2 = float(np.float32(np.floor((two_pi - c1) * 2 ** 22) / 2 ** 22))
    c3 = float(np.float32(two_pi - c1 - c2))
    for i, shift in ((0, 0.25), (1, 0.0)):
        a, k = junk[:, 64:128].rearrange("p (t f) -> p t f", t=TT), junk[:, 128:192].rearrange("p (t f) -> p t f", t=TT)
        V.do(V.chain().tensor_scalar(k, ang, 1 / two_pi, shift, ALU.mult, ALU.add))
        V.do(V.chain().tensor_scalar(k, k, MAGIC, None, ALU.add))
        V.do(V.chain().tensor_scalar(k, k, -MAGIC, None, ALU.add))
        V.do(V.chain().scalar_tensor_tensor(a, k, -c1, ang, ALU.mult, ALU.add))
        V.do(V.chain().scalar_tensor_tensor(a, k, -c2, a, ALU.mult, ALU.add))
        V.do(V.chain().scalar_tensor_tensor(a, k, -c3, a, ALU.mult, ALU.add))
        V.do(V.chain().tensor_scalar(a, a, 2 * pi * shift, 3.1415925, ALU.add, ALU.min))
        V.do(V.chain().tensor_scalar(a, a, -3.1415925, None, ALU.max))
        p = A.do(A.wait(V.now).activation(rope[:, i], a, ACT.Sin))
        V.wait(p)
    def view(buf, a, b):
        return buf[:, a:b, :].rearrange("p a b -> p (a b)")
    kz = view(tT, 12, 16).rearrange("p (b g n) -> p b g n", b=2, g=2)
    vb = view(tT, 16, 18).rearrange("p (g m d) -> p g m d", g=2, m=4)
    pcmp = view(tT, 18, 20).rearrange("p (t g m c) -> p t g m c", t=TT, g=2, m=4)
    cmpb = view(nT, 0, 4)[:, 0:32 * 2 * N_CMP].rearrange("p (k j g c) -> p k j g c", k=2, j=16, g=2)
    kpz = nT[:, 4:6, :]
    kcz = sb("kcz", [P, 2, 16])
    hidT = sb("hidT", [P, 2, 2, 32])
    cmp_in = tT[:, 8:12, :].rearrange("p a b -> p (a b)").rearrange("p (t k r d) -> p t k r d", t=TT, k=4, r=2)
    gain = big[:, 3200:3200 + D]
    loading = {}

    def load_gain(i):
        loading["gain"] = load(A if i else G, gain, io["gains"][i].partition_broadcast(P), V.now, PE.now)
    load_gain(0)
    for e in core.engines:
        e.wait(l_const, l_x, l_sm2, p)

    with core.loop(DEPTH, meet=True) as layer:
        l_sm = Point(sm_count, sm_count.const, dict(sm_count.steps))
        for e in core.engines:
            e.wait(l_sm)
        phase("w_in")
        start_run(48)
        n = norm_parts(x[:, :, :], s1("mix"), ())

        def evac_gate(p, o, b, pair):
            return scaled(A, p, block_of(z, b), o, func=ACT.Sigmoid)

        def evac_z(p, o, b, pair):
            dst = block_of(z, b)
            return scaled(A if pair == 1 else V, p, dst, o)
        def evac_glu(p, o, b, pair):
            if b == 0:
                return scaled(A, (p, A.now), ostage[:, :, :], o, func=ACT.Sigmoid)
            for t in range(TT):
                v = V.do(V.wait(p, A.now, last_of("rstd")).scalar_tensor_tensor(ostage[:, t, :], o[:, t, :], st[:, 8 + t:9 + t],
                                                                                ostage[:, t, :], ALU.mult, ALU.mult))
            return v
        gemm(nT_parts, KT, 2, evac_glu, n)
        u_rows = V.now
        gemm(nT_parts, KT, 1, evac_gate)
        LEFT = CONV_W - 1
        u = cbuf[:, 0:CONV_CT * (LEFT + T)].rearrange("p (c n) -> p c n", c=CONV_CT)
        m0 = V.do(V.e.memset(u[:, :, 0:LEFT], 0.0))

        def evac_u(p, o, c, k):
            return A.do(A.wait(p).copy(u[:, c:c + k, LEFT:LEFT + T], o))
        e = to_T(lambda c, t: ostage[:, t, c * P:(c + 1) * P], CONV_CT, u, evac_u, u_rows)
        cw = s1("conv_w").rearrange("p (c k) -> p c k", c=CONV_CT)

        def tap(k):
            for c in range(CONV_CT):
                V.wait(last_of(f"tap{c}"))
                if isinstance(k, int) and k == 0:
                    ins = V.e.tensor_scalar(acc[:, c, :], u[:, c, 0:T], cw[:, c, 0:1], s1("conv_b")[:, c:c + 1], ALU.mult, ALU.add)
                else:
                    at_ = slice(k, k + T) if isinstance(k, int) else ds(k, T)
                    w_ = slice(k, k + 1) if isinstance(k, int) else ds(k, 1)
                    ins = V.e.scalar_tensor_tensor(acc[:, c, :], u[:, c, at_], cw[:, c, w_], acc[:, c, :], ALU.mult, ALU.add)
                core.last[f"tap{c}"] = (V.do(ins),)
        gemm(nT_parts, KT, 1, evac_gate, first=1)
        V.wait(e, m0)
        tap(0)
        gemm(nT_parts, KT, 4, evac_gate, first=2, beside=lambda n_: tap(n_ + 1))
        gemm(nT_parts, KT, 4, evac_z, first=8, beside=lambda n_: tap(n_ + 17) if n_ + 17 < CONV_W else None)
        z_done = (V.now, A.now)
        V.wait(z_done, PE.now)
        for buf in (kz, vb, pcmp, kpz, kcz[:, :, :]):
            zeroed = V.do(V.e.memset(buf, 0.0))
        g_n = A.do(A.wait(z_done).activation(z[:, :, Z_GN:Z_GN + 24], z[:, :, Z_GN:Z_GN + 24], ACT.Sigmoid))
        conv_done = V.now
        phase("cmp")
        p = V.do(V.wait(z_done).tensor_copy(cmp_in[:, 0], z[:, 0, Z_KV:Z_KV + 256].rearrange("p (k d) -> p k d", k=4).unsqueeze(2).to_broadcast([P, 4, 2, 64])))
        p = V.do(V.wait(z_done).tensor_copy(cmp_in[:, 1], z[:, 1, Z_KV:Z_KV + 256].rearrange("p (k d) -> p k d", k=4).unsqueeze(2).to_broadcast([P, 4, 2, 64])))
        cmp_ready = p
        qT = tT
        q_ready = to_T(lambda c, t: z[:, t, Z_Q + c * P:Z_Q + (c + 1) * P], 4, qT, ready=z_done)

        def evac_k(p, o, c, k):
            a = A.do(A.wait(p, zeroed).copy(kz[0:64, :, 0, :], o[0:64]))
            return A.do(A.e.copy(kz[64:128, :, 1, :], o[64:128]))
        k_ready = to_T(lambda c, t: z[:, t, Z_KV + (2 + 2 * c) * P:Z_KV + (3 + 2 * c) * P], 2, None, evac_k, z_done)

        ones = c_("ones")
        acc4 = acc[:, 0:4, :]
        sq = cbuf[:, 0:4 * T].rearrange("p (c n) -> p c n", c=4)
        mu, rd = S[:, 0, 2, :], S[:, 0, 3, :]
        PE.wait(conv_done, free(4))
        for c in range(CONV_CT):
            m = PE.e.matmul(ps[:, 4, 0:T], ones, acc[:, c, :], start=(c == 0), stop=(c == CONV_CT - 1))
        p = PE.do(m)
        V.do(V.wait(p, A.now).tensor_scalar(mu, ps[:, 4, 0:T], 1.0 / 512, None, ALU.mult))
        released(V.now[0], 4)
        V.do(V.chain().tensor_tensor(acc4, acc4, mid(mu, 4), ALU.subtract))
        squares = A.do(A.wait(V.now, PE.now).activation(sq, acc4, ACT.Square))

        pos = s1("pos").rearrange("p (k j) -> p k j", k=2)

        def evac_b(p, o, c, k):
            V.wait(p)
            for i in range(k):
                kind, g = (c + i) // 2, (c + i) % 2
                for lo in range(2):
                    half_ = slice(64 * lo, 64 * lo + 64)
                    src = o[half_, i, :]
                    src = bass.AP(src.tensor, src.offset + lo, [list(src.ap[0]), [2, 16], [16, N_CMP]])
                    v = V.do(V.e.tensor_tensor(cmpb[half_, kind, :, g, :], src, bc(pos[half_, kind, :], N_CMP), ALU.add))
            return v
        b_ready = to_T(lambda c, t: cmp_in[:, t, c].rearrange("p r d -> p (r d)"), 4, None, evac_b, cmp_ready)
        PE.wait(squares, free(0))
        for c in range(CONV_CT):
            m = PE.e.matmul(ps[:, 0, 0:T], ones, sq[:, c, :], start=(c == 0), stop=(c == CONV_CT - 1))
        p = PE.do(m)
        V.do(V.wait(p).tensor_scalar(rd, ps[:, 0, 0:T], 1.0 / 512, EPS, ALU.mult, ALU.add))
        released(V.now[0], 0)
        V.do(V.chain().reciprocal(rd, rd))
        p = A.do(A.wait(V.now).activation(rd, rd, ACT.Sqrt))
        V.do(V.wait(p).tensor_tensor(acc4, acc4, mid(rd, 4), ALU.mult))
        A.wait(V.now)
        for c in range(CONV_CT):
            p = A.do(A.e.activation(acc[:, c, :], acc[:, c, :], ACT.Silu, bias=s1("ln_b")[:, c:c + 1], scale=s1("ln_g")[:, c:c + 1]))
        four = (nT_hi[:, 0:4, :], tT_lo[:, 4:8, :])
        a = A.do(A.wait(p).copy(four[0], acc4))
        conv_T = V.do(V.wait(a).tensor_tensor(four[1], acc4, four[0].bitcast(F32), ALU.subtract))
        PE.wait(b_ready, free(6))
        for kind in range(2):
            for cc in range(2):
                w = chunk()
                for j in range(8):
                    if j == 4:
                        PE.do(m, used)
                    m = PE.e.matmul(ps[0:30, 6, kind * 256:(kind + 1) * 256], cmpb[:, kind, 8 * cc + j, :, :].rearrange("p g c -> p (g c)"),
                                    w[:, j * 256:(j + 1) * 256], start=(cc == 0 and j == 0), stop=(cc == 1 and j == 7))
                p = PE.do(m, used)
        hid = S[0:30, 0, 0:2, :]
        v = V.do(V.wait(p, A.now, V.now).tensor_copy(hid, ps[0:30, 6, :].rearrange("p (k n) -> p k n", k=2)))
        released(v, 6)
        PE.wait(v, free(7))
        for kind in range(2):
            for ht in range(2):
                o = 32 * (2 * kind + ht)
                m = PE.e.matmul(ps[:, 7, o:o + 30], hid[:, kind, ht * P:(ht + 1) * P], ident[0:30, 0:30], start=True, stop=True)
        p = PE.do(m)
        for kind in range(2):
            for ht in range(2):
                o = 32 * (2 * kind + ht)
                a = A.do(A.wait(p).activation(hidT[:, kind, ht, 0:30], ps[:, 7, o:o + 30], ACT.Gelu_apprx_tanh,
                                              bias=s1("b1")[:, 2 * kind + ht:2 * kind + ht + 1]))
        released(a, 7)
        w2k, w2v = s1("w2k").rearrange("p (h n) -> p h n", h=2), s1("w2v").rearrange("p (h n) -> p h n", h=2)
        PE.wait(a, free(6, 7))
        for ht in range(2):
            m = PE.e.matmul(ps[:, 6, 0:30], w2k[:, ht, :], hidT[:, 0, ht, 0:30], start=(ht == 0), stop=(ht == 1))
        p = PE.do(m)
        for g in range(2):
            for ht in range(2):
                m = PE.e.matmul(ps[0:15, 7, g * 64:(g + 1) * 64], hidT[:, 1, ht, g * 15:(g + 1) * 15], w2v[:, ht, :],
                                start=(ht == 0), stop=(ht == 1))
        q = PE.do(m)
        V.wait(p, zeroed)
        V.do(V.e.tensor_copy(kcz[0:64, 0, 0:15], ps[0:64, 6, 0:15]))
        released(V.do(V.e.tensor_copy(kcz[64:128, 1, 0:15], ps[64:128, 6, 15:30])), 6)
        A.wait(q)
        for m_ in range(4):
            a = A.do(A.e.copy(vb[32 * m_:32 * m_ + 15, :, m_, :], ps[0:15, 7, 0:128].rearrange("p (g d) -> p g d", g=2)))
        released(a, 7)
        kv_ready = (V.now, A.now)
        phase("cmp_attn")
        PE.wait(kv_ready, q_ready, free(6, 7))
        for t in range(TT):
            for m_ in range(4):
                m = PE.e.matmul(ps[:, 6, (t * 4 + m_) * 32:(t * 4 + m_ + 1) * 32], qT[:, m_, t * P:(t + 1) * P],
                                kcz[:, :, :].rearrange("p g c -> p (g c)"), start=True, stop=True)
        p = PE.do(m)
        merged = xn

        def heads_parts(ready):
            for points in to_parts(lambda c, t: ostage[:, t, c * P:(c + 1) * P], 4, *four, ready):
                pass
            return points

        merged_at = []

        def evac_merge(j):
            def evac(p, o, b, pair):
                g = z[:, :, j * D + b * BLK:j * D + (b + 1) * BLK]
                dst = merged[:, :, b * BLK:(b + 1) * BLK]
                if j == 0:
                    return V.do(V.wait(p).tensor_tensor(dst, o, g, ALU.mult))
                e = V.do(V.wait(p, G.now).tensor_tensor(g, o, g, ALU.mult))
                merged_at.append(V.do(V.chain().tensor_tensor(dst, dst, g, ALU.add)))
                return e
            return evac
        sc = S[:, 0, 0, 0:TT * 8 * 16].rearrange("p (t h c) -> p t h c", t=TT, h=8)
        V.wait(p, PE.now, l_band)
        for t in range(TT):
            first = 31 + P * (1 - t)
            V.do(V.e.scalar_tensor_tensor(sc[:, t, :, 0:N_CMP], ps[:, 6, t * 128:(t + 1) * 128].rearrange("p (h c) -> p h c", h=8)[:, :, 0:N_CMP],
                                          0.125, band[:, :, first:first + 16 * (N_CMP - 1) + 1:16], ALU.mult, ALU.add))
        released(V.now[0], 6)
        scf = sc.rearrange("p t h c -> p (t h) c")[:, :, 0:N_CMP]
        cst = S[:, 1, 0, 0:128]
        cmx, csum, cf = cst[:, 0:16], cst[:, 16:32], cst[:, 32:48]
        V.do(V.chain().tensor_reduce(cmx, scf, AX_X, ALU.max))
        V.do(V.chain().tensor_tensor(scf, scf, bc(cmx, N_CMP), ALU.subtract))
        p = A.do(A.wait(V.now).activation(scf, scf, ACT.Exp))
        V.do(V.wait(p).tensor_reduce(csum, scf, AX_X, ALU.add))
        for t in range(TT):
            pc = V.do(V.wait(p, PE.now).tensor_copy(pcmp[:, t, :, :, 0:N_CMP], sc[:, t, :, 0:N_CMP].rearrange("p (m g) c -> p g m c", m=4)))
        V.do(V.chain().reciprocal(cf, csum))
        cf4 = cf.rearrange("p (t h) -> p t h", t=TT)
        gates = z[:, :, Z_GN:Z_GN + 24].rearrange("p t (j h) -> p t j h", j=3)
        V.do(V.wait(g_n, V.now).tensor_tensor(cf4, cf4, gates[:, :, 0, :], ALU.mult))
        V.do(V.chain().tensor_tensor(cf4, cf4, bc(c_("valid"), 8), ALU.mult))
        start_run(LAYER_HALVES)
        gemm(four, 4, 2, evac_merge(0), conv_T)
        PE.wait(pc, free(7, 6))
        for t in range(TT):
            for g in range(2):
                m = PE.e.transpose(ps[:, 7, (2 * t + g) * P:(2 * t + g + 1) * P], pcmp[:, t, g].rearrange("p m c -> p (m c)"), ident)
        p = PE.do(m)
        pcT = S[:, 1, 2:4, :].rearrange("p a b -> p (a b)")
        a = A.do(A.wait(p).copy(pcT, ps[:, 7, :]))
        released(a, 7)
        PE.wait(a, free(4, 5))
        for t in range(TT):
            for g in range(2):
                m = PE.e.matmul(ps[:, 4 + t, g * 256:(g + 1) * 256], pcT[:, (2 * t + g) * P:(2 * t + g + 1) * P],
                                vb[:, g].rearrange("p m d -> p (m d)"), start=True, stop=True)
        p = PE.do(m)
        ov = ostage[:, :, :].rearrange("p t (m g d) -> p t m g d", m=4, g=2)
        cfg = cf.rearrange("p (t m g) -> p t m g", t=TT, m=4)
        for t in range(TT):
            for g in range(2):
                v = V.do(V.wait(p, V.now).tensor_tensor(ov[:, t, :, g, :], ps[:, 4 + t, g * 256:(g + 1) * 256].rearrange("p (m d) -> p m d", m=4),
                                                 bc(cfg[:, t, :, g], 64), ALU.mult))
            released(v, 4 + t)
        for nm in ("S0", "S1", "rs0", "rs1", "PT0", "PT1"):
            core.last[nm] = V.now + A.now + PE.now
        phase("nsa_attn")
        fac = sb("fac", [P, 2, 4])
        with core.loop(2) as br:
            units = []
            for t in range(TT):
                for mp in range(2):
                    def scores(o, t=t, mp=mp):
                        for i in range(2):
                            m = PE.e.matmul(o[:, 2 * i:2 * i + 2, :].rearrange("p g k -> p (g k)"), qT[:, 2 * mp + i, t * P:(t + 1) * P],
                                            kz[:, ds(br, 1), :, :].rearrange("p a g k -> p (a g k)"), start=True, stop=True)
                        return m

                    def out(o, inv, ready, t=t, mp=mp):
                        f = fac[:, mp, :]
                        V.do(V.wait(*ready, V.now).tensor_tensor(f, inv, z[:, t, ds(Z_GN + 8 + br * 8 + 4 * mp, 4)], ALU.mult))
                        tmp = acc[:, 4 + mp, :].rearrange("p (h d) -> p h d", h=4)
                        e = V.do(V.chain().tensor_tensor(tmp, o, bc(f, 64), ALU.mult))
                        dst = ostage[:, t, 256 * mp:256 * (mp + 1)].rearrange("p (h d) -> p h d", h=4)
                        V.do(V.chain().tensor_tensor(dst, dst, tmp, ALU.add))
                        return e
                    off = P * (1 - t)
                    units.append(dict(
                        scores=scores, scale=0.125, add=band[:, 4 * mp:4 * mp + 4, off:off + T], dv=64, out=out, ready=(k_ready, q_ready),
                        value=lambda h, kt: z[:, kt, ds(Z_KV + 3 * P + br * (2 * P) + h % 2 * 64, 64)]))
            attention(units)
        nsa_done = V.now

        phase("w_nsa")
        gemm(four, 4, 2, evac_merge(1), heads_parts(nsa_done))

        phase("mla")
        gq = sm[:, S1["mq"][0]:S1["mkv"][1]]
        c_hi, c_lo = nT_hi[:, 0:5, :], tT_lo[:, 4:9, :]
        for e in to_parts(lambda c, t: z[:, t, Z_CQ + c * P:Z_CQ + (c + 1) * P], 5, c_hi, c_lo, (), gq):
            pass
        rstd([z[:, t, Z_CQ:Z_CQ + Q_RANK] for t in range(TT)], Q_RANK, 4, ())
        core.last["rstd"] = (rstd([z[:, t, Z_CKV:Z_CKV + KV_RANK] for t in range(TT)], KV_RANK, 6, ()),)
        QN, QP, KN, VN = 3072, 3584, 4096, 4608
        q_done = []
        for pair, (width, at) in enumerate(((512, QN), (256, QP))):
            PE.wait(free(2 * pair, 2 * pair + 1))
            for k in range(3):
                if k * width % HALF == 0:
                    w_hi, w_lo = next_half()
                PE.wait(e[k])
                o_ = k * width % HALF
                for t in range(TT):
                    tok = slice(t * P, (t + 1) * P)
                    m = three(ps[:, 2 * pair + t, 0:width], c_hi[:, k, tok], c_lo[:, k, tok], w_hi[:, o_:o_ + width], w_lo[:, o_:o_ + width],
                              k == 0, k == 2)
                if (k + 1) * width % HALF == 0:
                    PE.do(m, used)
            p = PE.do(m, used)
            v = scaled(V, p, z[:, :, at:at + width], ps[:, 2 * pair:2 * pair + 2, 0:width], 4)
            q_done.append(v)
            released(v, 2 * pair, 2 * pair + 1)
        next_half()
        PE.wait(free(7))
        PE.do(PE.e.matmul(ps[:, 7, 0:1], ident, ident[:, 0:1], start=True, stop=True), used)
        PE.wait(free(4, 5, 0, 1), e[4])
        for k in range(2):
            w_hi, w_lo = next_half()
            for hf, b in ((0, 4), (1, 0)):
                for t in range(TT):
                    tok, cols = slice(t * P, (t + 1) * P), slice(hf * BLK, (hf + 1) * BLK)
                    m = three(ps[:, b + t, :], c_hi[:, 3 + k, tok], c_lo[:, 3 + k, tok], w_hi[:, cols], w_lo[:, cols], k == 0, k == 1)
            p = PE.do(m, used)
        k_done = scaled(A, (p, PE.now), z[:, :, KN:KN + 512], ps[:, 4:6, :], 6)
        released(k_done, 4, 5)
        v_done = scaled(A, p, z[:, :, VN:VN + 512], ps[:, 0:2, :], 6)
        released(v_done, 0, 1)
        V.do(V.wait(V.now).tensor_copy(z[:, :, QP + 256:QP + 320], z[:, :, Z_KR:Z_KR + 64]))
        rot = tT[:, 16:19, :].rearrange("p a b -> p (a b)").rearrange("p (t h r) -> p t h r", t=TT, h=6)
        tmp = tT[:, 19:21, :].rearrange("p a b -> p (a b)")[:, 0:320].rearrange("p (h f) -> p h f", h=10)
        for t in range(TT):
            src = z[:, t, QP:QP + 320].rearrange("p (h r) -> p h r", h=5)
            x1, x2 = src[:, :, 0:32], src[:, :, 32:64]
            cos, sin = mid(rope[:, 0, t, :], 5), mid(rope[:, 1, t, :], 5)
            y1, y2, t1, t2 = rot[:, t, 0:5, 0:32], rot[:, t, 0:5, 32:64], tmp[:, 0:5, :], tmp[:, 5:10, :]
            V.do(V.chain().tensor_tensor(y1, x1, cos, ALU.mult))
            V.do(V.e.tensor_tensor(t1, x2, sin, ALU.mult))
            V.do(V.e.tensor_tensor(y2, x2, cos, ALU.mult))
            V.do(V.e.tensor_tensor(t2, x1, sin, ALU.mult))
            V.do(V.chain().tensor_tensor(y1, y1, t1, ALU.subtract))
            V.do(V.e.tensor_tensor(y2, y2, t2, ALU.add))
            V.do(V.chain().tensor_copy(rot[:, t, 5, :], rot[:, t, 4, :]))
        e1 = to_T(lambda c, t: z[:, t, QN + c * P:QN + (c + 1) * P], 4, tT, ready=q_done[0])
        kT = tT[:, 9:13, :]
        e2 = to_T(lambda c, t: z[:, t, KN + c * P:KN + (c + 1) * P], 4, kT, ready=k_done)
        e3 = to_T(lambda c, t: rot[:, t, 2 * c:2 * c + 2, :].rearrange("p h r -> p (h r)"), 2, tT[:, 13:15, :], ready=V.now)

        def evac_kp(p, o, c, k):
            A.do(A.wait(p).copy(kpz[0:64, 0, :], o[0:64, 0, :]))
            return A.do(A.e.copy(kpz[64:128, 1, :], o[64:128, 0, :]))
        e4 = to_T(lambda c, t: rot[:, t, 4:6, :].rearrange("p h r -> p (h r)"), 1, None, evac_kp, V.now)
        units = []
        for t in range(TT):
            def scores(o, t=t):
                for h in range(4):
                    PE.e.matmul(o[:, h, :], tT[:, h, t * P:(t + 1) * P], kT[:, h, :], start=True, stop=False)
                    m = PE.e.matmul(o[:, h, :], tT[:, 13 + h // 2, t * P:(t + 1) * P], kpz[:, h % 2, :], start=False, stop=True)
                return m
            off = P * (1 - t)
            units.append(dict(scores=scores, scale=192.0 ** -0.5, add=mid(mask[:, off:off + T], 4), dv=P, ready=(e1, e2, e3, e4, v_done),
                              value=lambda h, kt: z[:, kt, VN + h * P:VN + (h + 1) * P],
                              out=plain_out(ostage[:, t, :].rearrange("p (h d) -> p h d", h=4))))
        attention(units)
        gemm(four, 4, 2, evac_merge(2), heads_parts(V.now))
        phase("w_out")
        for e in to_parts(lambda c, t: merged[:, t, c * P:(c + 1) * P], KT, nT_hi, nT_lo, merged_at[-2:]):
            pass
        mrows = z[:, :, 0:D]
        A.wait(V.now, PE.now, G.now)
        A.e.dma_start(mrows, io["mem"]).then_inc(mem_count.h, 16)
        l_mem = mem_count.add(16)
        gemm(nT_parts, KT, 1, add_x, e)
        m_hi = Parts()
        n = norm_parts(mrows, s1("mem"), (l_mem, V.now), at=10, hi=m_hi, lo=tT_lo)
        gemm(nT_parts, KT, 1, add_x, first=1)

        phase("xattn")
        XK, XV, XQ = 0, 512, 1024
        x_done = V.now

        def evac_to(at, factors):
            def evac(p, o, b, pair):
                return scaled(A, (p, V.now), z[:, :, at + b * BLK:at + (b + 1) * BLK], o, factors)
            return evac
        gemm((m_hi, tT_lo), KT, 2, evac_to(0, 10), n)
        n = norm_parts(x[:, :, :], s1("xattn"), x_done)
        gemm(nT_parts, KT, 1, evac_to(XQ, 8), n)
        kT = tT[:, 12:16, :]
        e1 = to_T(lambda c, t: z[:, t, XQ + c * P:XQ + (c + 1) * P], 4, tT, ready=A.now)
        e2 = to_T(lambda c, t: z[:, t, XK + c * P:XK + (c + 1) * P], 4, kT, ready=A.now)
        units = []
        for t in range(TT):
            def scores(o, t=t):
                for h in range(4):
                    m = PE.e.matmul(o[:, h, :], tT[:, h, t * P:(t + 1) * P], kT[:, h, :], start=True, stop=True)
                return m
            units.append(dict(scores=scores, scale=P ** -0.5, add=None, dv=P, ready=(e1, e2),
                              value=lambda h, kt: z[:, kt, XV + h * P:XV + (h + 1) * P],
                              out=plain_out(ostage[:, t, :].rearrange("p (h d) -> p h d", h=4))))
        attention(units)
        halves_at = []
        gemm(four, 4, 2, lambda *a: halves_at.append(add_x(*a)) or halves_at[-1], heads_parts(V.now))
        phase("ffn")
        n = norm_parts(x[:, :, :], s1("ffn"), halves_at)
        A.wait(V.now)
        A.e.dma_start(sm[:, :], io["smalls"][ds(layer + 1, 1), :, :].rearrange("a p n -> p (a n)")).then_inc(sm_count.h, 16)
        sm_count.add(16)
        p = ffn_down(ffn_up(n))
        for hf in range(2):
            released(add_x(p, ps[:, 2 * hf:2 * hf + 2, :], hf, 0), 2 * hf, 2 * hf + 1)
        PE.wait(free(7))
        for _ in range(2):
            for _ in range(2):
                next_half()
                p = PE.do(PE.e.matmul(ps[:, 7, 0:1], ident, ident[:, 0:1], start=True, stop=True), used)

    wk = cbuf[:, 0:384].rearrange("p (a b) -> p a b", a=12)
    def scale_rows(buf, r):
        for t in range(TT):
            v = V.do(V.wait(r, loading["gain"], PE.now).scalar_tensor_tensor(buf[:, t, :], buf[:, t, :], st[:, t:t + 1], gain, ALU.mult, ALU.mult))
        return v

    def post_norm(factor, i, p):
        h = [ps[:, t:4:2, :] for t in range(TT)]
        for t in range(TT):
            a = A.do(A.wait(p, V.now, A.now).activation(ostage[:, :, :], h[t], ACT.Square, accum_out=st[:, t:t + 1]))
            V.do(V.wait(a, p, loading["gain"], PE.now).tensor_tensor(xn[:, t, :].rearrange("p (a n) -> p a n", a=2), h[t],
                                                             gain.rearrange("p (a n) -> p a n", a=2), ALU.mult))
        ready = V.now
        r = V.do(V.e.tensor_scalar(st[:, 0:TT], st[:, 0:TT], factor ** -2 / D, factor ** -2 * EPS, ALU.mult, ALU.add))
        r = G.do(G.wait(r).tensor_tensor(st[:, 0:TT], st[:, 0:TT], half[:, 0:TT], ALU.pow))
        if i + 1 < N_GAIN:
            load_gain(i + 1)
        out = []
        for hf in range(2):
            cols = slice(hf * BLK, (hf + 1) * BLK)
            for t in range(TT):
                v = V.do(V.wait(r, ready).scalar_tensor_tensor(x[:, t, cols], xn[:, t, cols], st[:, t:t + 1], x[:, t, cols], ALU.mult, ALU.add))
            out.append(v)
        released(out[0], 0, 1, 2, 3)
        return out

    def two_blocks(lhs, kts, ready):
        ends = []
        gemm(lhs, kts, 2, lambda p, o, b, pair: ends.append(p) or p, ready)
        return ends[1]

    def ffn2(pre, post, ready):
        n = norm_parts(x[:, :, :], s2("pre", 8 * pre, 8 * pre + 8), ready)
        return post_norm(0.5, post, ffn_down(ffn_up(n)))

    def softplus(out, src, k, tmp):
        m, e, zz, z2 = (tmp[:, i, 0:k] for i in range(4))
        V.do(V.chain().tensor_scalar(m, src, 0.0, None, ALU.max))
        V.do(V.chain().scalar_tensor_tensor(e, src, -1.0, src, ALU.mult, ALU.max))
        a = A.do(A.wait(V.now).activation(e, e, ACT.Exp, scale=-1.0))
        V.do(V.wait(a).tensor_scalar(zz, e, 2.0, None, ALU.add))
        V.do(V.chain().reciprocal(zz, zz))
        V.do(V.chain().tensor_tensor(zz, zz, e, ALU.mult))
        V.do(V.chain().tensor_tensor(z2, zz, zz, ALU.mult))
        V.do(V.chain().tensor_scalar(e, z2, 1.0 / 15, None, ALU.mult))
        for c in (13, 11, 9, 7, 5, 3):
            V.do(V.chain().scalar_tensor_tensor(e, e, 1.0 / c, z2, ALU.add, ALU.mult))
        V.do(V.chain().scalar_tensor_tensor(e, e, 1.0, zz, ALU.add, ALU.mult))
        return V.do(V.chain().scalar_tensor_tensor(out, e, 2.0, m, ALU.mult, ALU.add))

    def conv_tile(c, left, w, b, dst):
        src, out = left[:, ds(c, 1), :], dst[:, ds(c, 1), :]
        V.do(V.chain().tensor_scalar(out, src[:, :, 0:T], w[:, ds(c * 4, 1)], b[:, ds(c, 1)], ALU.mult, ALU.add))
        for k in range(1, 4):
            V.do(V.chain().scalar_tensor_tensor(out, src[:, :, k:k + T], w[:, ds(c * 4 + k, 1)], out, ALU.mult, ALU.add))

    phase("ffn_a")
    start_run(3 * 66 + 46 + 16 + 16)
    r = rstd([x[:, t, :] for t in range(TT)], D, 0, V.now)
    scale_rows(x, r)
    load_gain(1)
    x_ready = ffn2(0, 1, V.now)

    phase("hyb_in")
    cin = big[:, 0:12 * (T + 3)].rearrange("p (c n) -> p c n", c=12)
    m0 = G.do(G.wait(PE.now, V.now).memset(cin[:, :, 0:3], 0.0))
    n = norm_parts(x[:, :, :], s2("pre", 8, 16), x_ready)
    H_Z, H_X, H_Q, H_K, H_V = 0, 1024, 2560, 3584, 4608

    def evac_hyb(p, o, b, pair):
        return scaled(A, p, block_of(z, b), o)
    gemm(nT_parts, KT, 3, evac_hyb, n, first=2)
    xbc_done = (V.now, A.now)
    PE.wait(free(4, 5))
    w_hi, w_lo = next_half()
    for t in range(TT):
        for k in range(KT):
            tok, cols = slice(t * P, (t + 1) * P), slice(k * 24, (k + 1) * 24)
            m = three(ps[:, 4 + t, 0:24], nT_hi[:, k, tok], nT_lo[:, k, tok], w_hi[:, cols], w_lo[:, cols], k == 0, k == KT - 1)
    p = PE.do(m, used)
    next_half()
    PE.wait(free(7))
    PE.do(PE.e.matmul(ps[:, 7, 0:1], ident, ident[:, 0:1], start=True, stop=True), used)

    def evac_cin(p, o, c, k):
        return A.do(A.wait(p, m0).copy(cin[:, c:c + k, 3:3 + T], o))
    e = to_T(lambda c, t: z[:, t, H_X + c * P:H_X + (c + 1) * P], 12, None, evac_cin, xbc_done)
    dtb, fbb = mid(s2("dtb"), TT), mid(s2("fb"), TT)
    dt, dA, lam = wk[:, 2:4, 0:16], wk[:, 4:6, 0:16], wk[:, 10, 0:8]
    raw, sp = (b[:, 0:56] for b in (cbuf[:, 0:64], acc[:, 0, :]))
    raw2, sp2 = (b[:, 0:48].rearrange("p (t n) -> p t n", t=TT) for b in (raw, sp))
    for t in range(TT):
        r_ = st[:, 8 + t:9 + t]
        V.do(V.wait(p, last_of("rstd")).scalar_tensor_tensor(raw2[:, t, 0:16], ps[:, 4 + t, 0:16], r_, dtb[:, t, :], ALU.mult, ALU.add))
        V.do(V.e.scalar_tensor_tensor(raw2[:, t, 16:24], ps[:, 4 + t, 16:24], r_, fbb[:, t, :], ALU.mult, ALU.add))
    released(V.now[0], 4, 5)
    V.do(V.chain().tensor_scalar(raw2[:, :, 16:24], raw2[:, :, 16:24], -1.0, None, ALU.mult))
    V.do(V.e.tensor_scalar(raw[:, 48:56], s2("lam"), -1.0, None, ALU.mult))
    softplus(sp, raw, 56, acc[:, 2:6, :])
    lam_ready = V.do(V.chain().tensor_scalar(lam, sp[:, 48:56], -8.0, None, ALU.mult))
    a_neg = wk[:, 6, 0:16]
    p = A.do(A.wait(V.now).activation(a_neg, s2("alog"), ACT.Exp))
    V.do(V.wait(p, V.now).tensor_scalar(a_neg, a_neg, -1.0, None, ALU.mult))
    V.do(V.chain().tensor_copy(dt, sp2[:, :, 0:16]))
    V.do(V.chain().tensor_tensor(dA, dt, mid(a_neg, TT), ALU.mult))
    lf = wk[:, 7:9, 0:8]
    V.do(V.e.tensor_scalar(lf, sp2[:, :, 16:24], -1.0, None, ALU.mult))
    sums_ready = V.now
    xbcT = tT[:, 0:12, :]
    V.wait(e, m0, PE.now)

    with core.loop(2) as i:
        for j in range(2):
            p, o = gemm_block(nT_parts, KT, j, (), lambda n_: conv_tile(i * 6 + n_, cin, s2("cw"), s2("cb"), xbcT) if n_ < 6 else None, 4 * j)
            released(evac_hyb(p, o, i * 5 + j, j), 2 * j, 2 * j + 1)
    run["left"] -= 8
    a = A.do(A.wait(V.now).activation(xbcT, xbcT, ACT.Silu))
    up = c_("upper")
    tri = up[:, P:2 * P]
    PE.wait(sums_ready, free(6))
    for t in range(TT):
        PE.e.matmul(ps[:, 6, 16 * t:16 * t + 16], tri, dA[:, t, :], start=True, stop=True)
    PE.e.matmul(ps[:, 6, 32:40], tri, lf[:, 0, :], start=True, stop=True)
    PE.e.matmul(ps[:, 6, 40:48], c_("ones"), lf[:, 0, :], start=True, stop=False)
    p = PE.do(PE.e.matmul(ps[:, 6, 40:48], tri, lf[:, 1, :], start=False, stop=True))
    cs = cbuf[:, 384:432]
    V.do(V.wait(p).tensor_copy(cs, ps[:, 6, 0:48]))
    released(V.now[0], 6)
    acs, cumq = cs[:, 0:32].rearrange("p (t h) -> p t h", t=TT), cs[:, 32:48].rearrange("p (t h) -> p t h", t=TT)
    eacs = wk[:, 9, 0:16]
    A.do(A.wait(V.now).activation(eacs, acs[:, 1, :], ACT.Exp))

    gemm(nT_parts, KT, 2, evac_hyb, first=7)
    for t in range(TT):
        for q, (first, n_) in enumerate(((0, 4), (4, 4), (8, 2))):
            b = 6 + bank_turn[0] % 2
            bank_turn[0] += 1
            PE.wait(free(b), a)
            for i in range(n_):
                m = PE.e.transpose(ps[:, b, i * P:(i + 1) * P], tT[:, first + i, t * P:(t + 1) * P], ident)
            p = PE.do(m)
            dst = z[:, t, H_X + first * P:H_X + (first + n_) * P]
            if q % 2:
                released(A.do(A.wait(p).copy(dst, ps[:, b, 0:n_ * P])), b)
            else:
                released(V.do(V.wait(p).tensor_copy(dst, ps[:, b, 0:n_ * P])), b)
    gemm(nT_parts, KT, 2, evac_hyb, first=9)
    BT, CT = tT[:, 8:10, :], tT[:, 10:12, :]
    tok_ready = (V.now, A.now)
    phase("ssd")
    Sf = S[:, :, :, :].rearrange("p a b c -> p (a b c)").rearrange("p (h l) -> p h l", h=16)
    LT = PTs[:, :, :, :].rearrange("p a b c -> p (a b) c")
    S0 = acc[:, 0:4, :].rearrange("p a b -> p (a b)")
    X = xn
    for t in range(TT):
        xt = z[:, t, H_X:H_X + D]
        x3 = xt.rearrange("p (h d) -> p h d", h=16)
        V.wait(tok_ready, PE.now)
        V.do(V.chain().tensor_tensor(Sf, bc(dA[:, t, :], P), mid(tri, 16), ALU.mult))
        V.do(V.e.tensor_tensor(X[:, t, :].rearrange("p (h d) -> p h d", h=16), x3, bc(dt[:, t, :], 64), ALU.mult))
        PE.wait(V.now, free(0, 1, 2, 3))
        for b in range(4):
            m = PE.e.matmul(ps[:, b, :], c_("ones"), Sf[:, 4 * b:4 * b + 4, :].rearrange("p h l -> p (h l)"), start=True, stop=True)
        p = PE.do(m)
        PE.wait(free(4))
        for g in range(2):
            m = PE.e.matmul(ps[:, 4, g * P:(g + 1) * P], BT[:, g, t * P:(t + 1) * P], CT[:, g, t * P:(t + 1) * P], start=True, stop=True)
        pcb = PE.do(m)
        V.do(V.wait(p).tensor_tensor(LT, ps[:, 0:4, :].rearrange("p a (b l) -> p (a b) l", b=4), bc(acs[:, t, :], P), ALU.subtract))
        released(V.now[0], 0, 1, 2, 3)
        V.do(V.chain().tensor_tensor(LT, LT, mid(c_("maskU"), 16), ALU.add))
        a = A.do(A.wait(V.now).activation(LT, LT, ACT.Exp))
        V.wait(a)
        if t == 0:
            Xd = nT[:, 0:4, :].rearrange("p a b -> p (a b)")
            V.do(V.wait(PE.now).tensor_tensor(Xd.rearrange("p (h d) -> p h d", h=16), X[:, 0, :].rearrange("p (h d) -> p h d", h=16),
                                              LT[:, :, P - 1:P].to_broadcast([P, 16, 64]), ALU.mult))
            xd_ready = V.now
        for g in range(2):
            V.do(V.wait(pcb, V.now).tensor_tensor(LT[:, 8 * g:8 * g + 8, :], LT[:, 8 * g:8 * g + 8, :], mid(ps[:, 4, g * P:(g + 1) * P], 8), ALU.mult))
        released(V.now[0], 4)
        PE.wait(V.now, free(5, 6))
        for h in range(16):
            m = PE.e.matmul(ps[:, 5 + h // 8, h % 8 * 64:(h % 8 + 1) * 64], LT[:, h, :], X[:, t, h * 64:(h + 1) * 64], start=True, stop=True)
        py = PE.do(m)
        V.do(V.wait(V.now).tensor_tensor(x3, x3, bc(s2("dskip"), 64), ALU.mult))
        V.do(V.wait(py, V.now).tensor_tensor(xt, xt, ps[:, 5:7, :].rearrange("p a b -> p (a b)"), ALU.add))
        released(V.now[0], 5, 6)
        if t == 0:
            PE.wait(xd_ready, free(0, 1))
            for g in range(2):
                m = PE.e.matmul(ps[:, g, :], z[:, 0, H_X + D + g * P:H_X + D + (g + 1) * P], Xd[:, g * 512:(g + 1) * 512], start=True, stop=True)
            p = PE.do(m)
            s0_ready = A.do(A.wait(p, V.now).copy(S0, ps[:, 0:2, :].rearrange("p a b -> p (a b)")))
            released(s0_ready, 0, 1)
        else:
            PE.wait(s0_ready, free(0, 1))
            for g in range(2):
                m = PE.e.matmul(ps[:, g, :], CT[:, g, P:2 * P], S0[:, g * 512:(g + 1) * 512], start=True, stop=True)
            p = PE.do(m)
            yo = nT[:, 4:8, :].rearrange("p a b -> p (a b)")
            V.do(V.wait(p, A.now).tensor_tensor(yo.rearrange("p (h d) -> p h d", h=16), ps[:, 0:2, :].rearrange("p a (h d) -> p (a h) d", h=8), bc(eacs, 64), ALU.mult))
            released(V.now[0], 0, 1)
            V.do(V.chain().tensor_tensor(xt, xt, yo, ALU.add))
        a = A.do(A.wait(V.now).activation(z[:, t, 0:D], z[:, t, 0:D], ACT.Silu))
        V.do(V.wait(a).tensor_tensor(z[:, t, 0:D], z[:, t, 0:D], xt, ALU.mult))
    groups = [z[:, t, g * 512:(g + 1) * 512] for t in range(TT) for g in range(2)]
    r = rstd(groups, 512, 0, V.now)
    for i, s in enumerate(groups):
        V.do(V.wait(r).tensor_scalar(s, s, st[:, i:i + 1], None, ALU.mult))

    out_ready = [None] * 16
    for points in to_parts(lambda c, t: z[:, t, c * P:(c + 1) * P], 8, nT_hi, tT_lo, (V.now, PE.now), s2("ng")):
        out_ready[0:len(points)] = points

    phase("fox")
    for hg in range(2):
        V.wait(PE.now, A.now)
        for i in range(TT):
            V.do(V.chain().tensor_tensor(S[:, i], bc(lf[:, i, 4 * hg:4 * hg + 4], T), mid(up[:, P * (1 - i):P * (1 - i) + T], 4), ALU.mult))
        PE.wait(V.now, free(0, 1))
        for b in range(2):
            for i in range(TT):
                m = PE.e.matmul(ps[:, b, :], c_("ones"), S[:, i, 2 * b:2 * b + 2, :].rearrange("p h k -> p (h k)"), start=(i == 0), stop=(i == 1))
        p = PE.do(m)
        R = [z[:, t, H_X:H_X + D].rearrange("p (h k) -> p h k", h=4) for t in range(TT)]
        o = ps[:, 0:2, :].rearrange("p a (h k) -> p (a h) k", h=2)
        for t in range(TT):
            off = P * (1 - t)
            V.do(V.wait(p, V.now).scalar_tensor_tensor(R[t], o, -1.0, mid(mask[:, off:off + T], 4), ALU.mult, ALU.add))
            released(V.now[0], 0, 1)
            V.do(V.chain().tensor_tensor(R[t], R[t], bc(cumq[:, t, 4 * hg:4 * hg + 4], T), ALU.add))

        e1 = to_T(lambda c, t: z[:, t, H_Q + (4 * hg + c) * P:H_Q + (4 * hg + c + 1) * P], 4, nT[:, 0:4, :], ready=(V.now, A.now))
        e2 = to_T(lambda c, t: z[:, t, H_K + (4 * hg + c) * P:H_K + (4 * hg + c + 1) * P], 4, nT[:, 4:8, :], ready=(V.now, A.now))
        for nm in ("S0", "S1", "rs0", "rs1", "PT0", "PT1"):
            core.last[nm] = V.now + A.now + PE.now
        units = []
        for t in range(TT):
            def scores(o, t=t):
                for h in range(4):
                    m = PE.e.matmul(o[:, h, :], nT[:, h, t * P:(t + 1) * P], nT[:, 4 + h, :], start=True, stop=True)
                return m
            units.append(dict(scores=scores, scale=P ** -0.5, add=R[t], dv=P, ready=(e1, e2),
                              value=lambda h, kt, hg=hg: z[:, kt, H_V + (4 * hg + h) * P:H_V + (4 * hg + h + 1) * P],
                              out=plain_out(ostage[:, t, :].rearrange("p (h d) -> p h d", h=4))))
        attention(units)
        for points in to_parts(lambda c, t: ostage[:, t, c * P:(c + 1) * P], 4, xn_hi[:, 4 * hg:4 * hg + 4, :],
                               tT_lo[:, 8 + 4 * hg:12 + 4 * hg, :], V.now):
            out_ready[8 + 4 * hg:8 + 4 * hg + len(points)] = points
    phase("hyb_out")
    x_ready = post_norm(1.0, 2, two_blocks((Joined(nT_hi, xn_hi, 8), tT_lo), 16, out_ready))
    phase("ffn_bc")
    x_ready = ffn2(2, 3, x_ready)
    x_ready = ffn2(3, 4, x_ready)

    phase("rec")
    cin = big[:, 0:8 * (T + 3)].rearrange("p (c n) -> p c n", c=8)
    m0 = G.do(G.wait(PE.now, V.now).memset(cin[:, :, 0:3], 0.0))
    n = norm_parts(x[:, :, :], s2("pre", 32, 40), x_ready)
    gemm(nT_parts, KT, 2, evac_hyb, n, first=2)
    e = to_T(lambda c, t: z[:, t, D + c * P:D + (c + 1) * P], 8, None, evac_cin, (V.now, A.now))
    xT, rT = tT[:, 0:8, :], tT[:, 8:16, :]
    V.wait(e, m0)

    def conv_rec(n_):
        for k in range(4):
            src, w_ = cin[:, n_, k:k + T], s2("rw")[:, 4 * n_ + k:4 * n_ + k + 1]
            if k == 0:
                V.do(V.e.tensor_scalar(xT[:, n_, :], src, w_, s2("rb")[:, n_:n_ + 1], ALU.mult, ALU.add))
            else:
                V.do(V.chain().scalar_tensor_tensor(xT[:, n_, :], src, w_, xT[:, n_, :], ALU.mult, ALU.add))
    gemm(nT_parts, KT, 2, evac_hyb, beside=conv_rec)
    gate_ready = A.now

    def zbuf(t, i):
        return z[:, t, 2048 * (1 + i):2048 * (2 + i)].rearrange("p (c n) -> p c n", c=8)
    aT, th, iT, gT = zbuf(0, 0), zbuf(0, 1), zbuf(1, 0), zbuf(1, 1)
    w = chunk()
    PE.wait(V.now, free(0, 1, 2, 3, 4, 5, 6, 7))
    for j in range(16):
        if j == 8:
            PE.do(m, used)
        m = PE.e.matmul(ps[:, j // 2, j % 2 * T:(j % 2 + 1) * T], w[:, j * P:(j + 1) * P], xT[:, j % 8, :], start=True, stop=True)
    p = PE.do(m, used)
    for j in range(16):
        dst, bias = (rT, s2("ba", j, j + 1)) if j < 8 else (iT, s2("bx", j - 8, j - 7))
        a = A.do(A.wait(p, gate_ready).activation(dst[:, j % 8, :], ps[:, j // 2, j % 2 * T:(j % 2 + 1) * T], ACT.Sigmoid, bias=bias))
        released(a, j // 2)
    for func, dst in ((ACT.Exp, aT), (ACT.Tanh, th)):
        for c in range(8):
            p = A.do(A.wait(A.now, lam_ready).activation(dst[:, c, :], rT[:, c, :], func, scale=lam[:, c:c + 1]))
    V.do(V.wait(a).tensor_tensor(iT, iT, xT, ALU.mult))
    scans = []
    for c in range(0, 8, 4):
        k = slice(c, c + 4)
        V.do(V.wait(p).tensor_tensor(rT[:, k, :], aT[:, k, :], aT[:, k, :], ALU.mult))
        V.do(V.chain().scalar_tensor_tensor(th[:, k, :], rT[:, k, :], 1.0, th[:, k, :], ALU.add, ALU.mult))
        A.do(A.wait(V.now).activation(th[:, k, :], th[:, k, :], ACT.Sqrt, scale=-1.0))
        scans.append(A.now)
    for c in range(0, 8, 4):
        k = slice(c, c + 4)
        V.do(V.wait(scans[c // 4], V.now).tensor_tensor(iT[:, k, :], iT[:, k, :], th[:, k, :], ALU.mult))
        V.wait(V.now)
        for i in range(c, c + 4):
            V.do(V.e.tensor_tensor_scan(rT[:, i, :], aT[:, i, :], iT[:, i, :], 0.0, ALU.mult, ALU.add))

    def evac_g(p, o, c, k):
        return A.do(A.wait(p).activation(gT[:, c:c + k, :], o, ACT.Gelu_apprx_tanh))
    e = to_T(lambda c, t: z[:, t, c * P:(c + 1) * P], 8, None, evac_g, gate_ready)
    v = V.do(V.wait(e, V.now, PE.now).tensor_tensor(nT[:, :, :], rT, gT, ALU.mult))
    start_run(8 + 66)
    v = split_lhs(nT[:, :, :], nT_hi[:, :, :], nT_lo[:, :, :], v, KT)
    x_ready = post_norm(1.0, 5, two_blocks(nT_parts, KT, v))
    phase("ffn_d")
    ffn2(5, 6, x_ready)
    phase(None)
    for t in range(TT):
        p = load(A, io["out"][:, t, :], x[:, t, :], V.now, G.now)
        A.wait(p)
    core.meet()
    return core.seen


def t5_bucket(dist):
    f = np.float32
    ratio = np.log(np.maximum(dist, 1).astype(f) / f(16)) / f(log(8))
    return np.where(dist < 16, dist, np.minimum(16 + (ratio * f(16)).astype(np.int32), 31))


def constants():
    c = np.zeros((P, CC_W), np.float32)

    def put(name, a):
        c[:, CC[name][0]:CC[name][1]] = a
    p, n = np.arange(P)[:, None], np.arange(BAND)[None, :]
    put("ident", np.eye(P))
    put("ones", 1.0)
    put("upper", n - P >= p)
    put("maskU", np.where(n[:, :P] >= p, 0.0, NEG))
    put("mask", np.where(p + P - n >= 0, 0.0, NEG))
    put("freq", (np.float32(10000.0) ** (-np.arange(32, dtype=np.float32) / np.float32(32)))[None, :])
    put("valid", np.stack([(np.arange(P) >= 31), np.ones(P)], 1))
    hot = np.zeros((33, BLK), np.float32)
    d = 255 - np.arange(BLK)
    hot[t5_bucket(np.maximum(d, 0))[:256], np.arange(256)] = 1.0
    hot[32, 256:] = NEG
    return c, hot


def rows(a):
    return np.ascontiguousarray(a.reshape(TT, P, -1).transpose(1, 0, 2))


def feat(a):
    return a.reshape(-1, P).T


def layout(v):
    chunks = []

    def put(a):
        a = a.transpose(1, 0, 2).reshape(P, -1)
        c = np.zeros((P, CHUNK), np.float32)
        c[:, :a.shape[1]] = a
        chunks.append(c)

    def blocks(w):
        k, n = w.shape
        for b in range(0, n, BLK):
            part = np.zeros((k, BLK), np.float32)
            part[:, :min(BLK, n - b)] = w[:, b:b + BLK]
            for c in range(0, k, 4 * P):
                put(part[c:c + 4 * P].reshape(4, P, BLK))

    def ffn(w_in, w_out):
        gu = np.concatenate([w_in[:, :FF].reshape(D, GU, 256), w_in[:, FF:].reshape(D, GU, 256)], 2)
        blocks(gu.reshape(D, GU * BLK))
        for c in range(FT // 2):
            put(w_out[2 * c * P:(2 * c + 2) * P].reshape(2, P, D))

    smalls = np.zeros((DEPTH + 1, P, S1_W), np.float32)
    for l in range(DEPTH):
        def small(name, a):
            smalls[l, :, S1[name][0]:S1[name][1]] = a
        w = v["w_in"][l]
        at = np.cumsum([0, 1024, 512, 768, 24, 384, 256, 64, 3072])
        glu, q, kv, gn, cq, ckv, kr, gm = (w[:, a:b] for a, b in zip(at, at[1:]))
        q = q.reshape(D, 2, 4, 64).transpose(0, 2, 1, 3).reshape(D, 512)
        gn = gn.reshape(D, 2, 4, 3).transpose(0, 3, 2, 1).reshape(D, 24)
        blocks(np.concatenate([glu[:, 512:], glu[:, :512], gm, q, kv, cq, ckv, kr, gn], 1))
        for n in "kv":
            w1 = v["cmp_w1_" + n][l].reshape(2, 8, P, 256)
            put(w1[0])
            put(w1[1])
        blocks(v["w_branch_conv"][l])
        blocks(v["w_branch_nsa"][l].reshape(2, 4, 64, D).transpose(1, 0, 2, 3).reshape(512, D))
        uq = v["w_uq"][l].reshape(3, P, 4, 192)
        put(uq[..., :128].reshape(3, P, 512))
        put(uq[..., 128:].reshape(3, P, 256))
        ukv = v["w_ukv"][l].reshape(2, P, 4, 2, 128).transpose(0, 1, 3, 2, 4)
        put(ukv.reshape(2, P, 1024))
        blocks(v["w_branch_mla"][l])
        blocks(v["w_out"][l])
        blocks(v["w_xkv"][l])
        blocks(v["w_xq"][l])
        blocks(v["w_xo"][l])
        ffn(v["w_gate_up"][l], v["w_down"][l])
        for _ in range(2):
            put(np.zeros((1, P, 1), np.float32))
        for name in ("mix", "xattn", "mem", "ffn"):
            small(name, feat(v["norm_" + name][l]))
        small("conv_w", v["conv_w"][l].reshape(CONV_W, 4, P).transpose(2, 1, 0).reshape(P, -1))
        small("conv_b", feat(v["conv_b"][l]))
        small("ln_g", feat(v["conv_ln_g"][l]))
        small("ln_b", feat(v["conv_ln_b"][l]))
        small("pos", np.concatenate([feat(v["cmp_pos_k"][l].reshape(-1)), feat(v["cmp_pos_v"][l].reshape(-1))], 1))
        small("b1", np.concatenate([feat(v["cmp_b1_k"][l]), feat(v["cmp_b1_v"][l])], 1))
        w2k = v["cmp_w2_k"][l].reshape(2, P, 64).transpose(1, 0, 2)
        small("w2k", np.concatenate([w2k, w2k], 2).reshape(P, 256))
        small("w2v", v["cmp_w2_v"][l].reshape(2, P, 64).transpose(1, 0, 2).reshape(P, 128))
        small("mq", feat(v["mla_norm_q"][l]))
        small("mkv", feat(v["mla_norm_kv"][l]))

    smalls2 = np.zeros((P, S2_W), np.float32)

    def small2(name, a):
        smalls2[:, S2[name][0]:S2[name][1]] = a
    wi, wo, ng = v["ffn_w_in_2"], v["ffn_w_out_2"], v["norm_g_2"]
    ffn(wi[0, 0], wo[0, 0])
    w = v["hyb_w_in_2"][0]
    at = np.cumsum([0, 1024, 1536, 16, 1024, 1024, 1024, 8])
    zc, xbc, dt, q, k, vv, f = (w[:, a:b] for a, b in zip(at, at[1:]))
    blocks(xbc)
    put(np.concatenate([dt, f], 1).reshape(8, P, 24))
    blocks(np.concatenate([zc, q, k, vv], 1))
    blocks(v["hyb_w_out_2"][0])
    ffn(wi[0, 1], wo[0, 1])
    ffn(wi[1, 0], wo[1, 0])
    blocks(np.concatenate([v["rec_w_in_2"][0][:, D:], v["rec_w_in_2"][0][:, :D]], 1))
    put(np.concatenate([v["rec_w_a_2"][0], v["rec_w_x_2"][0]], 0))
    blocks(v["rec_w_out_2"][0])
    ffn(wi[1, 1], wo[1, 1])
    small2("pre", np.concatenate([feat(ng[l, i]) for l in range(2) for i in (0, 2, 4)], 1))
    small2("cw", v["ssm_conv_w_2"][0].reshape(4, 12, P).transpose(2, 1, 0).reshape(P, -1))
    small2("cb", feat(v["ssm_conv_b_2"][0]))
    small2("ng", feat(v["ssm_norm_g_2"][0]))
    small2("rw", v["rec_conv_w_2"][0].reshape(4, 8, P).transpose(2, 1, 0).reshape(P, -1))
    small2("rb", feat(v["rec_conv_b_2"][0]))
    small2("ba", feat(v["rec_b_a_2"][0]))
    small2("bx", feat(v["rec_b_x_2"][0]))
    small2("lam", feat(v["rec_lambda_2"][0]))
    small2("dtb", v["ssm_dt_bias_2"][0][None])
    small2("alog", v["ssm_a_log_2"][0][None])
    small2("dskip", v["ssm_d_2"][0][None])
    small2("fb", v["fox_b_f_2"][0][None])
    gains = np.stack([v["norm_final"]] + [ng[l, i] for l in range(2) for i in (1, 3, 5)])
    assert len(chunks) == 2 * LAYER_CHUNKS + TAIL_CHUNKS, len(chunks)
    const, hot = constants()
    rel = np.ones((33, 8), np.float32)
    rel[:32] = v["rel_bias"].reshape(32, 2, 4).transpose(0, 2, 1).reshape(32, 8)
    return {
        "w": np.stack(chunks), "const": const, "onehot": hot, "rel": rel, "x": rows(v["x"][0]), "mem": rows(v["mem"][0]),
        "positions": np.ascontiguousarray(v["positions"].reshape(TT, P).T), "smalls": smalls, "smalls2": smalls2, "gains": gains,
    }


def kernel(**inputs):
    import concourse.bacc as bacc
    from concourse.bass_utils import run_bass_kernel_spmd

    arrays = {"in_" + k: np.ascontiguousarray(a) for k, a in layout({k: np.asarray(a) for k, a in inputs.items()}).items()}
    learned = {}
    while True:
        nc = bacc.Bacc("TRN2", target_bir_lowering=False, num_devices=1)
        io = {k[3:]: nc.dram_tensor(k, a.shape, mybir.dt.from_np(a.dtype), kind="ExternalInput").ap() for k, a in arrays.items()}
        io["out"] = nc.dram_tensor("out", (P, TT, D), F32, kind="ExternalOutput").ap()
        io["skew"] = nc.dram_tensor("skew", (8, P * BLK), F32, kind="Internal").ap()
        seen = build(nc, io, learned)
        if seen == learned:
            break
        learned = seen
    r = run_bass_kernel_spmd(nc, [arrays], core_ids=[0])
    got = r.results[0]["out"]
    return got.transpose(1, 0, 2).reshape(1, T, D)
```

```python
from contextlib import contextmanager
from math import log, pi, sqrt

import numpy as np

import concourse.bass as bass
from concourse import mybir

F32 = mybir.dt.float32
F32R = mybir.dt.float32r
I32 = mybir.dt.int32
ALU = mybir.AluOpType
ACT = mybir.ActivationFunctionType
AX_X = mybir.AxisListType.X
ET = mybir.EngineType
ds = bass.ds

P = 128
TT = 2
T = P * TT
D = 1024
DEPTH = 2
KT = D // P
RING = 4
HALF = 1024
AHEAD = 4
CHUNK = 2048
BLK = 512
FF = 2816
FT = FF // P
GU = FF // 256
EPS = 1e-6
NEG = -1e30

Z_GM = 0
Z_Q = 4096
Z_KV = 4608
Z_CQ, Z_CKV, Z_KR, Z_GN = 5376, 5760, 6016, 6080
Z_COLS = 6104
ZW = 6144
CONV_W, CONV_CT = 31, 4
Q_RANK, KV_RANK = 384, 256
N_CMP = (T - 32) // 16 + 1
BAND = 384
S1 = {}
_o = 0
for _n, _w in (("mix", 8), ("xattn", 8), ("mem", 8), ("ffn", 8), ("conv_w", CONV_W * 4), ("conv_b", 4), ("ln_g", 4),
               ("ln_b", 4), ("pos", 32), ("b1", 4), ("w2k", 256), ("w2v", 128), ("mq", 3), ("mkv", 2)):
    S1[_n] = (_o, _o + _w)
    _o += _w
S1_W = _o
S2 = {}
_o = 0
for _n, _w in (("pre", 48), ("cw", 48), ("cb", 12), ("ng", 8), ("rw", 32), ("rb", 8), ("ba", 8), ("bx", 8), ("lam", 8),
               ("dtb", 16), ("alog", 16), ("dskip", 16), ("fb", 8)):
    S2[_n] = (_o, _o + _w)
    _o += _w
S2_W = _o
CC = {}
_o = 0
for _n, _w in (("ident", 128), ("ones", 128), ("upper", BAND), ("maskU", 128), ("mask", BAND), ("freq", 32), ("valid", 2)):
    CC[_n] = (_o, _o + _w)
    _o += _w
CC_W = _o
N_GAIN = 7

LAYER_CHUNKS = 24 + 4 + 2 + 2 + 3 + 2 + 4 + 4 + 2 + 2 + 33 + 2
TAIL_CHUNKS = 4 * 33 + 22 + 1 + 8 + 8 + 1 + 4
N_CHUNKS = 2 * LAYER_CHUNKS + TAIL_CHUNKS
LAYER_HALVES = 2 * (LAYER_CHUNKS - 24 - 4)
assert LAYER_CHUNKS % RING == 0


class Point:

    def __init__(self, sem, const, steps):
        self.sem, self.const, self.steps = sem, const, steps


class Count:

    def __init__(self, core, name):
        self.name, self.h, self.const, self.steps = name, core.nc.alloc_semaphore(name), 0, {}
        core.counts.append(self)

    def add(self, n=1):
        self.const += n
        return Point(self, self.const, dict(self.steps))


class Engine:
    def __init__(self, core, e, name):
        self.core, self.e, self.name, self.count, self.known = core, e, name, Count(core, "s_" + name), {}

    def wait(self, *points):
        for p in points:
            if callable(p):
                p = p()
            if isinstance(p, (tuple, list)):
                self.wait(*p)
                continue
            key = (p.sem.name, tuple(sorted(p.steps.items())))
            if self.known.get(key, -1) >= p.const or p.const <= 0 and not p.steps:
                continue
            self.known[key] = p.const
            v = p.const
            for name, step in p.steps.items():
                v = v + self.core.iteration(name) * step
            self.e.wait_ge(p.sem.h, v)
        return self.e

    def do(self, ins, count=None, n=1):
        count = count or self.count
        ins.then_inc(count.h, n)
        p = count.add(n)
        self.core.last[self.name] = (p,)
        return p

    @property
    def now(self):
        return self.core.last.get(self.name, ())

    def chain(self):
        return self.wait(self.now)


class Core:
    def __init__(self, nc, learned):
        self.nc, self.learned, self.counts, self.last, self.vars, self.trips = nc, learned, [], {}, {}, {}
        self.seen = {}
        self.PE, self.V = Engine(self, nc.tensor, "pe"), Engine(self, nc.vector, "dve")
        self.A, self.G = Engine(self, nc.scalar, "act"), Engine(self, nc.gpsimd, "pool")
        self.engines = (self.PE, self.V, self.A, self.G)
        self.n_loops = 0

    def iteration(self, name):
        return self.vars[name] if name in self.vars else self.trips[name] - 1

    @contextmanager
    def loop(self, n, meet=False):
        name = f"l{self.n_loops}"
        self.n_loops += 1
        if meet:
            self.meet()
        base = {c.name: c.const for c in self.counts}
        steps, ends = self.learned.get(name, ({}, {}))
        for c in self.counts:
            c.steps[name] = steps.get(c.name, 0)
        before = dict(self.last)
        if not meet:
            for key, points in ends.items():
                back = tuple(Point(next(c for c in self.counts if c.name == s), k - steps.get(s, 0), st)
                             for s, k, st in points)
                assert all(p.const > 0 for p in back), (name, key)
                self.last[key] = before.get(key, ()) + back
        started = dict(self.last)
        with self.nc.Fori(0, n, engines=(ET.Pool, ET.Activation, ET.PE, ET.DVE)) as i:
            self.vars[name] = i
            yield i
            if meet:
                self.phase(None)
                self.meet()
        self.seen[name] = (
            {c.name: c.const - base.get(c.name, 0) for c in self.counts},
            {k: [(p.sem.name, p.const, p.steps) for p in v if name in p.steps]
             for k, v in self.last.items() if v is not started.get(k)})
        del self.vars[name]
        self.trips[name] = n
        for c in self.counts:
            c.const += (n - 1) * (c.const - base.get(c.name, 0))
            c.steps.pop(name, None)
        for e in self.engines:
            e.known = {k: v for k, v in e.known.items() if name not in dict(k[1])}

    def meet(self):
        ends = [e.now for e in self.engines]
        for e in self.engines:
            e.wait(*ends)
        self.last = {e.name: self.last.get(e.name, ()) for e in self.engines}


def bc(ap, n):
    return ap.unsqueeze(len(ap.shape)).to_broadcast([*ap.shape, n])


def mid(ap, n):
    return ap.unsqueeze(1).to_broadcast([ap.shape[0], n, *ap.shape[1:]])


def build(nc, io, learned):
    core = Core(nc, learned)
    core.phase = lambda name: phase(name)
    PE, V, A, G = core.engines

    def sb(name, shape, dt=F32):
        return nc.alloc_sbuf_tensor(name, shape, dt)

    def twin(name, other, shape):
        if other is None:
            return sb(name, shape, F32R)
        return nc.alloc_sbuf_tensor_at(name, shape, F32R, offset=other)

    def sb_at(name, shape):
        at = (nc.sbuf_base + 31) // 32 * 32
        return sb(name, shape), at

    ps = nc.alloc_psum_tensor("ps", [P, 8, BLK], F32)
    ring, at = sb_at("ring", [P, RING, CHUNK])
    ring_lo = twin("ring_lo", at, [P, RING, CHUNK])
    upper_w = twin("upper_w", None, [P, AHEAD, HALF])
    x = sb("x", [P, TT, D])
    nT, at = sb_at("nT", [P, KT, T])
    nT_lo = twin("nT_lo", at, [P, KT, T])
    nT_hi = twin("nT_hi", None, [P, KT, T])
    big = sb("big", [P, 3200 + D])
    xn, at = sb_at("xn", [P, TT, D])
    xn_hi = twin("xn_hi", at, [P, KT, T])
    z, at = sb_at("z", [P, TT, ZW])
    z_hi = twin("z_hi", at, [P, TT, ZW])
    tT, at = sb_at("tT", [P, FT, T])
    tT_lo = twin("tT_lo", at, [P, FT, T])
    band = big[:, 0:8 * BAND].rearrange("p (h n) -> p h n", h=8)
    S = sb("S", [P, 2, 4, T])
    PTs = sb("PTs", [P, 2, 8, P])
    cbuf = sb("cbuf", [P, 1152])
    acc = sb("acc", [P, 6, T])
    const = sb("const", [P, CC_W])
    sm = sb("sm", [P, S1_W])
    sm2 = sb("sm2", [P, S2_W])
    st = sb("st", [P, 16])
    half = sb("half", [P, T])
    rope = sb("rope", [P, 2, TT, 32])
    ostage = sb("ostage", [P, TT, 512])
    junk = ostage[:, :, :].rearrange("p t n -> p (t n)")
    rs = sb("rs", [P, 2, 3, 4])

    def c_(name):
        a, b = CC[name]
        return const[:, a:b]

    def s1(name):
        a, b = S1[name]
        return sm[:, a:b]

    def s2(name, a=0, b=None):
        o, e = S2[name]
        return sm2[:, o + a:o + b if b is not None else e]

    ident, mask = c_("ident"), c_("mask")

    def load(queue, dst, src, *after):
        queue.wait(*after)
        c = Count(core, f"s_dma{len(core.counts)}")
        queue.e.dma_start(dst, src).then_inc(c.h, 16)
        return c.add(16)

    sm_count, mem_count = Count(core, "s_sm"), Count(core, "s_mem")
    loads_x = Count(core, "s_x")
    nc.sync.dma_start(x[:, :, :], io["x"]).then_inc(loads_x.h, 16)
    l_x = loads_x.add(16)
    const_count = Count(core, "s_const")
    nc.sync.dma_start(const[:, :], io["const"]).then_inc(const_count.h, 16)
    l_const = const_count.add(16)
    landed = [nc.alloc_semaphore(f"landed{s}") for s in range(RING)]
    used = Count(core, "used")
    cut = Count(core, "cut")
    with nc.named_scope("weights"):
        for s in range(RING):
            nc.sync.dma_start(ring[:, s, :], io["w"][s]).then_inc(landed[s], 16)
        whole = N_CHUNKS // RING
        with nc.Fori(0, whole - 1, engines=(ET.SP,)) as i:
            for s in range(RING):
                nc.sync.wait_ge(used.h, i * (2 * RING) + (2 * s + 3))
                nc.sync.dma_start(ring[:, s, :], io["w"][ds(i * RING + (RING + s), 1), :, :].rearrange("a p n -> p (a n)")
                                  ).then_inc(landed[s], 16)
        assert N_CHUNKS % RING == 0

    def landing(n):
        g = (used.const - 1 + n) // 2
        v = 16 * (g // RING + 1)
        for name, step in used.steps.items():
            assert step % (2 * RING) == 0 or not learned
            v = v + core.iteration(name) * (16 * step // (2 * RING))
        return landed[g % RING], v

    def chunk():
        assert used.const % 2 == 1
        sem, v = landing(0)
        PE.e.wait_ge(sem, v)
        return ring[:, (used.const - 1) // 2 % RING, :]

    run = {"left": 0, "ahead": 0}

    def start_run(halves):
        assert run["left"] == 0 and run["ahead"] == 0
        run["left"] = halves
        feed(AHEAD - 1)

    def feed(upto):
        while run["ahead"] < min(upto, run["left"]):
            n = run["ahead"]
            half_ = used.const - 1 + n
            at_ = (half_ // 2 % RING, slice(half_ % 2 * HALF, (half_ % 2 + 1) * HALF))
            src, rest = ring[:, at_[0], at_[1]], ring_lo[:, at_[0], at_[1]]
            up_ = upper_w[:, half_ % AHEAD, :]
            sem, v = landing(n)
            A.e.wait_ge(sem, v)
            if half_ - AHEAD >= 0:
                A.wait(Point(used, used.const + n - AHEAD + 1, dict(used.steps)))
            a = A.do(A.e.copy(up_, src))
            V.do(V.wait(a).tensor_tensor(rest, src, up_.bitcast(F32), ALU.subtract), cut)
            run["ahead"] += 1

    def next_half():
        feed(AHEAD)
        PE.wait(Point(cut, cut.const - run["ahead"] + 1, dict(cut.steps)))
        h = used.const - 1
        run["ahead"] -= 1
        run["left"] -= 1
        return upper_w[:, h % AHEAD, :], ring_lo[:, h // 2 % RING, h % 2 * HALF:(h % 2 + 1) * HALF]

    def three(out, hi, lo, w_hi, w_lo, start, stop):
        PE.e.matmul(out, hi, w_hi, start=start, stop=False)
        PE.e.matmul(out, hi, w_lo, start=False, stop=False)
        return PE.e.matmul(out, lo, w_hi, start=False, stop=stop)

    bank_turn = [0]
    scope = []

    def phase(name):
        if scope:
            scope.pop().__exit__(None, None, None)
        if name:
            scope.append(nc.named_scope(name))
            scope[-1].__enter__()

    def free(*banks):
        return [core.last.get(f"b{b}", ()) for b in banks]

    def released(point, *banks):
        for b in banks:
            core.last[f"b{b}"] = (point,)

    def gemm_block(lhs, kts, pair, ready, beside=None, at=0, by_row=False):
        each = isinstance(ready, list)
        banks = (pair, pair + 2) if by_row else (2 * pair, 2 * pair + 1)
        PE.wait(free(*banks), () if each else ready)
        for c in range(kts // 2):
            if isinstance(lhs, tuple):
                w_hi, w_lo = next_half()
            elif c % 2 == 0:
                w = chunk()
            for k in range(2):
                f, first, last = 2 * c + k, c == 0 and k == 0, 2 * c + k == kts - 1
                if each:
                    PE.wait(ready[f])
                for t in range(TT):
                    o, tok = ps[:, banks[t], :], slice(t * P, (t + 1) * P)
                    if isinstance(lhs, tuple):
                        m = three(o, lhs[0][:, f, tok], lhs[1][:, f, tok], w_hi[:, k * BLK:(k + 1) * BLK],
                                  w_lo[:, k * BLK:(k + 1) * BLK], first, last)
                    else:
                        m = PE.e.matmul(o, lhs[:, f, tok], w[:, (2 * (c % 2) + k) * BLK:(2 * (c % 2) + k + 1) * BLK], start=first, stop=last)
            p = PE.do(m, used)
            if beside:
                beside(at + c)
        return p, ps[:, banks[0]:banks[1] + 1:banks[1] - banks[0], :]

    def gemm(lhs, kts, blocks, evac, ready=(), first=0, beside=None, by_row=False):
        def body(at, j):
            p, o = gemm_block(lhs, kts, j, ready, beside, (at - first) * (kts // 2), by_row)
            released(evac(p, o, at, j), *((j, j + 2) if by_row else (2 * j, 2 * j + 1)))
        whole = blocks // 2 if kts == KT and isinstance(lhs, tuple) else 0
        while whole and run["left"] - 8 * whole < AHEAD - 1:
            whole -= 1
        if whole > 1:
            assert run["ahead"] == AHEAD - 1
            with core.loop(whole) as i:
                for j in range(2):
                    body(i * 2 + (j + first), j)
            run["left"] -= 8 * (whole - 1)
        else:
            whole = 0
        for b in range(2 * whole, blocks):
            body(first + b, b % 2)

    def block_of(buf, b):
        return buf[:, :, b * BLK:(b + 1) * BLK] if isinstance(b, int) else buf[:, :, ds(b * BLK, BLK)]

    def to_T(src, tiles, dst, evac=None, ready=()):
        out = ()
        for c in range(0, tiles, 2):
            n = min(2, tiles - c)
            b = 6 + bank_turn[0] % 2
            bank_turn[0] += 1
            PE.wait(free(b), ready)
            for i in range(n):
                for t in range(TT):
                    m = PE.e.transpose(ps[:, b, (i * TT + t) * P:(i * TT + t + 1) * P], src(c + i, t), ident)
            p = PE.do(m)
            o = ps[:, b, 0:n * T].rearrange("p (c n) -> p c n", c=n)
            if evac:
                e = evac(p, o, c, n)
            elif b == 6:
                e = V.do(V.wait(p).tensor_copy(dst[:, c:c + n, :], o))
            else:
                e = A.do(A.wait(p).copy(dst[:, c:c + n, :], o))
            released(e, b)
            out = out + (e,)
        return out[-2:]

    def rstd(srcs, n, at, ready):
        k = len(srcs)
        for i, s in enumerate(srcs):
            p = A.do(A.wait(ready, V.now, PE.now, A.now).activation(junk[:, 0:n], s, ACT.Square, accum_out=st[:, at + i:at + i + 1]))
        p = V.do(V.wait(p, G.now).tensor_scalar(st[:, at:at + k], st[:, at:at + k], 1.0 / n, EPS, ALU.mult, ALU.add))
        return G.do(G.wait(p).tensor_tensor(st[:, at:at + k], st[:, at:at + k], half[:, 0:k], ALU.pow))

    nT_parts = (nT_hi[:, :, :], nT_lo[:, :, :])

    class Parts:

        def __init__(self, at=0):
            self.at = at

        def __getitem__(self, key):
            _, c, tok = key
            if isinstance(c, slice):
                assert c.start // 11 == (c.stop - 1) // 11
                o = FF + c.start % 11 * T
                return z_hi[:, c.start // 11, o:o + (c.stop - c.start) * T].rearrange("p (c n) -> p c n", n=T)
            o = FF + c % 11 * T
            return z_hi[:, c // 11, o + (tok.start or 0):o + (T if tok.stop is None else tok.stop)]

    class Joined:

        def __init__(self, a, b, n):
            self.a, self.b, self.n = a, b, n

        def __getitem__(self, key):
            _, c, tok = key
            return self.a[:, c, tok] if c < self.n else self.b[:, c - self.n, tok]

    def to_parts(src, tiles, hi, lo, ready, gain=None, banks=(4, 5, 6, 7)):
        points = []
        for c in range(0, tiles, 2):
            b = banks[c // 2 % len(banks)]
            n = min(2, tiles - c)
            PE.wait(free(b), ready[c // 4] if isinstance(ready, list) else ready)
            for i in range(n):
                for t in range(TT):
                    m = PE.e.transpose(ps[:, b, (i * TT + t) * P:(i * TT + t + 1) * P], src(c + i, t), ident)
            p = PE.do(m)
            o = [ps[:, b, i * T:(i + 1) * T] for i in range(2)]
            for i in range(n):
                g = None if gain is None else gain[:, c + i:c + i + 1]
                a = A.do(A.wait(p).copy(hi[:, c + i, :], o[i]) if g is None else A.wait(p).mul(hi[:, c + i, :], o[i], g))
            V.wait(a)
            for i in range(n):
                g, h = None if gain is None else gain[:, c + i:c + i + 1], hi[:, c + i, :].bitcast(F32)
                v = V.do(V.e.tensor_tensor(lo[:, c + i, :], o[i], h, ALU.subtract) if g is None
                         else V.e.scalar_tensor_tensor(lo[:, c + i, :], o[i], g, h, ALU.mult, ALU.subtract))
                points.append(v)
            released(v, b)
            yield points

    def norm_parts(src, gain, ready, at=8, hi=nT_hi, lo=nT_lo):
        for points in to_parts(lambda c, t: src[:, t, c * P:(c + 1) * P], KT, hi, lo, ready, gain):
            pass
        ready = [q for r in ready for q in (r if isinstance(r, (tuple, list)) else (r,))] if isinstance(ready, list) else ready
        r = rstd([src[:, t, :] for t in range(TT)], D, at, ready)
        core.last["rstd"] = (r,)
        return points

    def scaled(engine, p, dst, o, at=8, func=ACT.Copy):
        for t in range(TT):
            if engine is A:
                e = A.do(A.wait(p, last_of("rstd")).activation(dst[:, t, :], o[:, t, :], func, scale=st[:, at + t:at + t + 1]))
            else:
                e = V.do(V.wait(p, last_of("rstd")).tensor_scalar(dst[:, t, :], o[:, t, :], st[:, at + t:at + t + 1], None, ALU.mult))
        return e

    def add_x(p, o, b, pair):
        cols = x[:, :, ds(b * BLK, BLK)] if not isinstance(b, int) else x[:, :, b * BLK:(b + 1) * BLK]
        return V.do(V.wait(p, A.now).tensor_tensor(cols, cols, o, ALU.add))

    def ffn_up(ready):
        def evac(p, o, b, pair):
            g = acc[:, 2 * pair:2 * pair + 2, :]
            a = scaled(A, (p, last_of(f"sg{pair}")), g, o[:, :, 0:256], func=ACT.Silu)
            dst = z[:, :, ds(b * 256, 256)] if not isinstance(b, int) else z[:, :, b * 256:(b + 1) * 256]
            for t in range(TT):
                v = V.do(V.wait(a).scalar_tensor_tensor(dst[:, t, :], o[:, t, 256:512], st[:, 8 + t:9 + t], g[:, t, :], ALU.mult, ALU.mult))
            core.last[f"sg{pair}"] = (v,)
            return v
        for j in range(2):
            core.last[f"sg{j}"] = V.now
        gemm(nT_parts, KT, GU, evac, ready)
        return V.now

    def last_of(name):
        return core.last.get(name, ())

    def ffn_down(ready):
        hi = Parts()
        parts = to_parts(lambda c, t: z[:, t, c * P:(c + 1) * P], FT, hi, tT_lo, ready, banks=(4, 5, 6, 7))
        for _ in range(3):
            points = next(parts)
        PE.wait(free(0, 1, 2, 3))
        for c in range(FT):
            if c % 2 and c + 5 < FT:
                next(parts)
            PE.wait(points[c])
            w_hi, w_lo = next_half()
            for h in range(2):
                for t in range(TT):
                    tok, cols = slice(t * P, (t + 1) * P), slice(h * BLK, (h + 1) * BLK)
                    m = three(ps[:, 2 * t + h, :], hi[:, c, tok], tT_lo[:, c, tok], w_hi[:, cols], w_lo[:, cols], c == 0, c == FT - 1)
            p = PE.do(m, used)
        return p

    def attention(units, beside={}):
        def front(u, i):
            s, b = i % 2, 2 * (i % 2)
            PE.wait(free(b, b + 1), u.get("ready", ()))
            o = ps[:, b:b + 2, :].rearrange("p a (h k) -> p (a h) k", h=2)
            p = PE.do(u["scores"](o))
            Su, nm, sums = S[:, s], rs[:, s, 0, :], rs[:, s, 1, :]
            V.wait(p, last_of(f"S{s}"), last_of(f"rs{s}"))
            if u["add"] is not None:
                v = V.do(V.e.scalar_tensor_tensor(Su, o, u["scale"], u["add"], ALU.mult, ALU.add))
                src, scale = Su, 1.0
                released(v, b, b + 1)
                V.wait(v)
                v = V.do(V.e.tensor_reduce(nm, Su, AX_X, ALU.max, negate=True))
            else:
                v = V.do(V.e.tensor_reduce(nm, o, AX_X, ALU.max, negate=True))
                v = V.do(V.wait(v).tensor_scalar(nm, nm, u["scale"], None, ALU.mult))
                src, scale = o, u["scale"]
            A.wait(v, last_of(f"S{s}"))
            for h in range(4):
                a = A.do(A.e.activation(Su[:, h, :], src[:, h, :], ACT.Exp, bias=nm[:, h:h + 1], scale=scale,
                                        accum_out=sums[:, h:h + 1]))
            if u["add"] is None:
                released(a, b, b + 1)
            core.last[f"P{s}"] = (a,)

        def middle(u, i):
            s = i % 2
            u["inverse"] = V.do(V.wait(last_of(f"P{s}")).reciprocal(rs[:, s, 2, :], rs[:, s, 1, :]))
            PE.wait(last_of(f"P{s}"), free(4, 5))
            for h in range(4):
                for kt in range(TT):
                    m = PE.e.transpose(ps[:, 4 + h // 2, (h % 2 * TT + kt) * P:(h % 2 * TT + kt + 1) * P],
                                       S[:, s, h, kt * P:(kt + 1) * P], ident)
            p = PE.do(m)
            core.last[f"S{s}"] = (p,)
            e0 = V.do(V.wait(p, last_of(f"PT{s}")).tensor_copy(PTs[:, s, 0:4, :], ps[:, 4, :].rearrange("p (a b) -> p a b", a=4)))
            e1 = A.do(A.wait(p, last_of(f"PT{s}")).copy(PTs[:, s, 4:8, :], ps[:, 5, :].rearrange("p (a b) -> p a b", a=4)))
            released(e0, 4)
            released(e1, 5)
            u["PT"] = (e0, e1)

        def back(u, i):
            s, b = i % 2, 6 + i % 2
            PE.wait(u["PT"], free(b), *u.get("values", ()))
            dv = u["dv"]
            for h in range(4):
                for kt in range(TT):
                    m = PE.e.matmul(ps[:, b, h * dv:(h + 1) * dv], PTs[:, s, 2 * h + kt, :], u["value"](h, kt),
                                    start=(kt == 0), stop=(kt == TT - 1))
            p = PE.do(m)
            core.last[f"PT{s}"] = (p,)
            e = u["out"](ps[:, b, 0:4 * dv].rearrange("p (h d) -> p h d", h=4), rs[:, s, 2, :], (p, u["inverse"]))
            core.last[f"rs{s}"] = (e,)
            released(e, b)
            return e

        front(units[0], 0)
        front(units[1], 1)
        beside.get("first", lambda: None)()
        for i in range(len(units)):
            middle(units[i], i)
            if i + 2 < len(units):
                front(units[i + 2], i + 2)
            e = back(units[i], i)
            beside.get(i, lambda: None)()
        return e

    def plain_out(dst):
        def out(o, inv, ready):
            return V.do(V.wait(*ready).tensor_tensor(dst, o, bc(inv, o.shape[2]), ALU.mult))
        return out

    relT = acc[0:33, 0, 0:8]
    hot = cbuf[0:33, 0:BLK]
    l_rel = load(A, relT, io["rel"])
    l_hot = load(A, hot, io["onehot"])
    l_pos = load(A, st[:, 0:TT].bitcast(I32), io["positions"])
    A.e.dma_start(sm[:, :], io["smalls"][0]).then_inc(sm_count.h, 16)
    sm_count.add(16)
    l_sm2 = load(A, sm2[:, :], io["smalls2"])
    halved = G.do(G.e.memset(half[:, :], -0.5))
    PE.wait(l_rel, l_hot)
    p = PE.do(PE.e.matmul(ps[0:8, 6, :], relT, hot, start=True, stop=True), used)
    p = V.do(V.wait(p).tensor_copy(acc[0:8, 2:4, :], ps[0:8, 6, :].rearrange("p (a b) -> p a b", a=2)))
    released(p, 6)
    skew = io["skew"]
    p = load(G, skew.rearrange("h (r j) -> h r j", r=P), mid(acc[0:8, 2:4, :].rearrange("p a b -> p (a b)"), P), p)
    G.wait(p)
    skewed = bass.AP(skew.tensor, skew.offset + P - 1, [[BLK - 1, P], [P * BLK, 8], [1, BAND]])
    l_band = load(G, band[:, :, :], skewed)
    V.wait(l_pos, l_const)
    V.do(V.e.tensor_copy(st[:, 2:4], st[:, 0:TT].bitcast(I32)))
    ang = junk[:, 0:64].rearrange("p (t f) -> p t f", t=TT)
    V.do(V.chain().tensor_tensor(ang, bc(st[:, 2:4], 32), mid(c_("freq"), TT), ALU.mult))
    MAGIC = 1.5 * 2.0 ** 23
    two_pi = 2 * pi
    c1 = float(np.float32(np.floor(two_pi * 2 ** 9) / 2 ** 9))
    c2 = float(np.float32(np.floor((two_pi - c1) * 2 ** 22) / 2 ** 22))
    c3 = float(np.float32(two_pi - c1 - c2))
    for i, shift in ((0, 0.25), (1, 0.0)):
        a, k = junk[:, 64:128].rearrange("p (t f) -> p t f", t=TT), junk[:, 128:192].rearrange("p (t f) -> p t f", t=TT)
        V.do(V.chain().tensor_scalar(k, ang, 1 / two_pi, shift, ALU.mult, ALU.add))
        V.do(V.chain().tensor_scalar(k, k, MAGIC, None, ALU.add))
        V.do(V.chain().tensor_scalar(k, k, -MAGIC, None, ALU.add))
        V.do(V.chain().scalar_tensor_tensor(a, k, -c1, ang, ALU.mult, ALU.add))
        V.do(V.chain().scalar_tensor_tensor(a, k, -c2, a, ALU.mult, ALU.add))
        V.do(V.chain().scalar_tensor_tensor(a, k, -c3, a, ALU.mult, ALU.add))
        V.do(V.chain().tensor_scalar(a, a, 2 * pi * shift, 3.1415925, ALU.add, ALU.min))
        V.do(V.chain().tensor_scalar(a, a, -3.1415925, None, ALU.max))
        p = A.do(A.wait(V.now).activation(rope[:, i], a, ACT.Sin))
        V.wait(p)
    def view(buf, a, b):
        return buf[:, a:b, :].rearrange("p a b -> p (a b)")
    kz = view(tT, 12, 16).rearrange("p (b g n) -> p b g n", b=2, g=2)
    vb = view(tT, 16, 18).rearrange("p (g m d) -> p g m d", g=2, m=4)
    pcmp = view(tT, 18, 20).rearrange("p (t g m c) -> p t g m c", t=TT, g=2, m=4)
    cmpb = view(nT, 0, 4)[:, 0:32 * 2 * N_CMP].rearrange("p (k j g c) -> p k j g c", k=2, j=16, g=2)
    kpz = nT[:, 4:6, :]
    kcz = sb("kcz", [P, 2, 16])
    hidT = sb("hidT", [P, 2, 2, 32])
    cmp_in = tT[:, 8:12, :].rearrange("p a b -> p (a b)").rearrange("p (t k r d) -> p t k r d", t=TT, k=4, r=2)
    gain = big[:, 3200:3200 + D]
    loading = {}

    def load_gain(i):
        loading["gain"] = load(A if i else G, gain, io["gains"][i].partition_broadcast(P), V.now, PE.now)
    load_gain(0)
    for e in core.engines:
        e.wait(l_const, l_x, p)

    with core.loop(DEPTH, meet=True) as layer:
        l_sm = Point(sm_count, sm_count.const, dict(sm_count.steps))
        for e in core.engines:
            e.wait(l_sm)
        phase("w_in")
        start_run(48)
        n = norm_parts(x[:, :, :], s1("mix"), ())

        def evac_gate(p, o, b, pair):
            return scaled(A, p, block_of(z, b), o, func=ACT.Sigmoid)

        def evac_z(p, o, b, pair):
            dst = block_of(z, b)
            return scaled(A if pair == 1 else V, p, dst, o)
        def evac_glu(p, o, b, pair):
            if b == 0:
                return scaled(A, (p, A.now), ostage[:, :, :], o, func=ACT.Sigmoid)
            for t in range(TT):
                v = V.do(V.wait(p, A.now, last_of("rstd")).scalar_tensor_tensor(ostage[:, t, :], o[:, t, :], st[:, 8 + t:9 + t],
                                                                                ostage[:, t, :], ALU.mult, ALU.mult))
            return v
        gemm(nT_parts, KT, 2, evac_glu, n)
        u_rows = V.now
        gemm(nT_parts, KT, 1, evac_gate)
        LEFT = CONV_W - 1
        u = cbuf[:, 0:CONV_CT * (LEFT + T)].rearrange("p (c n) -> p c n", c=CONV_CT)
        m0 = V.do(V.e.memset(u[:, :, 0:LEFT], 0.0))

        def evac_u(p, o, c, k):
            return A.do(A.wait(p).copy(u[:, c:c + k, LEFT:LEFT + T], o))
        e = to_T(lambda c, t: ostage[:, t, c * P:(c + 1) * P], CONV_CT, u, evac_u, u_rows)
        cw = s1("conv_w").rearrange("p (c k) -> p c k", c=CONV_CT)

        def tap(k):
            for c in range(CONV_CT):
                V.wait(last_of(f"tap{c}"))
                if isinstance(k, int) and k == 0:
                    ins = V.e.tensor_scalar(acc[:, c, :], u[:, c, 0:T], cw[:, c, 0:1], s1("conv_b")[:, c:c + 1], ALU.mult, ALU.add)
                else:
                    at_ = slice(k, k + T) if isinstance(k, int) else ds(k, T)
                    w_ = slice(k, k + 1) if isinstance(k, int) else ds(k, 1)
                    ins = V.e.scalar_tensor_tensor(acc[:, c, :], u[:, c, at_], cw[:, c, w_], acc[:, c, :], ALU.mult, ALU.add)
                core.last[f"tap{c}"] = (V.do(ins),)
        gemm(nT_parts, KT, 1, evac_gate, first=1)
        V.wait(e, m0)
        tap(0)
        gemm(nT_parts, KT, 4, evac_gate, first=2, beside=lambda n_: tap(n_ + 1))
        def rest(n_):
            if n_ + 17 < CONV_W:
                tap(n_ + 17)
            else:
                for buf in ((kz, kcz[:, :, :]), (vb, pcmp))[n_ + 17 - CONV_W]:
                    core.last["zeroed"] = (V.do(V.e.memset(buf, 0.0)),)
        gemm(nT_parts, KT, 4, evac_z, first=8, beside=rest)
        zeroed = last_of("zeroed")
        z_done = (V.now, A.now)
        g_n = A.do(A.wait(z_done).activation(z[:, :, Z_GN:Z_GN + 24], z[:, :, Z_GN:Z_GN + 24], ACT.Sigmoid))
        conv_done = V.now
        phase("cmp")
        p = V.do(V.wait(z_done).tensor_copy(cmp_in[:, 0], z[:, 0, Z_KV:Z_KV + 256].rearrange("p (k d) -> p k d", k=4).unsqueeze(2).to_broadcast([P, 4, 2, 64])))
        p = V.do(V.wait(z_done).tensor_copy(cmp_in[:, 1], z[:, 1, Z_KV:Z_KV + 256].rearrange("p (k d) -> p k d", k=4).unsqueeze(2).to_broadcast([P, 4, 2, 64])))
        cmp_ready = p
        kpz_zeroed = V.do(V.wait(PE.now).memset(kpz, 0.0))
        qT = tT
        q_ready = to_T(lambda c, t: z[:, t, Z_Q + c * P:Z_Q + (c + 1) * P], 4, qT, ready=z_done)

        def evac_k(p, o, c, k):
            a = A.do(A.wait(p, zeroed).copy(kz[0:64, :, 0, :], o[0:64]))
            return A.do(A.e.copy(kz[64:128, :, 1, :], o[64:128]))
        k_ready = to_T(lambda c, t: z[:, t, Z_KV + (2 + 2 * c) * P:Z_KV + (3 + 2 * c) * P], 2, None, evac_k, z_done)

        ones = c_("ones")
        acc4 = acc[:, 0:4, :]
        sq = cbuf[:, 0:4 * T].rearrange("p (c n) -> p c n", c=4)
        mu, rd = S[:, 0, 2, :], S[:, 0, 3, :]
        PE.wait(conv_done, free(4))
        for c in range(CONV_CT):
            m = PE.e.matmul(ps[:, 4, 0:T], ones, acc[:, c, :], start=(c == 0), stop=(c == CONV_CT - 1))
        p = PE.do(m)
        V.do(V.wait(p, A.now).tensor_scalar(mu, ps[:, 4, 0:T], 1.0 / 512, None, ALU.mult))
        released(V.now[0], 4)
        V.do(V.chain().tensor_tensor(acc4, acc4, mid(mu, 4), ALU.subtract))
        squares = A.do(A.wait(V.now, PE.now).activation(sq, acc4, ACT.Square))

        pos = s1("pos").rearrange("p (k j) -> p k j", k=2)

        def evac_b(p, o, c, k):
            V.wait(p)
            for i in range(k):
                kind, g = (c + i) // 2, (c + i) % 2
                for lo in range(2):
                    half_ = slice(64 * lo, 64 * lo + 64)
                    src = o[half_, i, :]
                    src = bass.AP(src.tensor, src.offset + lo, [list(src.ap[0]), [2, 16], [16, N_CMP]])
                    v = V.do(V.e.tensor_tensor(cmpb[half_, kind, :, g, :], src, bc(pos[half_, kind, :], N_CMP), ALU.add))
            return v
        b_ready = to_T(lambda c, t: cmp_in[:, t, c].rearrange("p r d -> p (r d)"), 4, None, evac_b, cmp_ready)
        PE.wait(squares, free(0))
        for c in range(CONV_CT):
            m = PE.e.matmul(ps[:, 0, 0:T], ones, sq[:, c, :], start=(c == 0), stop=(c == CONV_CT - 1))
        p = PE.do(m)
        V.do(V.wait(p).tensor_scalar(rd, ps[:, 0, 0:T], 1.0 / 512, EPS, ALU.mult, ALU.add))
        released(V.now[0], 0)
        V.do(V.chain().reciprocal(rd, rd))
        p = A.do(A.wait(V.now).activation(rd, rd, ACT.Sqrt))
        V.do(V.wait(p).tensor_tensor(acc4, acc4, mid(rd, 4), ALU.mult))
        A.wait(V.now)
        for c in range(CONV_CT):
            p = A.do(A.e.activation(acc[:, c, :], acc[:, c, :], ACT.Silu, bias=s1("ln_b")[:, c:c + 1], scale=s1("ln_g")[:, c:c + 1]))
        four = (nT_hi[:, 0:4, :], tT_lo[:, 4:8, :])
        a = A.do(A.wait(p).copy(four[0], acc4))
        conv_T = V.do(V.wait(a).tensor_tensor(four[1], acc4, four[0].bitcast(F32), ALU.subtract))
        PE.wait(b_ready, free(6))
        for kind in range(2):
            for cc in range(2):
                w = chunk()
                for j in range(8):
                    if j == 4:
                        PE.do(m, used)
                    m = PE.e.matmul(ps[0:30, 6, kind * 256:(kind + 1) * 256], cmpb[:, kind, 8 * cc + j, :, :].rearrange("p g c -> p (g c)"),
                                    w[:, j * 256:(j + 1) * 256], start=(cc == 0 and j == 0), stop=(cc == 1 and j == 7))
                p = PE.do(m, used)
        hid = S[0:30, 0, 0:2, :]
        v = V.do(V.wait(p, A.now, V.now).tensor_copy(hid, ps[0:30, 6, :].rearrange("p (k n) -> p k n", k=2)))
        released(v, 6)
        PE.wait(v, free(7))
        for kind in range(2):
            for ht in range(2):
                o = 32 * (2 * kind + ht)
                m = PE.e.matmul(ps[:, 7, o:o + 30], hid[:, kind, ht * P:(ht + 1) * P], ident[0:30, 0:30], start=True, stop=True)
        p = PE.do(m)
        for kind in range(2):
            for ht in range(2):
                o = 32 * (2 * kind + ht)
                a = A.do(A.wait(p).activation(hidT[:, kind, ht, 0:30], ps[:, 7, o:o + 30], ACT.Gelu_apprx_tanh,
                                              bias=s1("b1")[:, 2 * kind + ht:2 * kind + ht + 1]))
        released(a, 7)
        w2k, w2v = s1("w2k").rearrange("p (h n) -> p h n", h=2), s1("w2v").rearrange("p (h n) -> p h n", h=2)
        PE.wait(a, free(6, 7))
        for ht in range(2):
            m = PE.e.matmul(ps[:, 6, 0:30], w2k[:, ht, :], hidT[:, 0, ht, 0:30], start=(ht == 0), stop=(ht == 1))
        p = PE.do(m)
        for g in range(2):
            for ht in range(2):
                m = PE.e.matmul(ps[0:15, 7, g * 64:(g + 1) * 64], hidT[:, 1, ht, g * 15:(g + 1) * 15], w2v[:, ht, :],
                                start=(ht == 0), stop=(ht == 1))
        q = PE.do(m)
        V.wait(p, zeroed)
        V.do(V.e.tensor_copy(kcz[0:64, 0, 0:15], ps[0:64, 6, 0:15]))
        released(V.do(V.e.tensor_copy(kcz[64:128, 1, 0:15], ps[64:128, 6, 15:30])), 6)
        A.wait(q)
        for m_ in range(4):
            a = A.do(A.e.copy(vb[32 * m_:32 * m_ + 15, :, m_, :], ps[0:15, 7, 0:128].rearrange("p (g d) -> p g d", g=2)))
        released(a, 7)
        kv_ready = (V.now, A.now)
        start_run(LAYER_HALVES)
        phase("cmp_attn")
        PE.wait(kv_ready, q_ready, free(6, 7))
        for t in range(TT):
            for m_ in range(4):
                m = PE.e.matmul(ps[:, 6, (t * 4 + m_) * 32:(t * 4 + m_ + 1) * 32], qT[:, m_, t * P:(t + 1) * P],
                                kcz[:, :, :].rearrange("p g c -> p (g c)"), start=True, stop=True)
        p = PE.do(m)
        merged = xn

        def heads_parts(ready, parts=four):
            for points in to_parts(lambda c, t: ostage[:, t, c * P:(c + 1) * P], 4, *parts, ready):
                pass
            return points

        merged_at = []

        def evac_merge(j):
            def evac(p, o, b, pair):
                g = z[:, :, j * D + b * BLK:j * D + (b + 1) * BLK]
                dst = merged[:, :, b * BLK:(b + 1) * BLK]
                if j == 0:
                    return V.do(V.wait(p).tensor_tensor(dst, o, g, ALU.mult))
                e = V.do(V.wait(p, G.now).tensor_tensor(g, o, g, ALU.mult))
                merged_at.append(V.do(V.chain().tensor_tensor(dst, dst, g, ALU.add)))
                return e
            return evac
        sc = S[:, 0, 0, 0:TT * 8 * 16].rearrange("p (t h c) -> p t h c", t=TT, h=8)
        V.wait(p, PE.now, l_band)
        for t in range(TT):
            first = 31 + P * (1 - t)
            V.do(V.e.scalar_tensor_tensor(sc[:, t, :, 0:N_CMP], ps[:, 6, t * 128:(t + 1) * 128].rearrange("p (h c) -> p h c", h=8)[:, :, 0:N_CMP],
                                          0.125, band[:, :, first:first + 16 * (N_CMP - 1) + 1:16], ALU.mult, ALU.add))
        released(V.now[0], 6)
        scf = sc.rearrange("p t h c -> p (t h) c")[:, :, 0:N_CMP]
        cst = S[:, 1, 0, 0:128]
        cmx, csum, cf = cst[:, 0:16], cst[:, 16:32], cst[:, 32:48]
        V.do(V.chain().tensor_reduce(cmx, scf, AX_X, ALU.max))
        V.do(V.chain().tensor_tensor(scf, scf, bc(cmx, N_CMP), ALU.subtract))
        p = A.do(A.wait(V.now).activation(scf, scf, ACT.Exp))
        V.do(V.wait(p).tensor_reduce(csum, scf, AX_X, ALU.add))
        for t in range(TT):
            pc = V.do(V.wait(p, PE.now).tensor_copy(pcmp[:, t, :, :, 0:N_CMP], sc[:, t, :, 0:N_CMP].rearrange("p (m g) c -> p g m c", m=4)))
        V.do(V.chain().reciprocal(cf, csum))
        cf4 = cf.rearrange("p (t h) -> p t h", t=TT)
        gates = z[:, :, Z_GN:Z_GN + 24].rearrange("p t (j h) -> p t j h", j=3)
        V.do(V.wait(g_n, V.now).tensor_tensor(cf4, cf4, gates[:, :, 0, :], ALU.mult))
        V.do(V.chain().tensor_tensor(cf4, cf4, bc(c_("valid"), 8), ALU.mult))
        gemm(four, 4, 1, evac_merge(0), conv_T)

        def conv_product():
            p, o = gemm_block(four, 4, 3, ())
            released(evac_merge(0)(p, o, 1, 3), 6, 7)
        PE.wait(pc, free(7, 6))
        for t in range(TT):
            for g in range(2):
                m = PE.e.transpose(ps[:, 7, (2 * t + g) * P:(2 * t + g + 1) * P], pcmp[:, t, g].rearrange("p m c -> p (m c)"), ident)
        p = PE.do(m)
        pcT = S[:, 1, 2:4, :].rearrange("p a b -> p (a b)")
        a = A.do(A.wait(p).copy(pcT, ps[:, 7, :]))
        released(a, 7)
        PE.wait(a, free(4, 5))
        for t in range(TT):
            for g in range(2):
                m = PE.e.matmul(ps[:, 4 + t, g * 256:(g + 1) * 256], pcT[:, (2 * t + g) * P:(2 * t + g + 1) * P],
                                vb[:, g].rearrange("p m d -> p (m d)"), start=True, stop=True)
        p = PE.do(m)
        ov = ostage[:, :, :].rearrange("p t (m g d) -> p t m g d", m=4, g=2)
        cfg = cf.rearrange("p (t m g) -> p t m g", t=TT, m=4)
        for t in range(TT):
            for g in range(2):
                v = V.do(V.wait(p, V.now).tensor_tensor(ov[:, t, :, g, :], ps[:, 4 + t, g * 256:(g + 1) * 256].rearrange("p (m d) -> p m d", m=4),
                                                 bc(cfg[:, t, :, g], 64), ALU.mult))
            released(v, 4 + t)
        for nm in ("S0", "S1", "rs0", "rs1", "PT0", "PT1"):
            core.last[nm] = V.now + A.now + PE.now
        phase("nsa_attn")
        fac = sb("fac", [P, 2, 4])
        units = []
        for br in range(2):
            for t in range(TT):
                for mp in range(2):
                    def scores(o, t=t, mp=mp, br=br):
                        for i in range(2):
                            m = PE.e.matmul(o[:, 2 * i:2 * i + 2, :].rearrange("p g k -> p (g k)"), qT[:, 2 * mp + i, t * P:(t + 1) * P],
                                            kz[:, br, :, :].rearrange("p g k -> p (g k)"), start=True, stop=True)
                        return m

                    def out(o, inv, ready, t=t, mp=mp, br=br):
                        f = fac[:, mp, :]
                        V.do(V.wait(*ready, V.now).tensor_tensor(f, inv, z[:, t, Z_GN + 8 + br * 8 + 4 * mp:Z_GN + 12 + br * 8 + 4 * mp], ALU.mult))
                        tmp = acc[:, 4 + mp, :].rearrange("p (h d) -> p h d", h=4)
                        e = V.do(V.chain().tensor_tensor(tmp, o, bc(f, 64), ALU.mult))
                        dst = ostage[:, t, 256 * mp:256 * (mp + 1)].rearrange("p (h d) -> p h d", h=4)
                        V.do(V.chain().tensor_tensor(dst, dst, tmp, ALU.add))
                        return e
                    off = P * (1 - t)
                    units.append(dict(
                        scores=scores, scale=0.125, add=band[:, 4 * mp:4 * mp + 4, off:off + T], dv=64, out=out, ready=(k_ready, q_ready),
                        value=lambda h, kt, br=br: z[:, kt, Z_KV + (3 + 2 * br) * P + h % 2 * 64:Z_KV + (3 + 2 * br) * P + h % 2 * 64 + 64]))
        attention(units, {"first": conv_product})
        nsa_done = V.now

        phase("w_nsa")
        nsa_parts = tuple(z_hi[:, t, 0:D].rearrange("p (c n) -> p c n", c=4) for t in range(TT))
        nsa_ready = heads_parts(nsa_done, nsa_parts)

        def nsa_product():
            for b in range(2):
                p, o = gemm_block(nsa_parts, 4, 2 + b, nsa_ready)
                released(evac_merge(1)(p, o, b, 2 + b), 4 + 2 * b, 5 + 2 * b)

        phase("mla")
        gq = sm[:, S1["mq"][0]:S1["mkv"][1]]
        c_hi, c_lo = nT_hi[:, 0:5, :], tT_lo[:, 4:9, :]
        for e in to_parts(lambda c, t: z[:, t, Z_CQ + c * P:Z_CQ + (c + 1) * P], 5, c_hi, c_lo, (), gq):
            pass
        rstd([z[:, t, Z_CQ:Z_CQ + Q_RANK] for t in range(TT)], Q_RANK, 4, ())
        core.last["rstd"] = (rstd([z[:, t, Z_CKV:Z_CKV + KV_RANK] for t in range(TT)], KV_RANK, 6, ()),)
        QN, QP, KN, VN = 3072, 3584, 4096, 4608
        q_done = []
        for pair, (width, at) in enumerate(((512, QN), (256, QP))):
            PE.wait(free(2 * pair, 2 * pair + 1))
            for k in range(3):
                if k * width % HALF == 0:
                    w_hi, w_lo = next_half()
                PE.wait(e[k])
                o_ = k * width % HALF
                for t in range(TT):
                    tok = slice(t * P, (t + 1) * P)
                    m = three(ps[:, 2 * pair + t, 0:width], c_hi[:, k, tok], c_lo[:, k, tok], w_hi[:, o_:o_ + width], w_lo[:, o_:o_ + width],
                              k == 0, k == 2)
                if (k + 1) * width % HALF == 0:
                    PE.do(m, used)
            p = PE.do(m, used)
            v = scaled(V, p, z[:, :, at:at + width], ps[:, 2 * pair:2 * pair + 2, 0:width], 4)
            q_done.append(v)
            released(v, 2 * pair, 2 * pair + 1)
        next_half()
        PE.wait(free(7))
        PE.do(PE.e.matmul(ps[:, 7, 0:1], ident, ident[:, 0:1], start=True, stop=True), used)
        PE.wait(free(4, 5, 0, 1), e[4])
        for k in range(2):
            w_hi, w_lo = next_half()
            for hf, b in ((0, 4), (1, 0)):
                for t in range(TT):
                    tok, cols = slice(t * P, (t + 1) * P), slice(hf * BLK, (hf + 1) * BLK)
                    m = three(ps[:, b + t, :], c_hi[:, 3 + k, tok], c_lo[:, 3 + k, tok], w_hi[:, cols], w_lo[:, cols], k == 0, k == 1)
            p = PE.do(m, used)
        k_done = scaled(A, (p, PE.now), z[:, :, KN:KN + 512], ps[:, 4:6, :], 6)
        released(k_done, 4, 5)
        v_done = scaled(A, p, z[:, :, VN:VN + 512], ps[:, 0:2, :], 6)
        released(v_done, 0, 1)
        V.do(V.wait(V.now).tensor_copy(z[:, :, QP + 256:QP + 320], z[:, :, Z_KR:Z_KR + 64]))
        rot = tT[:, 16:19, :].rearrange("p a b -> p (a b)").rearrange("p (t h r) -> p t h r", t=TT, h=6)
        tmp = tT[:, 19:21, :].rearrange("p a b -> p (a b)")[:, 0:320].rearrange("p (h f) -> p h f", h=10)
        for t in range(TT):
            src = z[:, t, QP:QP + 320].rearrange("p (h r) -> p h r", h=5)
            x1, x2 = src[:, :, 0:32], src[:, :, 32:64]
            cos, sin = mid(rope[:, 0, t, :], 5), mid(rope[:, 1, t, :], 5)
            y1, y2, t1, t2 = rot[:, t, 0:5, 0:32], rot[:, t, 0:5, 32:64], tmp[:, 0:5, :], tmp[:, 5:10, :]
            V.do(V.chain().tensor_tensor(y1, x1, cos, ALU.mult))
            V.do(V.e.tensor_tensor(t1, x2, sin, ALU.mult))
            V.do(V.e.tensor_tensor(y2, x2, cos, ALU.mult))
            V.do(V.e.tensor_tensor(t2, x1, sin, ALU.mult))
            V.do(V.chain().tensor_tensor(y1, y1, t1, ALU.subtract))
            V.do(V.e.tensor_tensor(y2, y2, t2, ALU.add))
            V.do(V.chain().tensor_copy(rot[:, t, 5, :], rot[:, t, 4, :]))
        e1 = to_T(lambda c, t: z[:, t, QN + c * P:QN + (c + 1) * P], 4, tT, ready=q_done[0])
        kT = tT[:, 9:13, :]
        e2 = to_T(lambda c, t: z[:, t, KN + c * P:KN + (c + 1) * P], 4, kT, ready=k_done)
        e3 = to_T(lambda c, t: rot[:, t, 2 * c:2 * c + 2, :].rearrange("p h r -> p (h r)"), 2, tT[:, 13:15, :], ready=V.now)

        def evac_kp(p, o, c, k):
            A.do(A.wait(p, kpz_zeroed).copy(kpz[0:64, 0, :], o[0:64, 0, :]))
            return A.do(A.e.copy(kpz[64:128, 1, :], o[64:128, 0, :]))
        e4 = to_T(lambda c, t: rot[:, t, 4:6, :].rearrange("p h r -> p (h r)"), 1, None, evac_kp, V.now)
        units = []
        for t in range(TT):
            def scores(o, t=t):
                for h in range(4):
                    PE.e.matmul(o[:, h, :], tT[:, h, t * P:(t + 1) * P], kT[:, h, :], start=True, stop=False)
                    m = PE.e.matmul(o[:, h, :], tT[:, 13 + h // 2, t * P:(t + 1) * P], kpz[:, h % 2, :], start=False, stop=True)
                return m
            off = P * (1 - t)
            units.append(dict(scores=scores, scale=192.0 ** -0.5, add=mid(mask[:, off:off + T], 4), dv=P, ready=(e1, e2, e3, e4, v_done),
                              value=lambda h, kt: z[:, kt, VN + h * P:VN + (h + 1) * P],
                              out=plain_out(ostage[:, t, :].rearrange("p (h d) -> p h d", h=4))))
        attention(units, {"first": nsa_product})
        gemm(four, 4, 2, evac_merge(2), heads_parts(V.now))
        phase("w_out")
        for e in to_parts(lambda c, t: merged[:, t, c * P:(c + 1) * P], KT, nT_hi, nT_lo, merged_at[-2:]):
            pass
        mrows = z[:, :, 0:D]
        A.wait(V.now, PE.now, G.now)
        A.e.dma_start(mrows, io["mem"]).then_inc(mem_count.h, 16)
        l_mem = mem_count.add(16)
        gemm(nT_parts, KT, 1, add_x, e)
        m_hi = Parts()
        n = norm_parts(mrows, s1("mem"), (l_mem, V.now), at=10, hi=m_hi, lo=tT_lo)
        gemm(nT_parts, KT, 1, add_x, first=1)

        phase("xattn")
        XK, XV, XQ = 0, 512, 1024
        x_done = V.now

        def evac_to(at, factors):
            def evac(p, o, b, pair):
                return scaled(A, (p, V.now), z[:, :, at + b * BLK:at + (b + 1) * BLK], o, factors)
            return evac
        gemm((m_hi, tT_lo), KT, 1, evac_to(XK, 10), n)
        n = norm_parts(x[:, :, :], s1("xattn"), x_done)
        gemm(nT_parts, KT, 1, evac_to(XQ, 8), n)

        def memory_values():
            p, o = gemm_block((m_hi, tT_lo), KT, 3, ())
            v_ready.append(evac_to(XV, 10)(p, o, 0, 3))
            released(v_ready[0], 6, 7)
        v_ready = []
        kT = tT[:, 12:16, :]
        xqT = tT[:, 8:12, :]
        e1 = to_T(lambda c, t: z[:, t, XQ + c * P:XQ + (c + 1) * P], 4, xqT, ready=A.now)
        e2 = to_T(lambda c, t: z[:, t, XK + c * P:XK + (c + 1) * P], 4, kT, ready=A.now)
        units = []
        for t in range(TT):
            def scores(o, t=t):
                for h in range(4):
                    m = PE.e.matmul(o[:, h, :], xqT[:, h, t * P:(t + 1) * P], kT[:, h, :], start=True, stop=True)
                return m
            units.append(dict(scores=scores, scale=P ** -0.5, add=None, dv=P, ready=(e1, e2), values=v_ready,
                              value=lambda h, kt: z[:, kt, XV + h * P:XV + (h + 1) * P],
                              out=plain_out(ostage[:, t, :].rearrange("p (h d) -> p h d", h=4))))
        attention(units, {"first": memory_values})
        halves_at = []
        gemm(four, 4, 2, lambda *a: halves_at.append(add_x(*a)) or halves_at[-1], heads_parts(V.now))
        phase("ffn")
        n = norm_parts(x[:, :, :], s1("ffn"), halves_at)
        A.wait(V.now)
        A.e.dma_start(sm[:, :], io["smalls"][ds(layer + 1, 1), :, :].rearrange("a p n -> p (a n)")).then_inc(sm_count.h, 16)
        sm_count.add(16)
        p = ffn_down(ffn_up(n))
        for hf in range(2):
            released(add_x(p, ps[:, hf:4:2, :], hf, 0), hf, hf + 2)
        PE.wait(free(7))
        for _ in range(2):
            for _ in range(2):
                next_half()
                p = PE.do(PE.e.matmul(ps[:, 7, 0:1], ident, ident[:, 0:1], start=True, stop=True), used)

    wk = cbuf[:, 0:384].rearrange("p (a b) -> p a b", a=12)
    def post_norm(factor, i, p):
        h = [ps[:, 2 * t:2 * t + 2, :] for t in range(TT)]
        before = V.now
        squares = [A.do(A.wait(p, before, A.now).activation(ostage[:, :, :], h[t], ACT.Square, accum_out=st[:, t:t + 1])) for t in range(TT)]

        def weighted(t):
            return V.do(V.wait(squares[t], p, loading["gain"], PE.now).tensor_tensor(
                xn[:, t, :].rearrange("p (a n) -> p a n", a=2), h[t], gain.rearrange("p (a n) -> p a n", a=2), ALU.mult))
        weighted(0)
        r = V.do(V.wait(squares[1], G.now).tensor_scalar(st[:, 0:TT], st[:, 0:TT], factor ** -2 / D, factor ** -2 * EPS, ALU.mult, ALU.add))
        ready = weighted(1)
        r = G.do(G.wait(r).tensor_tensor(st[:, 0:TT], st[:, 0:TT], half[:, 0:TT], ALU.pow))
        if i + 1 < N_GAIN:
            load_gain(i + 1)
        out = []
        for hf in range(2):
            cols = slice(hf * BLK, (hf + 1) * BLK)
            for t in range(TT):
                v = V.do(V.wait(r, ready).scalar_tensor_tensor(x[:, t, cols], xn[:, t, cols], st[:, t:t + 1], x[:, t, cols], ALU.mult, ALU.add))
            out.append(v)
        released(out[0], 0, 1, 2, 3)
        return out

    def two_blocks(lhs, kts, ready, beside=None):
        ends = []
        gemm(lhs, kts, 2, lambda p, o, b, pair: ends.append(p) or p, ready, beside=beside, by_row=True)
        return ends[1]

    def ffn2(pre, post, ready):
        n = norm_parts(x[:, :, :], s2("pre", 8 * pre, 8 * pre + 8), ready)
        return post_norm(0.5, post, ffn_down(ffn_up(n)))

    def softplus(out, src, k, tmp):
        m, e, zz, z2 = (tmp[:, i, 0:k] for i in range(4))
        V.do(V.chain().tensor_scalar(m, src, 0.0, None, ALU.max))
        V.do(V.chain().scalar_tensor_tensor(e, src, -1.0, src, ALU.mult, ALU.max))
        a = A.do(A.wait(V.now).activation(e, e, ACT.Exp, scale=-1.0))
        V.do(V.wait(a).tensor_scalar(zz, e, 2.0, None, ALU.add))
        V.do(V.chain().reciprocal(zz, zz))
        V.do(V.chain().tensor_tensor(zz, zz, e, ALU.mult))
        V.do(V.chain().tensor_tensor(z2, zz, zz, ALU.mult))
        V.do(V.chain().tensor_scalar(e, z2, 1.0 / 15, None, ALU.mult))
        for c in (13, 11, 9, 7, 5, 3):
            V.do(V.chain().scalar_tensor_tensor(e, e, 1.0 / c, z2, ALU.add, ALU.mult))
        V.do(V.chain().scalar_tensor_tensor(e, e, 1.0, zz, ALU.add, ALU.mult))
        return V.do(V.chain().scalar_tensor_tensor(out, e, 2.0, m, ALU.mult, ALU.add))

    def conv_tile(c, left, w, b, dst):
        src, out = left[:, ds(c, 1), :], dst[:, ds(c, 1), :]
        a = A.do(A.wait(cin_ready).activation(out, src[:, :, 0:T], ACT.Identity, scale=w[:, ds(c * 4, 1)], bias=b[:, ds(c, 1)]))
        for k in range(1, 4):
            V.do(V.wait(a, V.now).scalar_tensor_tensor(out, src[:, :, k:k + T], w[:, ds(c * 4 + k, 1)], out, ALU.mult, ALU.add))

    for e in core.engines:
        e.wait(l_sm2)
    phase("ffn_a")
    r = rstd([x[:, t, :] for t in range(TT)], D, 0, V.now)
    start_run(3 * 66 + 46 + 16 + 16)
    x_ready = []
    for hf in range(2):
        cols = slice(hf * BLK, (hf + 1) * BLK)
        for t in range(TT):
            v = V.do(V.wait(r, loading["gain"]).scalar_tensor_tensor(x[:, t, cols], x[:, t, cols], st[:, t:t + 1], gain[:, cols], ALU.mult, ALU.mult))
        x_ready.append(v)
    load_gain(1)
    x_ready = ffn2(0, 1, x_ready)

    phase("hyb_in")
    cin = big[:, 0:12 * (T + 3)].rearrange("p (c n) -> p c n", c=12)
    m0 = G.do(G.wait(PE.now, V.now).memset(cin[:, :, 0:3], 0.0))
    n = norm_parts(x[:, :, :], s2("pre", 8, 16), x_ready)
    H_X, H_Q, H_K, H_V = 1024, 2560, 3584, 4608

    def evac_hyb(p, o, b, pair):
        return scaled(A, p, block_of(z, b), o)
    gemm(nT_parts, KT, 3, evac_hyb, n, first=2)
    xbc_done = (V.now, A.now)
    PE.wait(free(4, 5))
    w_hi, w_lo = next_half()
    for t in range(TT):
        for k in range(KT):
            tok, cols = slice(t * P, (t + 1) * P), slice(k * 24, (k + 1) * 24)
            m = three(ps[:, 4 + t, 0:24], nT_hi[:, k, tok], nT_lo[:, k, tok], w_hi[:, cols], w_lo[:, cols], k == 0, k == KT - 1)
    p = PE.do(m, used)
    next_half()
    PE.wait(free(7))
    PE.do(PE.e.matmul(ps[:, 7, 0:1], ident, ident[:, 0:1], start=True, stop=True), used)

    def evac_cin(p, o, c, k):
        return A.do(A.wait(p, m0).copy(cin[:, c:c + k, 3:3 + T], o))
    e = to_T(lambda c, t: z[:, t, H_X + c * P:H_X + (c + 1) * P], 12, None, evac_cin, xbc_done)
    dtb, fbb = mid(s2("dtb"), TT), mid(s2("fb"), TT)
    dt, dA, lam = wk[:, 2:4, 0:16], wk[:, 4:6, 0:16], wk[:, 10, 0:8]
    raw, sp = (b[:, 0:56] for b in (cbuf[:, 0:64], acc[:, 0, :]))
    raw2, sp2 = (b[:, 0:48].rearrange("p (t n) -> p t n", t=TT) for b in (raw, sp))
    for t in range(TT):
        r_ = st[:, 8 + t:9 + t]
        V.do(V.wait(p, last_of("rstd")).scalar_tensor_tensor(raw2[:, t, 0:16], ps[:, 4 + t, 0:16], r_, dtb[:, t, :], ALU.mult, ALU.add))
        V.do(V.e.scalar_tensor_tensor(raw2[:, t, 16:24], ps[:, 4 + t, 16:24], r_, fbb[:, t, :], ALU.mult, ALU.add))
    released(V.now[0], 4, 5)
    V.do(V.chain().tensor_scalar(raw2[:, :, 16:24], raw2[:, :, 16:24], -1.0, None, ALU.mult))
    V.do(V.e.tensor_scalar(raw[:, 48:56], s2("lam"), -1.0, None, ALU.mult))
    softplus(sp, raw, 56, acc[:, 2:6, :])
    lam_ready = V.do(V.chain().tensor_scalar(lam, sp[:, 48:56], -8.0, None, ALU.mult))
    a_neg = wk[:, 6, 0:16]
    p = A.do(A.wait(V.now).activation(a_neg, s2("alog"), ACT.Exp))
    V.do(V.wait(p, V.now).tensor_scalar(a_neg, a_neg, -1.0, None, ALU.mult))
    V.do(V.chain().tensor_copy(dt, sp2[:, :, 0:16]))
    V.do(V.chain().tensor_tensor(dA, dt, mid(a_neg, TT), ALU.mult))
    lf = wk[:, 7:9, 0:8]
    V.do(V.e.tensor_scalar(lf, sp2[:, :, 16:24], -1.0, None, ALU.mult))
    negf = wk[:, 7:9, 8:16]
    V.do(V.e.tensor_copy(negf, sp2[:, :, 16:24]))
    sums_ready = V.now
    xbcT = tT[:, 0:12, :]
    cin_ready = (e, m0, PE.now)
    V.wait(cin_ready)
    with core.loop(2) as i:
        for j in range(2):
            p, o = gemm_block(nT_parts, KT, j, (), lambda n_: conv_tile(i * 6 + n_ - n_ // 4, cin, s2("cw"), s2("cb"), xbcT) if n_ % 4 < 3 else None, 4 * j)
            released(evac_hyb(p, o, i * 5 + j, j), 2 * j, 2 * j + 1)
    run["left"] -= 8
    silu_ready = A.do(A.wait(V.now).activation(xbcT, xbcT, ACT.Silu))
    for t in range(TT):
        z_silu = A.do(A.wait(A.now).activation(z[:, t, 0:D], z[:, t, 0:D], ACT.Silu))
    Sf = S[:, :, :, :].rearrange("p a b c -> p (a b c)").rearrange("p (h l) -> p h l", h=16)
    LT = [PTs[:, :, :, :].rearrange("p a b c -> p (a b) c"), big[:, 0:2048].rearrange("p (h l) -> p h l", h=16)]
    Xd = big[:, 2048:3072]
    X = xn
    S0, cbs = acc[:, 0:4, :].rearrange("p a b -> p (a b)"), acc[:, 4:6, :].rearrange("p a (g l) -> p (a g) l", g=2)
    BT, CT = tT[:, 8:10, :], tT[:, 10:12, :]
    xt = [z[:, t, H_X:H_X + D] for t in range(TT)]
    ssd = {}
    up = c_("upper")
    tri = up[:, P:2 * P]
    cs = cbuf[:, 384:432]
    acs, cumq = cs[:, 0:32].rearrange("p (t h) -> p t h", t=TT), cs[:, 32:48].rearrange("p (t h) -> p t h", t=TT)
    eacs = wk[:, 9, 0:16]

    def heads(a, n=16):
        return a.rearrange("p (h d) -> p h d", h=n)

    def sums():
        PE.wait(sums_ready, free(6))
        for t in range(TT):
            PE.e.matmul(ps[:, 6, 16 * t:16 * t + 16], tri, dA[:, t, :], start=True, stop=True)
        PE.e.matmul(ps[:, 6, 32:40], tri, lf[:, 0, :], start=True, stop=True)
        PE.e.matmul(ps[:, 6, 40:48], c_("ones"), lf[:, 0, :], start=True, stop=False)
        p = PE.do(PE.e.matmul(ps[:, 6, 40:48], tri, lf[:, 1, :], start=False, stop=True))
        ssd["acs"] = V.do(V.wait(p).tensor_copy(cs, ps[:, 6, 0:48]))
        released(ssd["acs"], 6)
        A.do(A.wait(V.now).activation(eacs, acs[:, 1, :], ACT.Exp))

    def to_rows(t):
        for q, (first, n_) in enumerate(((0, 4), (4, 4), (8, 2))):
            b = 6 + bank_turn[0] % 2
            bank_turn[0] += 1
            PE.wait(free(b), silu_ready)
            for i in range(n_):
                m = PE.e.transpose(ps[:, b, i * P:(i + 1) * P], tT[:, first + i, t * P:(t + 1) * P], ident)
            p = PE.do(m)
            ssd["rows", t, q] = A.do(A.wait(p).copy(z[:, t, H_X + first * P:H_X + (first + n_) * P], ps[:, b, 0:n_ * P]))
            released(ssd["rows", t, q], b)

    def triangle(t):
        ssd["Sf", t] = V.do(V.wait(last_of("Sf"), PE.now).tensor_tensor(Sf, bc(dA[:, t, :], P), mid(tri, 16), ALU.mult))

    def steps(t):
        ssd["X", t] = G.do(G.wait(ssd["rows", t, 1], ssd["rows", t, 2], ssd["acs"], PE.now).tensor_tensor(heads(X[:, t, :]), heads(xt[t]), bc(dt[:, t, :], 64), ALU.mult))
        ssd["dx", t] = G.do(G.wait(G.now).tensor_tensor(heads(xt[t]), heads(xt[t]), bc(s2("dskip"), 64), ALU.mult))

    def row_sums(t):
        PE.wait(ssd["Sf", t], free(4, 5, 6, 7))
        for b in range(4):
            m = PE.e.matmul(ps[:, 4 + b, :], c_("ones"), Sf[:, 4 * b:4 * b + 4, :].rearrange("p h l -> p (h l)"), start=True, stop=True)
        ssd["sums", t] = PE.do(m)
        core.last["Sf"] = (ssd["sums", t],)

    def segments(t):
        v = V.do(V.wait(ssd["sums", t], ssd["acs"]).tensor_tensor(LT[t], ps[:, 4:8, :].rearrange("p a (b l) -> p (a b) l", b=4), bc(acs[:, t, :], P), ALU.subtract))
        released(v, 4, 5, 6, 7)

    def decays(t):
        v = V.do(V.chain().tensor_tensor(LT[t], LT[t], mid(c_("maskU"), 16), ALU.add))
        ssd["L", t] = A.do(A.wait(v).activation(LT[t], LT[t], ACT.Exp))

    def products():
        PE.wait(free(4))
        for t in range(TT):
            for g in range(2):
                m = PE.e.matmul(ps[:, 4, (2 * t + g) * P:(2 * t + g + 1) * P], BT[:, g, t * P:(t + 1) * P], CT[:, g, t * P:(t + 1) * P], start=True, stop=True)
        p = PE.do(m)
        ssd["cb"] = A.do(A.wait(p, V.now).copy(cbs, ps[:, 4, :].rearrange("p (a l) -> p a l", a=4)))
        released(ssd["cb"], 4)

    def to_end():
        ssd["Xd"] = V.do(V.wait(ssd["L", 0], ssd["X", 0]).tensor_tensor(heads(Xd), heads(X[:, 0, :]), LT[0][:, :, P - 1:P].to_broadcast([P, 16, 64]), ALU.mult))

    def weigh(t):
        for g in range(2):
            ssd["W", t] = V.do(V.wait(ssd["cb"], ssd["L", t], V.now).tensor_tensor(LT[t][:, 8 * g:8 * g + 8, :], LT[t][:, 8 * g:8 * g + 8, :],
                                                                             mid(cbs[:, 2 * t + g, :], 8), ALU.mult))

    R = [[tT[:, 12 + 4 * t:16 + 4 * t, :] for t in range(TT)], [xt[t].rearrange("p (h k) -> p h k", h=4) for t in range(TT)]]

    terms = [S, big[:, 0:2048].rearrange("p (i h k) -> p i h k", i=TT, h=4)]

    def key_terms(hg):
        for i in range(TT):
            v = V.do(V.wait(last_of("Sf"), PE.now).tensor_tensor(terms[hg][:, i], bc(negf[:, i, 4 * hg:4 * hg + 4], T), mid(up[:, P * (1 - i):P * (1 - i) + T], 4), ALU.mult))
        ssd["terms", hg] = v

    def key_sums(hg):
        PE.wait(ssd["terms", hg], free(4, 5))
        for b in range(2):
            for i in range(TT):
                m = PE.e.matmul(ps[:, 4 + b, :], c_("ones"), terms[hg][:, i, 2 * b:2 * b + 2, :].rearrange("p h k -> p (h k)"), start=(i == 0), stop=(i == 1))
        ssd["keys", hg] = PE.do(m)
        core.last["Sf"] = (ssd["keys", hg],)

    def added(hg):
        V.wait(ssd["keys", hg], V.now)
        for t in range(TT):
            for h in range(4):
                c = cumq[:, t, 4 * hg + h:4 * hg + h + 1]
                v = V.do(V.e.scalar_tensor_tensor(R[hg][t][:, h, :], ps[:, 4 + h // 2, h % 2 * T:(h % 2 + 1) * T], c, mask[:, P * (1 - t):P * (1 - t) + T], ALU.add, ALU.add))
        released(v, 4, 5)

    QT, KTs = [nT[:, 0:4, :], tT[:, 8:12, :]], [nT[:, 4:8, :], acc[:, 0:4, :]]

    def queries_keys(hg):
        e = ()
        for at, dst in ((H_Q, QT[hg]), (H_K, KTs[hg])):
            e += to_T(lambda c, t: z[:, t, at + (4 * hg + c) * P:at + (4 * hg + c + 1) * P], 4, None,
                      lambda p, o, c, k: A.do(A.wait(p).copy(dst[:, c:c + k, :], o)), (V.now, A.now))
        ssd["qk", hg] = e

    work = [lambda: (sums(), triangle(0)), lambda: None, lambda: to_rows(0), lambda: row_sums(0), lambda: segments(0),
            lambda: (decays(0), to_rows(1)), lambda: triangle(1), lambda: (products(), steps(0)), lambda: (row_sums(1), to_end()),
            lambda: segments(1), lambda: decays(1), lambda: (weigh(0), steps(1)), lambda: weigh(1), lambda: key_terms(0),
            lambda: None, lambda: key_sums(0)]
    for b in (0, 2):
        gemm(nT_parts, KT, 2, evac_hyb, first=7 + b, beside=lambda n_, b=b: work[4 * b + n_]())
    phase("ssd")
    added(0)
    y_banks = ((5, 6), (4, 7))

    def within(t):
        PE.wait(ssd["W", t], ssd["X", t], free(*y_banks[t]))
        for h in range(16):
            m = PE.e.matmul(ps[:, y_banks[t][h // 8], h % 8 * 64:(h % 8 + 1) * 64], LT[t][:, h, :], X[:, t, h * 64:(h + 1) * 64], start=True, stop=True)
        p = PE.do(m)
        for g in range(2):
            v = V.do(V.wait(p, V.now, ssd["dx", t]).tensor_tensor(xt[t][:, g * 512:(g + 1) * 512], xt[t][:, g * 512:(g + 1) * 512], ps[:, y_banks[t][g], :], ALU.add))
            released(v, y_banks[t][g])
    PE.wait(ssd["Xd"], ssd["rows", 0, 2], free(0, 1))
    for g in range(2):
        m = PE.e.matmul(ps[:, g, :], z[:, 0, H_X + D + g * P:H_X + D + (g + 1) * P], Xd[:, g * 512:(g + 1) * 512], start=True, stop=True)
    p = PE.do(m)
    s0_ready = A.do(A.wait(p).copy(S0, ps[:, 0:2, :].rearrange("p a b -> p (a b)")))
    released(s0_ready, 0, 1)
    within(0)
    V.do(V.wait(z_silu, V.now).tensor_tensor(z[:, 0, 0:D], z[:, 0, 0:D], xt[0], ALU.mult))
    PE.wait(s0_ready, free(2, 3))
    for g in range(2):
        m = PE.e.matmul(ps[:, 2 + g, :], CT[:, g, P:2 * P], S0[:, g * 512:(g + 1) * 512], start=True, stop=True)
    p = PE.do(m)
    yo = PTs[:, 0, :, :].rearrange("p a b -> p (a b)")
    V.do(V.wait(p).tensor_tensor(heads(yo), ps[:, 2:4, :].rearrange("p a (h d) -> p (a h) d", h=8), bc(eacs, 64), ALU.mult))
    released(V.now[0], 2, 3)
    V.do(V.wait(V.now, ssd["dx", 1]).tensor_tensor(xt[1], xt[1], yo, ALU.add))
    within(1)
    V.do(V.wait(V.now).tensor_tensor(z[:, 1, 0:D], z[:, 1, 0:D], xt[1], ALU.mult))
    phase("fox")
    for hg in range(2):
        queries_keys(hg)
    key_terms(1)
    key_sums(1)
    out_ready = [None] * 16

    def y_norm():
        added(1)
        groups = [z[:, t, g * 512:(g + 1) * 512] for t in range(TT) for g in range(2)]
        r = rstd(groups, 512, 0, V.now)
        for i, s in enumerate(groups):
            V.do(V.wait(r).tensor_scalar(s, s, st[:, i:i + 1], None, ALU.mult))
        ssd["y"] = V.now

    def y_parts():
        for points in to_parts(lambda c, t: z[:, t, c * P:(c + 1) * P], 8, nT_hi, tT_lo, ssd["y"], s2("ng")):
            out_ready[0:len(points)] = points

    for nm in ("S0", "S1", "rs0", "rs1", "PT0", "PT1"):
        core.last[nm] = V.now + A.now + PE.now
    units = []
    heads_out = [[ostage[:, t, :] for t in range(TT)], [z[:, t, H_Q:H_Q + 512] for t in range(TT)]]
    for hg in range(2):
        for t in range(TT):
            def scores(o, t=t, hg=hg):
                for h in range(4):
                    m = PE.e.matmul(o[:, h, :], QT[hg][:, h, t * P:(t + 1) * P], KTs[hg][:, h, :], start=True, stop=True)
                return m
            units.append(dict(scores=scores, scale=P ** -0.5, add=R[hg][t], dv=P, ready=(V.now, lambda hg=hg: ssd["qk", hg]),
                              value=lambda h, kt, hg=hg: z[:, kt, H_V + (4 * hg + h) * P:H_V + (4 * hg + h + 1) * P],
                              out=plain_out(heads(heads_out[hg][t], 4))))
    attention(units, {"first": y_norm, 1: y_parts})
    heads_done = V.now

    def heads_beside(n_):
        if n_ == 2:
            for points in to_parts(lambda c, t: heads_out[c // 4][t][:, c % 4 * P:(c % 4 + 1) * P], 8, xn_hi, tT_lo[:, 8:16, :], heads_done):
                out_ready[8:8 + len(points)] = points
    phase("hyb_out")
    x_ready = post_norm(1.0, 2, two_blocks((Joined(nT_hi, xn_hi, 8), tT_lo), 16, out_ready, heads_beside))
    phase("ffn_bc")
    x_ready = ffn2(2, 3, x_ready)
    x_ready = ffn2(3, 4, x_ready)

    phase("rec")
    cin = big[:, 0:8 * (T + 3)].rearrange("p (c n) -> p c n", c=8)
    m0 = G.do(G.wait(PE.now, V.now).memset(cin[:, :, 0:3], 0.0))
    n = norm_parts(x[:, :, :], s2("pre", 32, 40), x_ready)
    gemm(nT_parts, KT, 2, evac_hyb, n, first=2)
    e = to_T(lambda c, t: z[:, t, D + c * P:D + (c + 1) * P], 8, None, evac_cin, (V.now, A.now))
    xT, rT = tT[:, 0:8, :], tT[:, 8:16, :]
    cin_ready = (e, m0, PE.now)
    V.wait(cin_ready)

    def conv_rec(n_):
        for k in range(4):
            src, w_ = cin[:, n_, k:k + T], s2("rw")[:, 4 * n_ + k:4 * n_ + k + 1]
            if k == 0:
                a = A.do(A.wait(cin_ready).activation(xT[:, n_, :], src, ACT.Identity, scale=w_, bias=s2("rb")[:, n_:n_ + 1]))
            else:
                V.do(V.wait(a, V.now).scalar_tensor_tensor(xT[:, n_, :], src, w_, xT[:, n_, :], ALU.mult, ALU.add))
    gemm(nT_parts, KT, 2, evac_hyb, beside=conv_rec)
    gate_ready = A.now

    def zbuf(t, i):
        return z[:, t, 2048 * (1 + i):2048 * (2 + i)].rearrange("p (c n) -> p c n", c=8)
    aT, th, iT, gT = zbuf(0, 0), zbuf(0, 1), zbuf(1, 0), zbuf(1, 1)
    def evac_g(p, o, c, k):
        return A.do(A.wait(p).activation(gT[:, c:c + k, :], o, ACT.Gelu_apprx_tanh))
    to_T(lambda c, t: z[:, t, c * P:(c + 1) * P], 8, None, evac_g, gate_ready)
    gelu_ready = A.now
    w = chunk()
    PE.wait(V.now, free(0, 1, 2, 3, 4, 5, 6, 7))
    gates_at = []
    for j in range(16):
        m = PE.e.matmul(ps[:, j // 2, j % 2 * T:(j % 2 + 1) * T], w[:, j * P:(j + 1) * P], xT[:, j % 8, :], start=True, stop=True)
        if j % 8 == 7:
            gates_at.append(PE.do(m, used))
    for j in range(16):
        dst, bias = (rT, s2("ba", j, j + 1)) if j < 8 else (iT, s2("bx", j - 8, j - 7))
        a = A.do(A.wait(gates_at[j // 8]).activation(dst[:, j % 8, :], ps[:, j // 2, j % 2 * T:(j % 2 + 1) * T], ACT.Sigmoid, bias=bias))
        released(a, j // 2)
        if j == 7:
            r_ready = a
    i_ready = a
    parts = [slice(0, 4), slice(4, 8)]
    V.wait(r_ready, lam_ready)
    for k in parts:
        p = V.do(V.e.tensor_tensor(rT[:, k, :], rT[:, k, :], bc(lam[:, k], T), ALU.mult))
        A.do(A.wait(p).activation(aT[:, k, :], rT[:, k, :], ACT.Exp))
        A.do(A.e.activation(th[:, k, :], rT[:, k, :], ACT.Tanh))
    tanh_ready = A.now
    V.do(V.wait(i_ready).tensor_tensor(iT, iT, xT, ALU.mult))
    start_run(8 + 66)
    roots = []
    for k in parts:
        V.do(V.wait(tanh_ready, V.now).tensor_tensor(rT[:, k, :], aT[:, k, :], aT[:, k, :], ALU.mult))
        V.do(V.chain().scalar_tensor_tensor(th[:, k, :], rT[:, k, :], 1.0, th[:, k, :], ALU.add, ALU.mult))
        roots.append(A.do(A.wait(V.now).activation(th[:, k, :], th[:, k, :], ACT.Sqrt, scale=-1.0)))
    h_ready = []
    for k, root in zip(parts, roots):
        V.do(V.wait(root, V.now).tensor_tensor(iT[:, k, :], iT[:, k, :], th[:, k, :], ALU.mult))
        V.wait(V.now)
        for c in range(k.start, k.stop):
            V.do(V.e.tensor_tensor_scan(rT[:, c, :], aT[:, c, :], iT[:, c, :], 0.0, ALU.mult, ALU.add))
        p = V.do(V.wait(V.now, gelu_ready).tensor_tensor(nT[:, k, :], rT[:, k, :], gT[:, k, :], ALU.mult))
        a = A.do(A.wait(p).copy(nT_hi[:, k, :], nT[:, k, :]))
        h_ready += [V.do(V.wait(a).tensor_tensor(nT_lo[:, k, :], nT[:, k, :], nT_hi[:, k, :].bitcast(F32), ALU.subtract))] * 4
    x_ready = post_norm(1.0, 5, two_blocks(nT_parts, KT, h_ready))
    phase("ffn_d")
    ffn2(5, 6, x_ready)
    phase(None)
    for t in range(TT):
        p = load(A, io["out"][:, t, :], x[:, t, :], V.now, G.now)
        A.wait(p)
    core.meet()
    return core.seen


def t5_bucket(dist):
    f = np.float32
    ratio = np.log(np.maximum(dist, 1).astype(f) / f(16)) / f(log(8))
    return np.where(dist < 16, dist, np.minimum(16 + (ratio * f(16)).astype(np.int32), 31))


def constants():
    c = np.zeros((P, CC_W), np.float32)

    def put(name, a):
        c[:, CC[name][0]:CC[name][1]] = a
    p, n = np.arange(P)[:, None], np.arange(BAND)[None, :]
    put("ident", np.eye(P))
    put("ones", 1.0)
    put("upper", n - P >= p)
    put("maskU", np.where(n[:, :P] >= p, 0.0, NEG))
    put("mask", np.where(p + P - n >= 0, 0.0, NEG))
    put("freq", (np.float32(10000.0) ** (-np.arange(32, dtype=np.float32) / np.float32(32)))[None, :])
    put("valid", np.stack([(np.arange(P) >= 31), np.ones(P)], 1))
    hot = np.zeros((33, BLK), np.float32)
    d = 255 - np.arange(BLK)
    hot[t5_bucket(np.maximum(d, 0))[:256], np.arange(256)] = 1.0
    hot[32, 256:] = NEG
    return c, hot


def rows(a):
    return np.ascontiguousarray(a.reshape(TT, P, -1).transpose(1, 0, 2))


def feat(a):
    return a.reshape(-1, P).T


def layout(v):
    chunks = []

    def put(a):
        a = a.transpose(1, 0, 2).reshape(P, -1)
        c = np.zeros((P, CHUNK), np.float32)
        c[:, :a.shape[1]] = a
        chunks.append(c)

    def blocks(w):
        k, n = w.shape
        for b in range(0, n, BLK):
            part = np.zeros((k, BLK), np.float32)
            part[:, :min(BLK, n - b)] = w[:, b:b + BLK]
            for c in range(0, k, 4 * P):
                put(part[c:c + 4 * P].reshape(4, P, BLK))

    def ffn(w_in, w_out):
        gu = np.concatenate([w_in[:, :FF].reshape(D, GU, 256), w_in[:, FF:].reshape(D, GU, 256)], 2)
        blocks(gu.reshape(D, GU * BLK))
        for c in range(FT // 2):
            put(w_out[2 * c * P:(2 * c + 2) * P].reshape(2, P, D))

    smalls = np.zeros((DEPTH + 1, P, S1_W), np.float32)
    for l in range(DEPTH):
        def small(name, a):
            smalls[l, :, S1[name][0]:S1[name][1]] = a
        w = v["w_in"][l]
        at = np.cumsum([0, 1024, 512, 768, 24, 384, 256, 64, 3072])
        glu, q, kv, gn, cq, ckv, kr, gm = (w[:, a:b] for a, b in zip(at, at[1:]))
        q = q.reshape(D, 2, 4, 64).transpose(0, 2, 1, 3).reshape(D, 512)
        gn = gn.reshape(D, 2, 4, 3).transpose(0, 3, 2, 1).reshape(D, 24)
        blocks(np.concatenate([glu[:, 512:], glu[:, :512], gm, q, kv, cq, ckv, kr, gn], 1))
        for n in "kv":
            w1 = v["cmp_w1_" + n][l].reshape(2, 8, P, 256)
            put(w1[0])
            put(w1[1])
        blocks(v["w_branch_conv"][l])
        uq = v["w_uq"][l].reshape(3, P, 4, 192)
        put(uq[..., :128].reshape(3, P, 512))
        put(uq[..., 128:].reshape(3, P, 256))
        ukv = v["w_ukv"][l].reshape(2, P, 4, 2, 128).transpose(0, 1, 3, 2, 4)
        put(ukv.reshape(2, P, 1024))
        blocks(v["w_branch_nsa"][l].reshape(2, 4, 64, D).transpose(1, 0, 2, 3).reshape(512, D))
        blocks(v["w_branch_mla"][l])
        blocks(v["w_out"][l])
        blocks(np.concatenate([v["w_xkv"][l][:, :512], v["w_xq"][l], v["w_xkv"][l][:, 512:]], 1))
        blocks(v["w_xo"][l])
        ffn(v["w_gate_up"][l], v["w_down"][l])
        for _ in range(2):
            put(np.zeros((1, P, 1), np.float32))
        for name in ("mix", "xattn", "mem", "ffn"):
            small(name, feat(v["norm_" + name][l]))
        small("conv_w", v["conv_w"][l].reshape(CONV_W, 4, P).transpose(2, 1, 0).reshape(P, -1))
        small("conv_b", feat(v["conv_b"][l]))
        small("ln_g", feat(v["conv_ln_g"][l]))
        small("ln_b", feat(v["conv_ln_b"][l]))
        small("pos", np.concatenate([feat(v["cmp_pos_k"][l].reshape(-1)), feat(v["cmp_pos_v"][l].reshape(-1))], 1))
        small("b1", np.concatenate([feat(v["cmp_b1_k"][l]), feat(v["cmp_b1_v"][l])], 1))
        w2k = v["cmp_w2_k"][l].reshape(2, P, 64).transpose(1, 0, 2)
        small("w2k", np.concatenate([w2k, w2k], 2).reshape(P, 256))
        small("w2v", v["cmp_w2_v"][l].reshape(2, P, 64).transpose(1, 0, 2).reshape(P, 128))
        small("mq", feat(v["mla_norm_q"][l]))
        small("mkv", feat(v["mla_norm_kv"][l]))

    smalls2 = np.zeros((P, S2_W), np.float32)

    def small2(name, a):
        smalls2[:, S2[name][0]:S2[name][1]] = a
    wi, wo, ng = v["ffn_w_in_2"], v["ffn_w_out_2"], v["norm_g_2"]
    ffn(wi[0, 0], wo[0, 0])
    w = v["hyb_w_in_2"][0]
    at = np.cumsum([0, 1024, 1536, 16, 1024, 1024, 1024, 8])
    zc, xbc, dt, q, k, vv, f = (w[:, a:b] for a, b in zip(at, at[1:]))
    blocks(xbc)
    put(np.concatenate([dt, f], 1).reshape(8, P, 24))
    blocks(np.concatenate([zc, q, k, vv], 1))
    blocks(v["hyb_w_out_2"][0])
    ffn(wi[0, 1], wo[0, 1])
    ffn(wi[1, 0], wo[1, 0])
    blocks(np.concatenate([v["rec_w_in_2"][0][:, D:], v["rec_w_in_2"][0][:, :D]], 1))
    put(np.concatenate([v["rec_w_a_2"][0], v["rec_w_x_2"][0]], 0))
    blocks(v["rec_w_out_2"][0])
    ffn(wi[1, 1], wo[1, 1])
    small2("pre", np.concatenate([feat(ng[l, i]) for l in range(2) for i in (0, 2, 4)], 1))
    small2("cw", v["ssm_conv_w_2"][0].reshape(4, 12, P).transpose(2, 1, 0).reshape(P, -1))
    small2("cb", feat(v["ssm_conv_b_2"][0]))
    small2("ng", feat(v["ssm_norm_g_2"][0]))
    small2("rw", v["rec_conv_w_2"][0].reshape(4, 8, P).transpose(2, 1, 0).reshape(P, -1))
    small2("rb", feat(v["rec_conv_b_2"][0]))
    small2("ba", feat(v["rec_b_a_2"][0]))
    small2("bx", feat(v["rec_b_x_2"][0]))
    small2("lam", feat(v["rec_lambda_2"][0]))
    small2("dtb", v["ssm_dt_bias_2"][0][None])
    small2("alog", v["ssm_a_log_2"][0][None])
    small2("dskip", v["ssm_d_2"][0][None])
    small2("fb", v["fox_b_f_2"][0][None])
    gains = np.stack([v["norm_final"]] + [ng[l, i] for l in range(2) for i in (1, 3, 5)])
    assert len(chunks) == 2 * LAYER_CHUNKS + TAIL_CHUNKS, len(chunks)
    const, hot = constants()
    rel = np.ones((33, 8), np.float32)
    rel[:32] = v["rel_bias"].reshape(32, 2, 4).transpose(0, 2, 1).reshape(32, 8)
    return {
        "w": np.stack(chunks), "const": const, "onehot": hot, "rel": rel, "x": rows(v["x"][0]), "mem": rows(v["mem"][0]),
        "positions": np.ascontiguousarray(v["positions"].reshape(TT, P).T), "smalls": smalls, "smalls2": smalls2, "gains": gains,
    }


def kernel(**inputs):
    import concourse.bacc as bacc
    from concourse.bass_utils import run_bass_kernel_spmd

    arrays = {"in_" + k: np.ascontiguousarray(a) for k, a in layout({k: np.asarray(a) for k, a in inputs.items()}).items()}
    learned = {}
    while True:
        nc = bacc.Bacc("TRN2", target_bir_lowering=False, num_devices=1)
        io = {k[3:]: nc.dram_tensor(k, a.shape, mybir.dt.from_np(a.dtype), kind="ExternalInput").ap() for k, a in arrays.items()}
        io["out"] = nc.dram_tensor("out", (P, TT, D), F32, kind="ExternalOutput").ap()
        io["skew"] = nc.dram_tensor("skew", (8, P * BLK), F32, kind="Internal").ap()
        seen = build(nc, io, learned)
        if seen == learned:
            break
        learned = seen
    r = run_bass_kernel_spmd(nc, [arrays], core_ids=[0])
    got = r.results[0]["out"]
    return got.transpose(1, 0, 2).reshape(1, T, D)
```
